# Optimizing a Trainium2 kernel written in Bass

```python
import math
import jax, jax.numpy as jnp
from jax import lax
import numpy as np

D_MODEL = 1024
BATCH = 1
SEQ = 256
DEPTH = 2

CHUNK = 64
N_MIXERS = 2
MLSTM_HEADS = 4
MLSTM_DK = 128
MLSTM_DV = 256
CONV_W = 4
POOL_WINDOWS = (2, 4, 8, 16)
POOL_GROUPS = 4
POOL_GW = D_MODEL // POOL_GROUPS
MEM_LEN = 256
XATTN_HEADS = 4
XATTN_HD = D_MODEL // XATTN_HEADS
D_FF = 4 * D_MODEL
N_A = (DEPTH + 1) // 2
N_B = DEPTH // 2
ALPHA = (2 * DEPTH) ** 0.25
BETA = (8 * DEPTH) ** -0.25
LN_EPS = 1e-5


def layer_norm(x, g, b):
    xf = x.astype(jnp.float32)
    mu = jnp.mean(xf, axis=-1, keepdims=True)
    var = jnp.mean(jnp.square(xf - mu), axis=-1, keepdims=True)
    y = (xf - mu) * lax.rsqrt(var + LN_EPS) * g.astype(jnp.float32) + b.astype(jnp.float32)
    return y.astype(x.dtype)

def causal_dwconv(u, w):
    S = u.shape[1]
    up = jnp.pad(u, ((0, 0), (CONV_W - 1, 0), (0, 0)))
    acc = up[:, 0:S] * w[0]
    for j in range(1, CONV_W):
        acc = acc + up[:, j:j + S] * w[j]
    return acc

def mlstm_chunk_step(carry, inp):
    C, n, m = carry
    q, k, v, ig, lf = inp
    L = q.shape[2]
    b = jnp.cumsum(lf, axis=-1)
    tril = jnp.tril(jnp.ones((L, L), dtype=bool))
    dmat = jnp.where(tril, b[..., :, None] - b[..., None, :] + ig[..., None, :], -jnp.inf)
    inter = b + m[..., None]
    m_t = jnp.maximum(inter, jnp.max(dmat, axis=-1))
    wts = jnp.exp(dmat - m_t[..., None])
    sc = jnp.einsum('bhtd,bhsd->bhts', q, k) * wts
    a_t = jnp.exp(inter - m_t)
    num = jnp.einsum('bhts,bhsv->bhtv', sc, v) + a_t[..., None] * jnp.einsum('bhtd,bhdv->bhtv', q, C)
    den = jnp.sum(sc, axis=-1) + a_t * jnp.einsum('bhtd,bhd->bht', q, n)
    h = num / jnp.maximum(jnp.abs(den), jnp.exp(-m_t))[..., None]
    b_last = b[..., -1]
    g = b_last[..., None] - b + ig
    m_new = jnp.maximum(b_last + m, jnp.max(g, axis=-1))
    decay = jnp.exp(b_last + m - m_new)
    wk = jnp.exp(g - m_new[..., None])
    C_new = decay[..., None, None] * C + jnp.einsum('bhs,bhsd,bhsv->bhdv', wk, k, v)
    n_new = decay[..., None] * n + jnp.einsum('bhs,bhsd->bhd', wk, k)
    return (C_new, n_new, m_new), h

def mlstm_mixer(x, w_in, gate_b, conv_w, norm_g, w_out):
    B, S, _ = x.shape
    H, DK, DV, L = MLSTM_HEADS, MLSTM_DK, MLSTM_DV, CHUNK
    NC = S // L
    nqk, nv = 2 * H * DK, H * DV
    proj = x @ w_in
    qk = jax.nn.silu(causal_dwconv(proj[..., :nqk], conv_w))
    v = proj[..., nqk:nqk + nv]
    o = proj[..., nqk + nv:nqk + nv + D_MODEL]
    gates = proj[..., nqk + nv + D_MODEL:].astype(jnp.float32) + gate_b.astype(jnp.float32)
    i_pre = gates[..., :H]
    log_f = jax.nn.log_sigmoid(gates[..., H:])

    def to_chunks(t, d):
        return t.astype(jnp.float32).reshape(B, NC, L, H, d).transpose(1, 0, 3, 2, 4)

    q = to_chunks(qk[..., :H * DK], DK) * (DK ** -0.5)
    k = to_chunks(qk[..., H * DK:], DK)
    vc = to_chunks(v, DV)
    ic = i_pre.reshape(B, NC, L, H).transpose(1, 0, 3, 2)
    fc = log_f.reshape(B, NC, L, H).transpose(1, 0, 3, 2)
    init = (jnp.zeros((B, H, DK, DV), jnp.float32),
            jnp.zeros((B, H, DK), jnp.float32),
            jnp.zeros((B, H), jnp.float32))
    _, h = lax.scan(mlstm_chunk_step, init, (q, k, vc, ic, fc))
    h = h.transpose(1, 0, 3, 2, 4).reshape(B, S, H, DV)
    h = h * lax.rsqrt(jnp.mean(jnp.square(h), axis=-1, keepdims=True) + LN_EPS)
    h = h.reshape(B, S, H * DV) * norm_g.astype(jnp.float32)
    y = (jax.nn.sigmoid(o.astype(jnp.float32)) * h).astype(x.dtype)
    return y @ w_out

def pool_mixer(x, w_grp, scale):
    B, S, D = x.shape
    xg = x.astype(jnp.float32).reshape(B, S, POOL_GROUPS, POOL_GW)
    cs = jnp.cumsum(xg, axis=1)
    t1 = (jnp.arange(S) + 1).astype(jnp.float32)
    pooled = []
    for j, w in enumerate(POOL_WINDOWS):
        c = cs[:, :, j]
        lo = jnp.concatenate([jnp.zeros((B, w, POOL_GW), jnp.float32), c[:, :S - w]], axis=1)
        cnt = jnp.minimum(t1, float(w))[None, :, None]
        pooled.append((c - lo) / cnt)
    pooled = jnp.stack(pooled, axis=2)
    diff = pooled - xg
    y = jnp.einsum('bsgc,gcd->bsgd', diff, w_grp.astype(jnp.float32)).reshape(B, S, D)
    return (y * scale.astype(jnp.float32)).astype(x.dtype)

def memory_cross_attn(x, mem_k, mem_v, wq, wo):
    B, S, _ = x.shape
    q = (x @ wq).reshape(B, S, XATTN_HEADS, XATTN_HD).astype(jnp.float32)
    s = jnp.einsum('bshd,bmhd->bhsm', q, mem_k) * (XATTN_HD ** -0.5)
    p = jax.nn.softmax(s, axis=-1)
    o = jnp.einsum('bhsm,bmhd->bshd', p, mem_v).reshape(B, S, D_MODEL).astype(x.dtype)
    return o @ wo

def sq_relu_mlp(x, w1, b1, w2, b2):
    return jnp.square(jax.nn.relu(x @ w1 + b1)) @ w2 + b2

def first_inputs(seed: int = 0) -> dict:
    key = jax.random.key(seed)
    ks = jax.random.split(key, 20)
    H = MLSTM_HEADS
    nqk, nv = 2 * H * MLSTM_DK, H * MLSTM_DV
    p_in = nqk + nv + D_MODEL + 2 * H
    nrm = jax.random.normal
    f_bias = jnp.linspace(3.0, 6.0, H, dtype=jnp.float32)
    gate_b = jnp.concatenate([0.1 * nrm(ks[3], (N_A, H)),
                              f_bias[None, :] + 0.1 * nrm(ks[4], (N_A, H))], axis=-1)
    return {
        "x": nrm(ks[0], (BATCH, SEQ, D_MODEL), jnp.float32),
        "mem": nrm(ks[1], (BATCH, MEM_LEN, D_MODEL), jnp.float32),
        "mlstm_w_in": nrm(ks[2], (N_A, D_MODEL, p_in), jnp.float32) * D_MODEL ** -0.5,
        "mlstm_gate_b": gate_b,
        "mlstm_conv_w": nrm(ks[5], (N_A, CONV_W, nqk), jnp.float32) * CONV_W ** -0.5,
        "mlstm_norm_g": 1.0 + 0.02 * nrm(ks[6], (N_A, nv), jnp.float32),
        "mlstm_w_out": nrm(ks[7], (N_A, nv, D_MODEL), jnp.float32) * (nv ** -0.5) * BETA,
        "pool_w": nrm(ks[8], (N_B, POOL_GROUPS, POOL_GW, POOL_GW), jnp.float32) * (POOL_GW ** -0.5) * BETA,
        "pool_scale": 1.0 + 0.02 * nrm(ks[9], (N_B, D_MODEL), jnp.float32),
        "mem_w_kv": nrm(ks[10], (D_MODEL, 2 * D_MODEL), jnp.float32) * D_MODEL ** -0.5,
        "xattn_wq": nrm(ks[11], (DEPTH, D_MODEL, D_MODEL), jnp.float32) * D_MODEL ** -0.5,
        "xattn_wo": nrm(ks[12], (DEPTH, D_MODEL, D_MODEL), jnp.float32) * (D_MODEL ** -0.5) * BETA,
        "mlp_w1": nrm(ks[13], (DEPTH, D_MODEL, D_FF), jnp.float32) * D_MODEL ** -0.5,
        "mlp_b1": 0.01 * nrm(ks[14], (DEPTH, D_FF), jnp.float32),
        "mlp_w2": nrm(ks[15], (DEPTH, D_FF, D_MODEL), jnp.float32) * (D_FF ** -0.5) * BETA,
        "mlp_b2": 0.01 * nrm(ks[16], (DEPTH, D_MODEL), jnp.float32),
        "ln_g": 1.0 + 0.02 * nrm(ks[17], (DEPTH, 3, D_MODEL), jnp.float32),
        "ln_b": 0.02 * nrm(ks[18], (DEPTH, 3, D_MODEL), jnp.float32),
    }

def first_block(x, mem, mlstm_w_in, mlstm_gate_b, mlstm_conv_w, mlstm_norm_g, mlstm_w_out,
              pool_w, pool_scale, mem_w_kv, xattn_wq, xattn_wo,
              mlp_w1, mlp_b1, mlp_w2, mlp_b2, ln_g, ln_b):
    B = mem.shape[0]
    kv = (mem @ mem_w_kv).astype(jnp.float32)
    mem_k = kv[..., :D_MODEL].reshape(B, MEM_LEN, XATTN_HEADS, XATTN_HD)
    mem_v = kv[..., D_MODEL:].reshape(B, MEM_LEN, XATTN_HEADS, XATTN_HD)
    for i in range(DEPTH):
        j = i // N_MIXERS
        if i % N_MIXERS == 0:
            y = mlstm_mixer(x, mlstm_w_in[j], mlstm_gate_b[j], mlstm_conv_w[j],
                            mlstm_norm_g[j], mlstm_w_out[j])
        else:
            y = pool_mixer(x, pool_w[j], pool_scale[j])
        x = layer_norm(ALPHA * x + y, ln_g[i, 0], ln_b[i, 0])
        x = layer_norm(ALPHA * x + memory_cross_attn(x, mem_k, mem_v, xattn_wq[i], xattn_wo[i]),
                       ln_g[i, 1], ln_b[i, 1])
        x = layer_norm(ALPHA * x + sq_relu_mlp(x, mlp_w1[i], mlp_b1[i], mlp_w2[i], mlp_b2[i]),
                       ln_g[i, 2], ln_b[i, 2])
    return x


DEPTH_2 = 1

N_DIFF_HEADS = 4
DIFF_HEAD_DIM = 64
DIFF_WIDTH = N_DIFF_HEADS * 2 * DIFF_HEAD_DIM
N_MLA_HEADS = 4
MLA_NOPE_DIM = 128
MLA_ROPE_DIM = 64
MLA_QK_DIM = MLA_NOPE_DIM + MLA_ROPE_DIM
MLA_V_DIM = 128
MLA_Q_RANK = 384
MLA_KV_RANK = 256
MLA_WIDTH = N_MLA_HEADS * MLA_V_DIM
MIX_WIDTH = DIFF_WIDTH + MLA_WIDTH
IN_WIDTH = 3 * DIFF_WIDTH + MLA_Q_RANK + MLA_KV_RANK + MLA_ROPE_DIM
IN_SPLITS = [DIFF_WIDTH, 2 * DIFF_WIDTH, 3 * DIFF_WIDTH,
             3 * DIFF_WIDTH + MLA_Q_RANK, 3 * DIFF_WIDTH + MLA_Q_RANK + MLA_KV_RANK]
D_FF_2 = -(-8 * D_MODEL // (3 * 256)) * 256
N_MOD = 6
Q_BLOCK = 128
ROPE_THETA = 10000.0
EPS = 1e-6


def rms_norm(x, g):
    xf = x.astype(jnp.float32)
    y = xf * lax.rsqrt(jnp.mean(xf * xf, axis=-1, keepdims=True) + EPS)
    return (y * g.astype(jnp.float32)).astype(x.dtype)

def apply_rope(x, cos, sin):
    half = x.shape[-1] // 2
    x1, x2 = x[..., :half], x[..., half:]
    return jnp.concatenate([x1 * cos - x2 * sin, x1 * sin + x2 * cos], axis=-1)

def _scores(q, k, start, end, scale):
    s = jnp.einsum('bqhd,bkhd->bhqk', q[:, start:end], k[:, :end],
                   preferred_element_type=jnp.float32)
    return s * scale

def diff_attention(q1, q2, k1, k2, v, lam, slopes):
    S = q1.shape[1]
    scale = DIFF_HEAD_DIM ** -0.5
    outs = []
    for start in range(0, S, Q_BLOCK):
        end = start + Q_BLOCK
        rel = jnp.arange(start, end)[:, None] - jnp.arange(end)[None, :]
        causal = rel >= 0
        alibi = -slopes[:, None, None] * rel.astype(jnp.float32)[None]
        s1 = jnp.where(causal, _scores(q1, k1, start, end, scale) + alibi, -jnp.inf)
        s2 = jnp.where(causal, _scores(q2, k2, start, end, scale) + alibi, -jnp.inf)
        p = jax.nn.softmax(s1, axis=-1) - lam * jax.nn.softmax(s2, axis=-1)
        outs.append(jnp.einsum('bhqk,bkhd->bqhd', p.astype(v.dtype), v[:, :end]))
    return jnp.concatenate(outs, axis=1)

def causal_attention(q, k, v, scale):
    S = q.shape[1]
    outs = []
    for start in range(0, S, Q_BLOCK):
        end = start + Q_BLOCK
        causal = (jnp.arange(start, end)[:, None] - jnp.arange(end)[None, :]) >= 0
        s = jnp.where(causal, _scores(q, k, start, end, scale), -jnp.inf)
        p = jax.nn.softmax(s, axis=-1)
        outs.append(jnp.einsum('bhqk,bkhd->bqhd', p.astype(v.dtype), v[:, :end]))
    return jnp.concatenate(outs, axis=1)

def hybrid_mixer(h, w_in, lq1, lk1, lq2, lk2, g_diff_out, g_q_lat, w_q_up,
                 g_kv_lat, w_kv_up, w_out, cos, sin, lambda_init):
    B, S, _ = h.shape
    proj = h @ w_in
    dq, dk, dv, q_lat, kv_lat, k_rope = jnp.split(proj, IN_SPLITS, axis=-1)

    dq = dq.reshape(B, S, N_DIFF_HEADS, 2, DIFF_HEAD_DIM)
    dk = dk.reshape(B, S, N_DIFF_HEADS, 2, DIFF_HEAD_DIM)
    dv = dv.reshape(B, S, N_DIFF_HEADS, 2 * DIFF_HEAD_DIM)
    lam = (jnp.exp(jnp.sum(lq1.astype(jnp.float32) * lk1.astype(jnp.float32)))
           - jnp.exp(jnp.sum(lq2.astype(jnp.float32) * lk2.astype(jnp.float32)))
           + lambda_init)
    slopes = 2.0 ** (-8.0 * jnp.arange(1, N_DIFF_HEADS + 1, dtype=jnp.float32) / N_DIFF_HEADS)
    o_diff = diff_attention(dq[..., 0, :], dq[..., 1, :], dk[..., 0, :], dk[..., 1, :],
                            dv, lam, slopes)
    o_diff = rms_norm(o_diff, g_diff_out) * (1.0 - lambda_init)

    q = (rms_norm(q_lat, g_q_lat) @ w_q_up).reshape(B, S, N_MLA_HEADS, MLA_QK_DIM)
    q_nope, q_pe = q[..., :MLA_NOPE_DIM], q[..., MLA_NOPE_DIM:]
    q_pe = apply_rope(q_pe, cos[:, None, :], sin[:, None, :])
    kv = (rms_norm(kv_lat, g_kv_lat) @ w_kv_up).reshape(B, S, N_MLA_HEADS, MLA_NOPE_DIM + MLA_V_DIM)
    k_nope, v = kv[..., :MLA_NOPE_DIM], kv[..., MLA_NOPE_DIM:]
    k_pe = apply_rope(k_rope, cos, sin)
    k_pe = jnp.broadcast_to(k_pe[:, :, None, :], (B, S, N_MLA_HEADS, MLA_ROPE_DIM))
    q_full = jnp.concatenate([q_nope, q_pe], axis=-1)
    k_full = jnp.concatenate([k_nope, k_pe], axis=-1)
    o_mla = causal_attention(q_full, k_full, v, MLA_QK_DIM ** -0.5)

    merged = jnp.concatenate([o_diff.reshape(B, S, DIFF_WIDTH),
                              o_mla.reshape(B, S, MLA_WIDTH)], axis=-1)
    return merged @ w_out

def swiglu(h, w_gate, w_up, w_down):
    return (jax.nn.silu(h @ w_gate) * (h @ w_up)) @ w_down

def second_inputs(seed: int = 0) -> dict:
    key = jax.random.key(seed)
    ks = jax.random.split(key, 24)
    f32 = jnp.float32

    def w(k, fan_in, fan_out, mult=1.0):
        return jax.random.normal(k, (DEPTH_2, fan_in, fan_out), f32) * (fan_in ** -0.5) * mult

    def gain(k, n):
        return 1.0 + 0.1 * jax.random.normal(k, (DEPTH_2, n), f32)

    gate_offset = jnp.repeat(jnp.array([0.0, 0.0, 1.0, 0.0, 0.0, 1.0], f32), D_MODEL)
    return {
        "x": jax.random.normal(ks[0], (BATCH, SEQ, D_MODEL), f32),
        "c": jax.random.normal(ks[1], (BATCH, D_MODEL), f32),
        "w_ada": w(ks[2], D_MODEL, N_MOD * D_MODEL, 0.1),
        "b_ada": 0.02 * jax.random.normal(ks[3], (DEPTH_2, N_MOD * D_MODEL), f32) + gate_offset[None],
        "g_mix": gain(ks[4], D_MODEL),
        "w_in": w(ks[5], D_MODEL, IN_WIDTH),
        "lambda_q1": 0.1 * jax.random.normal(ks[6], (DEPTH_2, DIFF_HEAD_DIM), f32),
        "lambda_k1": 0.1 * jax.random.normal(ks[7], (DEPTH_2, DIFF_HEAD_DIM), f32),
        "lambda_q2": 0.1 * jax.random.normal(ks[8], (DEPTH_2, DIFF_HEAD_DIM), f32),
        "lambda_k2": 0.1 * jax.random.normal(ks[9], (DEPTH_2, DIFF_HEAD_DIM), f32),
        "g_diff_out": gain(ks[10], 2 * DIFF_HEAD_DIM),
        "g_q_lat": gain(ks[11], MLA_Q_RANK),
        "w_q_up": w(ks[12], MLA_Q_RANK, N_MLA_HEADS * MLA_QK_DIM),
        "g_kv_lat": gain(ks[13], MLA_KV_RANK),
        "w_kv_up": w(ks[14], MLA_KV_RANK, N_MLA_HEADS * (MLA_NOPE_DIM + MLA_V_DIM)),
        "w_out": w(ks[15], MIX_WIDTH, D_MODEL),
        "g_ffn": gain(ks[16], D_MODEL),
        "w_ffn_gate": w(ks[17], D_MODEL, D_FF_2),
        "w_ffn_up": w(ks[18], D_MODEL, D_FF_2),
        "w_ffn_down": w(ks[19], D_FF_2, D_MODEL),
        "g_final": 1.0 + 0.1 * jax.random.normal(ks[20], (D_MODEL,), f32),
    }

def second_block(x, c, w_ada, b_ada, g_mix, w_in, lambda_q1, lambda_k1, lambda_q2, lambda_k2,
              g_diff_out, g_q_lat, w_q_up, g_kv_lat, w_kv_up, w_out, g_ffn,
              w_ffn_gate, w_ffn_up, w_ffn_down, g_final):
    S = x.shape[1]
    inv_freq = ROPE_THETA ** (-jnp.arange(0, MLA_ROPE_DIM, 2, dtype=jnp.float32) / MLA_ROPE_DIM)
    ang = jnp.arange(S, dtype=jnp.float32)[:, None] * inv_freq[None, :]
    cos = jnp.cos(ang).astype(x.dtype)
    sin = jnp.sin(ang).astype(x.dtype)
    c_act = jax.nn.silu(c)
    for l in range(DEPTH_2):
        lambda_init = 0.8 - 0.6 * math.exp(-0.3 * l)
        mod = c_act @ w_ada[l] + b_ada[l]
        sh_a, sc_a, g_a, sh_f, sc_f, g_f = jnp.split(mod[:, None, :], N_MOD, axis=-1)
        h = rms_norm(x, g_mix[l]) * (1.0 + sc_a) + sh_a
        x = x + g_a * hybrid_mixer(h, w_in[l], lambda_q1[l], lambda_k1[l], lambda_q2[l],
                                   lambda_k2[l], g_diff_out[l], g_q_lat[l], w_q_up[l],
                                   g_kv_lat[l], w_kv_up[l], w_out[l], cos, sin, lambda_init)
        h = rms_norm(x, g_ffn[l]) * (1.0 + sc_f) + sh_f
        x = x + g_f * swiglu(h, w_ffn_gate[l], w_ffn_up[l], w_ffn_down[l])
    return rms_norm(x, g_final)


def setup_inputs(seed=0):
    out = dict(first_inputs(seed))
    for name, value in second_inputs(seed + 1).items():
        if name != "x":
            out[name + "_2"] = value
    return out


def reference(
    x, mem, mlstm_w_in, mlstm_gate_b, mlstm_conv_w, mlstm_norm_g, mlstm_w_out, pool_w,
    pool_scale, mem_w_kv, xattn_wq, xattn_wo, mlp_w1, mlp_b1, mlp_w2, mlp_b2, ln_g, ln_b, c_2,
    w_ada_2, b_ada_2, g_mix_2, w_in_2, lambda_q1_2, lambda_k1_2, lambda_q2_2, lambda_k2_2,
    g_diff_out_2, g_q_lat_2, w_q_up_2, g_kv_lat_2, w_kv_up_2, w_out_2, g_ffn_2, w_ffn_gate_2,
    w_ffn_up_2, w_ffn_down_2, g_final_2,
):
    x = first_block(
        x, mem, mlstm_w_in, mlstm_gate_b, mlstm_conv_w, mlstm_norm_g, mlstm_w_out, pool_w,
        pool_scale, mem_w_kv, xattn_wq, xattn_wo, mlp_w1, mlp_b1, mlp_w2, mlp_b2, ln_g, ln_b,
    )
    return second_block(
        x, c_2, w_ada_2, b_ada_2, g_mix_2, w_in_2, lambda_q1_2, lambda_k1_2, lambda_q2_2,
        lambda_k2_2, g_diff_out_2, g_q_lat_2, w_q_up_2, g_kv_lat_2, w_kv_up_2, w_out_2, g_ffn_2,
        w_ffn_gate_2, w_ffn_up_2, w_ffn_down_2, g_final_2,
    )


_drawn_inputs = setup_inputs


def setup_inputs(seed=0):
    import zlib

    import numpy as np

    out = dict(_drawn_inputs(seed))
    spreads = {}
    factors = {'mlstm_norm_g': 8.0,
     'pool_scale': 8.0,
     'mlp_b1': 6.071,
     'mlp_b2': 3.276,
     'lambda_q1_2': 3.104,
     'g_q_lat_2': 4.933}
    for name, (base, spread) in spreads.items():
        noise = np.random.default_rng([zlib.crc32(name.encode()), seed]).standard_normal(out[name].shape)
        drawn = base * np.exp(spread * noise) if base else spread * noise
        out[name] = __import__('jax').numpy.asarray(drawn.astype(out[name].dtype))
    for name, factor in factors.items():
        out[name] = (out[name] * factor).astype(out[name].dtype)
    return out
```

```python
import math
from contextlib import ExitStack

import numpy as np

import concourse.bass as bass
from concourse import mybir

F32 = mybir.dt.float32
F32R = mybir.dt.float32r
ACT = mybir.ActivationFunctionType
ALU = mybir.AluOpType
AX = mybir.AxisListType.X

ALPHA = 4 ** 0.25
LN_EPS = 1e-5
EPS = 1e-6
NEG = -1e30
NR = 4
NS = 4
AHEAD = 3
CH = 2048
LAMBDA_INIT = 0.8 - 0.6 * math.exp(0.0)


class Lane:

    def __init__(self, sem):
        self.sem, self.n, self.q, self.seen = sem, 0, [], {}

    def wait(self, *tokens):
        for t in tokens:
            if t is None:
                continue
            if isinstance(t, list):
                self.wait(*t)
                continue
            sem, val = t
            if self.seen.get(id(sem), 0) < val:
                self.seen[id(sem)] = val
                self.q.append(lambda e, s=sem, v=val: e.wait_ge(s, v))

    def run(self, f):
        self.q.append(f)

    def do(self, f):
        self.n += 1
        self.q.append(lambda e, f=f: f(e).then_inc(self.sem, 1))
        return (self.sem, self.n)

    def last(self):
        return (self.sem, self.n)

    def emit(self, e):
        for f in self.q:
            f(e)


def build_program(nc, I, out):
    ctx = ExitStack()
    with ctx:
        def sb(name, shape, dt=F32):
            return ctx.enter_context(nc.sbuf_tensor(name, shape, dt))

        def sem(name):
            return ctx.enter_context(nc.semaphore(name))

        RAW = [sb(f"raw{i}", [128, CH]) for i in range(NR)]
        WH = [sb(f"wh{i}", [128, CH], F32R) for i in range(NS)]
        WL = [sb(f"wl{i}", [128, CH], F32R) for i in range(NS)]
        X = sb("X", [128, 2, 1024])
        U = sb("U", [128, 2, 1024])
        S = sb("S", [128, 8, 256])
        XH = sb("XH", [128, 8, 256], F32R)
        XL = sb("XL", [128, 8, 256], F32R)
        KV = sb("KV", [128, 4096])
        AR = sb("AR", [128, 8800])
        FH = [sb(f"fh{i}", [128, 512], F32R) for i in range(2)]
        FL = [sb(f"fl{i}", [128, 512], F32R) for i in range(2)]
        BV = [sb(f"bv{i}", [128, 1024]) for i in range(2)]
        IDN = sb("IDN", [128, 128])
        ONE = sb("ONE", [128, 128])
        PC = sb("PC", [128, 384])
        SM = sb("SM", [128, 416])
        MSK = sb("MSK", [128, 256])
        BN = sb("BN", [128, 2, 16])

        MOD = AR[:, 0:6144]
        sm_at = [0]

        def cols(n):
            sm_at[0] += n
            assert sm_at[0] <= 416
            return SM[:, sm_at[0] - n:sm_at[0]]

        YB = [ctx.enter_context(nc.psum_tensor(f"YB{i}", [128, 512], F32)) for i in range(4)]
        WBt = [ctx.enter_context(nc.psum_tensor(f"WB{i}", [128, 512], F32)) for i in range(4)]

        PE, DVE, AC, PO = (Lane(sem("s_" + n)) for n in ("pe", "dve", "act", "pool"))
        SP = Lane(None)
        s_raw = [sem(f"s_raw{i}") for i in range(NR)]
        s_dma = {}

        def load(lane, name, *pairs):
            if name not in s_dma:
                s_dma[name] = [sem("d_" + name), 0]
            s = s_dma[name]
            for dst, src in pairs:
                s[1] += 16
                lane.run(lambda e, d=dst, r=src, q=s[0]: e.dma_start(d, r).then_inc(q, 16))
            return (s[0], s[1])

        def now():
            return [PE.last(), DVE.last(), AC.last(), PO.last()]

        bank_free = [None] * 4
        bank_at = [0]

        def bank():
            i = bank_at[0] % 4
            bank_at[0] += 1
            PE.wait(bank_free[i])
            return i, WBt[i]

        chunks = []

        def add(src, a, b, kind="mm"):
            chunks.append((src, a, b, kind))

        def rows(w, k0, nk, c0, c1):
            return w[k0 * 128:(k0 + nk) * 128, c0:c1].rearrange("(k p) c -> p k c", p=128)

        w_in, w_kv = I["mlstm_w_in"][0], I["mem_w_kv"]
        for j in range(4):
            add(rows(w_in, 0, 8, 256 * j, 256 * j + 256), 8, 256)
        for j in range(4):
            for kh in range(2):
                add(rows(w_in, 4 * kh, 4, 1024 + 512 * j, 1536 + 512 * j), 4, 512)
        for j in range(4):
            add(rows(w_kv, 0, 8, 256 * j, 256 * j + 256), 8, 256)
        for j in range(2):
            for kh in range(2):
                add(rows(w_kv, 4 * kh, 4, 1024 + 512 * j, 1536 + 512 * j), 4, 512)
        for j in range(4):
            add(rows(I["mlstm_w_out"][0], 2 * j, 2, 0, 1024), 2, 1024)
        ada = [(k, c) for k in range(8) for c in range(3)]
        for i in range(2):
            if i == 1:
                add(I["pool_w"][0].rearrange("g (k p) c -> p (g k) c", p=128), 8, 256)
            for j in range(4):
                add(rows(I["xattn_wq"][i], 0, 8, 256 * j, 256 * j + 256), 8, 256)
            for j in range(4):
                add(rows(I["xattn_wo"][i], 2 * j, 2, 0, 1024), 2, 1024)
            for j in range(17):
                if j < 16:
                    add(rows(I["mlp_w1"][i], 0, 8, 256 * j, 256 * j + 256), 8, 256)
                if j > 0:
                    add(rows(I["mlp_w2"][i], 2 * j - 2, 2, 0, 1024), 2, 1024)
                if 2 <= j < 14:
                    k, c = ada.pop(0)
                    add(I["w_ada_2"][0][k * 128:(k + 1) * 128, 2048 * c:2048 * c + 2048], 1, 2048, ("ada", k, c))
        w2i = I["w_in_2"][0]
        for j in range(4):
            add(rows(w2i, 0, 8, 256 * j, 256 * j + 256), 8, 256)
        for c0, c1 in ((1024, 1536), (1536, 1920), (1920, 2240)):
            for kh in range(2):
                add(rows(w2i, 4 * kh, 4, c0, c1), 4, c1 - c0)
        for j in range(2):
            add(rows(I["w_q_up_2"][0], 0, 3, 384 * j, 384 * j + 384), 3, 384, "qup")
        add(rows(I["w_kv_up_2"][0], 0, 2, 0, 1024), 2, 1024)
        for j in range(4):
            add(rows(I["w_out_2"][0], 2 * j, 2, 0, 1024), 2, 1024)
        for j in range(12):
            if j < 11:
                add(rows(I["w_ffn_gate_2"][0], 0, 8, 256 * j, 256 * j + 256), 8, 256)
                add(rows(I["w_ffn_up_2"][0], 0, 8, 256 * j, 256 * j + 256), 8, 256)
            if j > 0:
                add(rows(I["w_ffn_down_2"][0], 2 * j - 2, 2, 0, 1024), 2, 1024)

        issued, split_n, mm_n = [0], [0], [0]
        raw_free = [None] * NR
        slot_done = [None] * NS
        ready = {}
        cact = cols(8)
        small = {}

        def issue():
            n = issued[0]
            if n >= len(chunks):
                return
            issued[0] += 1
            src, a, b, _ = chunks[n]
            SP.wait(raw_free[n % NR])
            dst = RAW[n % NR][:, 0:a * b]
            if len(src.shape) == 3:
                dst = dst.rearrange("p (a b) -> p a b", a=a)
            SP.run(lambda e: e.dma_start(dst, src).then_inc(s_raw[n % NR], 16))

        def split_next():
            n = split_n[0]
            split_n[0] += 1
            src, a, b, kind = chunks[n]
            landed = (s_raw[n % NR], 16 * (n // NR + 1))
            raw = RAW[n % NR]
            if isinstance(kind, tuple):
                _, k, c = kind
                acc = MOD[:, 2048 * c:2048 * c + 2048]
                DVE.wait(landed, small["cact"], small.get(("ada", c)))
                if k == 0:
                    t = DVE.do(lambda e: e.tensor_scalar(acc, raw[:, :], cact[:, 0:1], None, ALU.mult))
                else:
                    t = DVE.do(lambda e: e.scalar_tensor_tensor(acc, raw[:, :], cact[:, k:k + 1], acc,
                                                                ALU.mult, ALU.add))
                small[("ada", c)] = t
                raw_free[n % NR] = [t]
                issue()
                return False
            m = mm_n[0]
            mm_n[0] += 1
            s = m % NS
            AC.wait(landed, slot_done[s])
            DVE.wait(landed, slot_done[s])
            if kind == "qup":
                r = raw[:, 0:1152].rearrange("p (k h c) -> p k h c", k=3, h=2)
                parts = []
                for w in (WH[s], WL[s]):
                    o = w[:, 0:1536].rearrange("p (k c) -> p k c", k=3)
                    parts.append([
                        o[:, :, 0:256].rearrange("p k (h c) -> p k h c", h=2),
                        o[:, :, 256:384].rearrange("p k (h c) -> p k h c", h=2),
                        o[:, :, 384:512].rearrange("p k (h c) -> p k h c", h=2)[:, :, :, 0:32],
                        o[:, :, 384:512].rearrange("p k (h c) -> p k h c", h=2)[:, :, :, 32:64]])
                srcs = [r[:, :, :, 0:128], r[:, :, :, 128:192], r[:, :, :, 160:192], r[:, :, :, 128:160]]
                for hi, lo, x in zip(parts[0], parts[1], srcs):
                    th = AC.do(lambda e, hi=hi, x=x: e.copy(hi, x))
                    DVE.wait(th)
                    tl = DVE.do(lambda e, hi=hi, lo=lo, x=x: e.tensor_tensor(lo, x, hi.bitcast(F32), ALU.subtract))
            else:
                hi, lo, x = WH[s][:, 0:a * b], WL[s][:, 0:a * b], raw[:, 0:a * b]
                th = AC.do(lambda e: e.copy(hi, x))
                DVE.wait(th)
                tl = DVE.do(lambda e: e.tensor_tensor(lo, x, hi.bitcast(F32), ALU.subtract))
            raw_free[n % NR] = [th, tl]
            ready[m] = (s, [th, tl])
            issue()
            return True

        used = [0]

        def use():
            m = used[0]
            used[0] += 1
            while mm_n[0] <= m + AHEAD - 1 and split_n[0] < len(chunks):
                split_next()
            s, toks = ready.pop(m)
            PE.wait(*toks)
            return s

        def release(s, tok):
            slot_done[s] = tok
            if split_n[0] < len(chunks):
                while split_n[0] < len(chunks) and not split_next():
                    pass

        def mm(o, l, r, start, stop):
            return lambda e: e.matmul(o, l, r, start=start, stop=stop)

        def three(o, lh, ll, rh, rl, start, stop, signal):
            PE.run(mm(o, lh, rh, start, False))
            PE.run(mm(o, lh, rl, False, False))
            f = mm(o, ll, rh, False, stop)
            return PE.do(f) if signal else PE.run(f)

        def fm_gemm(s, a, b, off, o, xh=None, xl=None):
            xh, xl = xh or XH, xl or XL
            for k in range(a):
                l = slice(k * b + off, k * b + off + 128)
                t = three(o, WH[s][:, l], WL[s][:, l], xh[:, k, :], xl[:, k, :],
                          k == 0, k == a - 1, k == a - 1)
            return t

        def tm_gemm(s, a, b, c0, c1, o, t, k0, start, stop, xh=None, xl=None):
            xh, xl = xh or XH, xl or XL
            tk = slice(128 * t, 128 * t + 128)
            tok = None
            for k in range(a):
                r = slice(k * b + c0, k * b + c1)
                tok = three(o, xh[:, k0 + k, tk], xl[:, k0 + k, tk], WH[s][:, r], WL[s][:, r],
                            start and k == 0, stop and k == a - 1, k == a - 1)
            return tok

        yb_free = [None] * 4

        def row_chunk(j, n, xh, xl, xk, wait):
            s = use()
            PE.wait(*wait)
            if j == 0:
                PE.wait(*yb_free)
            toks = []
            for t in range(2):
                for nb in range(2):
                    for k in range(2):
                        tk = slice(128 * t, 128 * t + 128)
                        r = slice(k * 1024 + nb * 512, k * 1024 + nb * 512 + 512)
                        PE.run(mm(YB[2 * t + nb][:, :], xh[:, xk + k, tk], WH[s][:, r], j == 0 and k == 0, False))
                        PE.run(mm(YB[2 * t + nb][:, :], xh[:, xk + k, tk], WL[s][:, r], False, False))
                        f = mm(YB[2 * t + nb][:, :], xl[:, xk + k, tk], WH[s][:, r], False,
                               j == n - 1 and k == 1)
                        if k == 1:
                            tok = PE.do(f)
                        else:
                            PE.run(f)
                toks.append(tok)
            release(s, tok)
            return toks

        def hilo(hi, lo, src, *wait):
            AC.wait(*wait)
            DVE.wait(*wait)
            th = AC.do(lambda e: e.copy(hi, src))
            DVE.wait(th)
            tl = DVE.do(lambda e: e.tensor_tensor(lo, src, hi.bitcast(F32), ALU.subtract))
            return [th, tl]

        xfree = [None]

        def turn(t, src, nk, wait, g=None, b=None, S_=None, H=None, L=None):
            S_, H, L = S_ if S_ is not None else S, H if H is not None else XH, L if L is not None else XL
            tk = slice(128 * t, 128 * t + 128)
            toks = []
            for half in range((nk + 3) // 4):
                ks = range(4 * half, min(nk, 4 * half + 4))
                i, W = bank()
                PE.wait(*wait)
                for k in ks:
                    f = (lambda e, k=k, W=W: e.transpose(W[:, 128 * (k % 4):128 * (k % 4) + 128],
                                                         src(k), IDN[:, :]))
                    tp = PE.do(f)
                lane = AC if half % 2 == 0 else DVE
                lane.wait(tp, *xfree)
                if g is None:
                    o = S_[:, ks[0]:ks[-1] + 1, tk]
                    w = W[:, 0:128 * len(ks)].rearrange("p (k c) -> p k c", k=len(ks))
                    if lane is AC:
                        te = AC.do(lambda e, o=o, w=w: e.copy(o, w))
                    else:
                        te = DVE.do(lambda e, o=o, w=w: e.tensor_copy(o, w))
                else:
                    for k in ks:
                        w = W[:, 128 * (k % 4):128 * (k % 4) + 128]
                        gg, bb = g(k), (b(k) if b else 0.0)
                        if lane is AC:
                            te = AC.do(lambda e, k=k, w=w, gg=gg, bb=bb: e.activation(
                                S_[:, k, tk], w, ACT.Identity, bias=bb, scale=gg))
                        else:
                            te = DVE.do(lambda e, k=k, w=w, gg=gg, bb=bb: e.tensor_scalar(
                                S_[:, k, tk], w, gg, bb, ALU.mult, ALU.add))
                bank_free[i] = te
                AC.wait(*xfree)
                DVE.wait(*xfree)
                toks += hilo(H[:, ks[0]:ks[-1] + 1, tk], L[:, ks[0]:ks[-1] + 1, tk],
                             S_[:, ks[0]:ks[-1] + 1, tk], te)
            return toks

        MH = cols(2)
        t_mh = PO.do(lambda e: e.memset(MH, -0.5))

        def rsqrt(o, x, *wait):
            PO.wait(*wait, t_mh)
            return PO.do(lambda e: e.tensor_tensor(o, x, MH[:, 0:o.shape[1]], ALU.pow))

        def stats(t, wait, rms, src=U):
            st = BN[:, t, 0:12]
            DVE.wait(*wait)
            for h in range(2):
                tb = DVE.do(lambda e, h=h: e.bn_stats(BN[:, t, 6 * h:6 * h + 6], src[:, t, 512 * h:512 * h + 512]))
            DVE.wait(tb)
            tb = DVE.do(lambda e: e.bn_aggr(BN[:, t, 12:14], st))
            if rms:
                DVE.wait(tb)
                tb = DVE.do(lambda e: e.scalar_tensor_tensor(BN[:, t, 13:14], BN[:, t, 12:13], BN[:, t, 12:13],
                                                             BN[:, t, 13:14], ALU.mult, ALU.add))
            DVE.wait(tb)
            tb = DVE.do(lambda e: e.tensor_scalar(BN[:, t, 13:14], BN[:, t, 13:14], EPS if rms else LN_EPS, None,
                                                  ALU.add))
            return rsqrt(BN[:, t, 14:15], BN[:, t, 13:14], tb)

        bv_n = [0]
        bv_free = [None] * 2

        def bvec(src):
            n = bv_n[0]
            bv_n[0] += 1
            PO.wait(bv_free[n % 2])
            tok = load(PO, f"bv{n % 2}", (BV[n % 2][:, :], src.partition_broadcast(128)))
            return n % 2, tok

        x_ready = [[None], [None]]

        def layer_norm(ytoks, i, j, b2=False, turned=True, yscale=None):
            toks = []
            gi, tg = bvec(I["ln_g"][i, j]) if yscale is None else (None, None)
            bi, tb_ = bvec(I["ln_b"][i, j]) if yscale is None else (None, None)
            for t in range(2):
                DVE.wait(ytoks[t], *x_ready[t])
                for h in range(2):
                    cs = slice(512 * h, 512 * h + 512)
                    if yscale is not None:
                        DVE.wait(yscale[1])
                        tu = DVE.do(lambda e, t=t, h=h, cs=cs: e.tensor_tensor(
                            U[:, t, cs], YB[2 * t + h][:, :], BV[yscale[0]][:, cs], ALU.mult))
                        yb_free[2 * t + h] = tu
                        DVE.wait(tu)
                        tu = DVE.do(lambda e, t=t, cs=cs: e.scalar_tensor_tensor(
                            U[:, t, cs], X[:, t, cs], ALPHA, U[:, t, cs], ALU.mult, ALU.add))
                    else:
                        tu = DVE.do(lambda e, t=t, h=h, cs=cs: e.scalar_tensor_tensor(
                            U[:, t, cs], X[:, t, cs], 1.0 if b2 else ALPHA, YB[2 * t + h][:, :],
                            ALU.mult, ALU.add))
                        yb_free[2 * t + h] = tu
                if yscale is not None and t == 1:
                    bv_free[yscale[0]] = tu
                tr = stats(t, [tu], False)
                DVE.wait(tr)
                tz = DVE.do(lambda e, t=t: e.tensor_scalar(U[:, t, :], U[:, t, :], BN[:, t, 12:13],
                                                           BN[:, t, 14:15], ALU.subtract, ALU.mult))
                x_ready[t] = [tz]
                if turned:
                    c = 32 + (i * 3 + j) * 8
                    toks += turn(t, lambda k, t=t: U[:, t, 128 * k:128 * k + 128], 8, [tz],
                                 lambda k, c=c: PC[:, c + k:c + k + 1],
                                 lambda k, c=c: PC[:, c + 48 + k:c + 49 + k])
            if yscale is not None:
                gi, tg = bvec(I["ln_g"][i, j])
                bi, tb_ = bvec(I["ln_b"][i, j])
            for t in range(2):
                L = DVE if t == 1 and not turned else PO
                L.wait(*x_ready[t], tg)
                tx = L.do(lambda e, t=t: e.tensor_tensor(X[:, t, :], U[:, t, :], BV[gi][:, :], ALU.mult))
                L.wait(tx, tb_)
                x_ready[t] = [L.do(lambda e, t=t: e.tensor_tensor(X[:, t, :], X[:, t, :], BV[bi][:, :], ALU.add))]
            bv_free[gi] = bv_free[bi] = [x_ready[0][0], x_ready[1][0]]
            return toks

        t_idn = load(SP, "idn", (IDN[:, :], I["c_idn"]))
        t_x = load(SP, "x", (X[:, :, :], I["x"][0].rearrange("(t p) c -> p t c", p=128)))
        for _ in range(NR):
            issue()
        GRAW = cols(64).rearrange("p (k c) -> p k c", k=8)
        gb = cols(2)
        t_g = load(AC, "gates", (GRAW, w_in[:, 3072:3080].rearrange("(k p) c -> p k c", p=128)),
                   (gb[0:4, 0:1], I["mlstm_gate_b"][0, 0:4].rearrange("(p a) -> p a", a=1)),
                   (gb[0:4, 1:2], I["mlstm_gate_b"][0, 4:8].rearrange("(p a) -> p a", a=1)))

        QP = AR[:, 0:8 * 260].rearrange("p (k c) -> p k c", k=8)
        QC = AR[:, 2080:2080 + 2048].rearrange("p (k c) -> p k c", k=8)
        V1 = AR[:, 4128:4128 + 2064].rearrange("p (t h c) -> p t h c", t=2, h=4)
        OG = AR[:, 6192:6192 + 2048].rearrange("p (t c) -> p t c", t=2)
        GT = AR[:, 8240:8240 + 256]
        ROWS = QC.rearrange("p k c -> p (k c)")[:, 0:384].rearrange("p (r c) -> p r c", r=3)
        G = [BV[0][0:4, 256 * n:256 * n + 256] for n in range(4)] + [BV[1][0:4, 0:256]]
        CSEL = BV[1][0:4, 256:768]

        ms_rows = PO.do(lambda e: e.memset(ROWS[:, 2, :], 0.0))
        vec = lambda v: v.rearrange("(k c) -> k c", c=128)
        mat = lambda v: v.rearrange("i (k c) -> (i k) c", c=128)
        lnr = lambda v: v.rearrange("i j (k c) -> (i j k) c", c=128)
        PO.wait(ms_rows)
        t_rows = load(PO, "rows",
                      (ROWS[0:32, 0, :], mat(I["mlstm_conv_w"][0])),
                      (ROWS[32:80, 0, :], lnr(I["ln_g"])),
                      (ROWS[80:128, 0, :], lnr(I["ln_b"])),
                      (ROWS[0:64, 1, :], mat(I["mlp_b1"])),
                      (ROWS[64:72, 1, :], vec(I["mlstm_norm_g"][0])),
                      (ROWS[72:120, 1, :], vec(I["b_ada_2"][0])),
                      (ROWS[120:128, 1, :], vec(I["c_2"][0])),
                      (ROWS[0:8, 2, :], vec(I["g_mix_2"][0])),
                      (ROWS[8:16, 2, :], vec(I["g_ffn_2"][0])),
                      (ROWS[16:19, 2, :], vec(I["g_q_lat_2"][0])),
                      (ROWS[19:21, 2, :], vec(I["g_kv_lat_2"][0])),
                      (ROWS[21:22, 2, :], vec(I["g_diff_out_2"][0])))
        t_tab = load(PO, "tab", (CSEL, I["c_sel"]), (MSK[:, :], I["c_msk"]))
        t_mem = load(PO, "mem", (U[:, :, :], I["mem"][0].rearrange("(t p) c -> p t c", p=128)))
        GH = FH[0][:, :].rearrange("p (k c) -> p k c", k=8)
        GL = FL[0][:, :].rearrange("p (k c) -> p k c", k=8)
        ms_one = DVE.do(lambda e: e.memset(ONE[:, :], 1.0))
        DVE.do(lambda e: e.memset(GH.bitcast(F32), 0.0))
        z2 = DVE.do(lambda e: e.memset(GL.bitcast(F32), 0.0))
        z3 = DVE.do(lambda e: e.memset(QP[:, :, 0:3], 0.0))
        z4 = DVE.do(lambda e: e.memset(V1[:, :, :, 256:258], 1.0))
        z5 = DVE.do(lambda e: e.memset(GT[0:64, :], 0.0))

        PE.wait(t_idn, t_x)
        xt = []
        for t in range(2):
            xt += turn(t, lambda k, t=t: X[:, t, 128 * k:128 * k + 128], 8, [t_x])
        AC.wait(t_g, z2)
        DVE.wait(t_g)
        for o, c in ((0, 0), (32, 4)):
            th = AC.do(lambda e, o=o, c=c: e.copy(GH[:, :, o:o + 4], GRAW[:, :, c:c + 4]))
            DVE.wait(th)
            tl = DVE.do(lambda e, o=o, c=c: e.tensor_tensor(GL[:, :, o:o + 4], GRAW[:, :, c:c + 4],
                                                            GH[:, :, o:o + 4].bitcast(F32), ALU.subtract))
        gi, GW = bank()
        PE.wait(th, tl, z2, *xt)
        for k in range(8):
            tgm = three(GW[0:64, 0:256], GH[:, k, :], GL[:, k, :], XH[:, k, :], XL[:, k, :],
                        k == 0, k == 7, k == 7)
        DVE.wait(tgm, t_g)
        DVE.do(lambda e: e.tensor_scalar(G[0], GW[0:4, 0:256], gb[0:4, 0:1], None, ALU.add))
        tb = DVE.do(lambda e: e.tensor_copy(G[1], GW[32:36, 0:256]))
        bank_free[gi] = tb
        DVE.wait(tb)
        tb = DVE.do(lambda e: e.tensor_scalar(G[1], G[1], gb[0:4, 1:2], None, ALU.add))
        DVE.wait(tb)
        tc = DVE.do(lambda e: e.scalar_tensor_tensor(G[2], G[1], -1.0, G[1], ALU.mult, ALU.max))
        AC.wait(tc)
        td = AC.do(lambda e: e.activation(G[3], G[2], ACT.Exp, scale=-1.0))
        AC.wait(td)
        td = AC.do(lambda e: e.activation(G[4], G[3], ACT.Ln, bias=1.0))

        ci, CW = bank()
        PE.wait(t_rows)
        for r in range(3):
            tp = PE.do(lambda e, r=r: e.transpose(CW[:, 128 * r:128 * r + 128], ROWS[:, r, :], IDN[:, :]))
        AC.wait(tp)
        t_pc = AC.do(lambda e: e.copy(PC[:, :], CW[:, 0:384]))
        bank_free[ci] = t_pc
        C_LNG, C_LNB, C_B1, C_NG, C_BA, C_C = 32, 80, 128, 192, 200, 248
        C_GM, C_GF, C_GQ, C_GK, C_GD = 256, 264, 272, 275, 277

        DVE.wait(td, z5)
        t1 = DVE.do(lambda e: e.scalar_tensor_tensor(G[2], G[1], 0.0, G[4], ALU.min, ALU.subtract))
        t2 = DVE.do(lambda e: e.memset(G[3], 1.0))
        DVE.wait(t1, t2)
        t1 = DVE.do(lambda e: e.tensor_tensor_scan(G[1], G[3], G[2], 0.0, ALU.mult, ALU.add))
        DVE.wait(t1)
        t1 = DVE.do(lambda e: e.tensor_tensor(GT[0:4, :], G[0], G[1], ALU.subtract))
        DVE.wait(t1)
        tM = DVE.do(lambda e: e.tensor_tensor_scan(G[4], GT[0:4, :], GT[0:4, :], 0.0, ALU.max, ALU.max))
        DVE.wait(tM)
        t3 = DVE.do(lambda e: e.tensor_tensor(G[2], G[1], G[4], ALU.add))
        AC.wait(t3)
        tem = AC.do(lambda e: e.activation(GT[32:36, :], G[2], ACT.Exp, scale=-1.0))
        AC.wait(t_pc)
        small["cact"] = AC.do(lambda e: e.activation(cact, PC[:, C_C:C_C + 8], ACT.Silu))

        for j in range(4):
            s = use()
            i, W = bank()
            for f in range(2):
                tp = fm_gemm(s, 8, 256, 128 * f, W[:, 256 * f:256 * f + 256])
            release(s, tp)
            AC.wait(tp)
            te = AC.do(lambda e, j=j, W=W: e.copy(QP[:, 2 * j:2 * j + 2, 3:259],
                                                  W[:, :].rearrange("p (f c) -> p f c", f=2)))
            bank_free[i] = te
            DVE.wait(te, t_pc)
            for f in range(2):
                k = 2 * j + f
                cw = lambda n, k=k: PC[:, 8 * n + k:8 * n + k + 1]
                tv = DVE.do(lambda e, k=k, cw=cw: e.tensor_scalar(QC[:, k, :], QP[:, k, 0:256], cw(0), None,
                                                                  ALU.mult))
                for n in range(1, 4):
                    DVE.wait(tv)
                    tv = DVE.do(lambda e, k=k, n=n, cw=cw: e.scalar_tensor_tensor(
                        QC[:, k, :], QP[:, k, n:n + 256], cw(n), QC[:, k, :], ALU.mult, ALU.add))
            AC.wait(tv)
            t_qc = AC.do(lambda e, j=j: e.activation(QC[:, 2 * j:2 * j + 2, :], QC[:, 2 * j:2 * j + 2, :], ACT.Silu))
        t_conv = tv
        ui, UW = bank()
        PE.wait(tem, tM)
        for t in range(2):
            tp = PE.do(lambda e, t=t: e.transpose(UW[:, 64 * t:64 * t + 64], GT[0:64, 128 * t:128 * t + 128],
                                                  IDN[0:64, 0:64]))
        UC = cols(72)
        DVE.wait(tp)
        t_uc = DVE.do(lambda e: e.tensor_copy(UC.rearrange("p (t c) -> p t c", t=2),
                                              UW[:, 0:128].rearrange("p (t c) -> p t c", t=2)[:, :, 0:36]))
        bank_free[ui] = t_uc

        def tm_panel(width, evac):
            bs = [bank() for _ in range(2)]
            for kh in range(2):
                s = use()
                for t in range(2):
                    tp = tm_gemm(s, 4, width, 0, width, bs[t][1][:, 0:width], t, 4 * kh, kh == 0, kh == 1)
                    if kh == 1:
                        bank_free[bs[t][0]] = evac(t, bs[t][1], tp)
                release(s, tp)

        def ev_v(j, dst):
            def f(t, W, tp):
                AC.wait(tp)
                return AC.do(lambda e: e.copy(dst(t), W[:, :].rearrange("p (h c) -> p h c", h=2)))
            return f

        AC.wait(z4)
        for j in range(2):
            tm_panel(512, ev_v(j, lambda t, j=j: V1[:, t, 2 * j:2 * j + 2, 0:256]))
        t_v1 = AC.last()

        def ev_o(j):
            def f(t, W, tp):
                AC.wait(tp)
                return AC.do(lambda e: e.activation(OG[:, t, 512 * j:512 * j + 512], W[:, :], ACT.Sigmoid))
            return f

        for j in range(2):
            tm_panel(512, ev_o(j))
        t_og = AC.last()
        x_gemm = PE.last()

        DT = [AR[:, 384 * n:384 * n + 384] for n in range(2)]
        SC = [AR[:, 768 + 384 * n:1152 + 384 * n] for n in range(2)]
        sc_tok, sc_free, dt_free = {}, [None] * 2, [None] * 2

        def head_a(h):
            bi, MB = bank()
            PE.wait(tM, t_tab)
            tp = PE.do(mm(MB[:, 0:256], CSEL[:, 128 * h:128 * h + 128], G[4], True, True))
            si, SW = bank()
            PE.wait(t_qc)
            PE.run(mm(SW[:, 0:256], QC[:, 4 + h, 0:128], QC[:, h, :], True, True))
            tq = PE.do(mm(SW[:, 256:384], QC[:, 4 + h, 128:256], QC[:, h, 128:256], True, True))
            D, C = DT[h % 2], SC[h % 2]
            DVE.wait(tp, t_tab, dt_free[h % 2], t_conv)
            DVE.do(lambda e: e.scalar_tensor_tensor(D[:, 0:256], MB[:, 0:256], -1.0, MSK[:, :],
                                                    ALU.mult, ALU.add))
            td = DVE.do(lambda e: e.scalar_tensor_tensor(D[:, 256:384], MB[:, 128:256], -1.0, MSK[:, 0:128],
                                                         ALU.mult, ALU.add))
            bank_free[bi] = td
            AC.wait(td, t_uc)
            AC.do(lambda e: e.activation(D[:, 0:256], D[:, 0:256], ACT.Exp, bias=UC[:, h:h + 1]))
            te = AC.do(lambda e: e.activation(D[:, 256:384], D[:, 256:384], ACT.Exp, bias=UC[:, 36 + h:37 + h]))
            DVE.wait(te, tq, sc_free[h % 2])
            sc_tok[h] = DVE.do(lambda e: e.scalar_tensor_tensor(C, SW[:, 0:384], 128 ** -0.5, D,
                                                                ALU.mult, ALU.mult))
            dt_free[h % 2] = bank_free[si] = sc_tok[h]

        y_tok = []

        def head_c(h):
            C = SC[h % 2]
            PE.wait(sc_tok[h], t_v1, z4)
            for t in range(2):
                b = (2 * h + t) % 4
                Y = YB[b]
                PE.wait(yb_free[b])
                if t == 0:
                    tn = PE.do(mm(Y[:, 0:258], C[:, 0:128], V1[:, 0, h, :], True, True))
                else:
                    PE.run(mm(Y[:, 0:258], C[:, 128:256], V1[:, 0, h, :], True, False))
                    tn = PE.do(mm(Y[:, 0:258], C[:, 256:384], V1[:, 1, h, :], False, True))
                    sc_free[h % 2] = tn
                w = cols(4)
                em = UC[:, 36 * t + 32 + h:36 * t + 33 + h]
                DVE.wait(tn)
                t1 = DVE.do(lambda e, w=w, Y=Y, em=em: e.tensor_scalar(w[:, 0:1], Y[:, 256:257], -1.0, em,
                                                                       ALU.mult, ALU.max))
                DVE.wait(t1)
                t1 = DVE.do(lambda e, w=w, Y=Y: e.tensor_scalar(w[:, 0:1], Y[:, 256:257], w[:, 0:1], None,
                                                                ALU.max))
                DVE.wait(t1)
                t1 = DVE.do(lambda e, w=w: e.reciprocal(w[:, 1:2], w[:, 0:1]))
                AC.wait(t1)
                t2 = AC.do(lambda e, w=w, Y=Y, t=t: e.activation(JK, Y[:, 0:256], ACT.Square,
                                                                 scale=w[:, 1:2], accum_out=w[:, 2:3]))
                PO.wait(t2)
                t3 = PO.do(lambda e, w=w: e.tensor_scalar(w[:, 2:3], w[:, 2:3], 1 / 256, LN_EPS,
                                                          ALU.mult, ALU.add))
                t3 = rsqrt(w[:, 3:4], w[:, 2:3], t3)
                PO.wait(t3)
                t3 = PO.do(lambda e, w=w: e.tensor_tensor(w[:, 3:4], w[:, 3:4], w[:, 1:2], ALU.mult))
                DVE.wait(t3, t_og, mem_turned)
                yb_free[b] = t4 = DVE.do(lambda e, w=w, Y=Y, t=t: e.scalar_tensor_tensor(
                    U[:, t, 256 * h:256 * h + 256], Y[:, 0:256], w[:, 3:4],
                    OG[:, t, 256 * h:256 * h + 256], ALU.mult, ALU.mult))
                y_tok.append(t4)

        JK = AR[:, 1536:1792]
        KT = KV[:, 0:2048].rearrange("p (k c) -> p k c", k=8)
        VM = KV[:, 2048:4096].rearrange("p (t c) -> p t c", t=2)

        def k_chunk(j):
            s = use()
            i, W = bank()
            PE.wait(*mt)
            for f in range(2):
                tp = fm_gemm(s, 8, 256, 128 * f, W[:, 256 * f:256 * f + 256])
            release(s, tp)
            AC.wait(tp)
            bank_free[i] = AC.do(lambda e: e.copy(KT[:, 2 * j:2 * j + 2, :],
                                                  W[:, :].rearrange("p (f c) -> p f c", f=2)))

        def ev_m(j):
            def f(t, W, tp):
                AC.wait(tp)
                return AC.do(lambda e: e.copy(VM[:, t, 512 * j:512 * j + 512], W[:, :]))
            return f

        head_a(0)
        xfree[:] = [x_gemm, AC.last(), DVE.last()]
        mt = []
        for t in range(2):
            mt += turn(t, lambda k, t=t: U[:, t, 128 * k:128 * k + 128], 8, [t_mem])
        mem_turned = PE.last()
        head_a(1)
        k_chunk(0)
        head_c(0)
        k_chunk(1)
        head_a(2)
        head_c(1)
        k_chunk(2)
        head_a(3)
        head_c(2)
        k_chunk(3)
        head_c(3)
        for j in range(2):
            tm_panel(512, ev_m(j))
        t_kv = AC.last()
        xfree[:] = now()
        yt = []
        for t in range(2):
            yt += turn(t, lambda k, t=t: U[:, t, 128 * k:128 * k + 128], 8, y_tok[t::2],
                       lambda k: PC[:, C_NG + k:C_NG + k + 1])
        for j in range(4):
            ys = row_chunk(j, 4, XH, XL, 2 * j, yt)
        x_ready = [[t_x], [t_x]]
        xfree[:] = now()
        xt = layer_norm(ys, 0, 0)

        TMP = AR[:, 6144:8800]
        xa_free = {}

        def xattn(xt, first):
            QT = [TMP[:, 512 * n:512 * n + 512] for n in range(2)]
            PB = [TMP[:, 1024 + 512 * n:1536 + 512 * n] for n in range(2)]
            PT = TMP[:, 2048:2560]
            tok = {}
            xo = {}

            def p0(h):
                s = use()
                i, W = bank()
                PE.wait(*xt)
                for f in range(2):
                    tp = fm_gemm(s, 8, 256, 128 * f, W[:, 256 * f:256 * f + 256])
                release(s, tp)
                AC.wait(tp, xa_free.get(("q", h % 2)), *first)
                bank_free[i] = tok["q", h] = AC.do(lambda e: e.copy(QT[h % 2], W[:, :]))
                if h == 3:
                    tok["wq"] = tp

            def p1(h):
                i, W = bank()
                PE.wait(tok["q", h], t_kv)
                Q = QT[h % 2].rearrange("p (f c) -> p f c", f=2)
                for t in range(2):
                    for f in range(2):
                        m = mm(W[:, 256 * t:256 * t + 256], Q[:, f, 128 * t:128 * t + 128],
                               KT[:, 2 * h + f, :], f == 0, f == 1)
                        tp = PE.do(m) if t * f else PE.run(m)
                xa_free["q", h % 2] = tp
                w = cols(6)
                W3 = W[:, :].rearrange("p (t c) -> p t c", t=2)
                P = PB[h % 2].rearrange("p (t c) -> p t c", t=2)
                DVE.wait(tp)
                t1 = DVE.do(lambda e: e.tensor_reduce(w[:, 0:2], W3, AX, ALU.max))
                DVE.wait(t1)
                t1 = DVE.do(lambda e: e.tensor_scalar(w[:, 0:2], w[:, 0:2], -1 / 16, None, ALU.mult))
                AC.wait(t1, xa_free.get(("p", h % 2)), *first)
                for t in range(2):
                    te = AC.do(lambda e, t=t: e.activation(P[:, t, :], W3[:, t, :], ACT.Exp, bias=w[:, t:t + 1],
                                                           scale=1 / 16, accum_out=w[:, 2 + t:3 + t]))
                bank_free[i] = te
                DVE.wait(te)
                t1 = DVE.do(lambda e: e.reciprocal(w[:, 4:6], w[:, 2:4]))
                DVE.wait(t1)
                for t in range(2):
                    t2 = DVE.do(lambda e, t=t: e.tensor_scalar(P[:, t, :], P[:, t, :], w[:, 4 + t:5 + t], None,
                                                               ALU.mult))
                tok["p", h] = t2

            def p2(h):
                i, W = bank()
                P = PB[h % 2].rearrange("p (t c) -> p t c", t=2)
                PE.wait(tok["p", h])
                for m in range(2):
                    for t in range(2):
                        tp = PE.do(lambda e, m=m, t=t: e.transpose(
                            W[:, 256 * m + 128 * t:256 * m + 128 * t + 128], P[:, t, 128 * m:128 * m + 128],
                            IDN[:, :]))
                xa_free["p", h % 2] = tp
                AC.wait(tp, xa_free.get("pt"))
                bank_free[i] = tok["pt", h] = AC.do(lambda e: e.copy(PT, W[:, :]))

            def p3(h):
                i, W = bank()
                PE.wait(tok["pt", h])
                for d in range(2):
                    for m in range(2):
                        f = mm(W[:, 256 * d:256 * d + 256], VM[:, m, 256 * h + 128 * d:256 * h + 128 * d + 128],
                               PT[:, 256 * m:256 * m + 256], m == 0, m == 1)
                        tp = PE.do(f) if d * m else PE.run(f)
                xa_free["pt"] = tp
                DVE.wait(tp, tok["wq"])
                o = S[:, 2 * h:2 * h + 2, :]
                bank_free[i] = te = DVE.do(lambda e: e.tensor_copy(o, W[:, :].rearrange("p (f c) -> p f c", f=2)))
                AC.wait(tok["wq"])
                xo[h] = hilo(XH[:, 2 * h:2 * h + 2, :], XL[:, 2 * h:2 * h + 2, :], o, te)

            def r(h):
                return row_chunk(h, 4, XH, XL, 2 * h, xo[h])

            for f, h in ((p0, 0), (p0, 1), (p1, 0), (p0, 2), (p1, 1), (p2, 0), (p0, 3), (p3, 0), (p1, 2), (p2, 1),
                         (p1, 3), (p3, 1), (p2, 2), (r, 0), (p3, 2), (p2, 3), (r, 1), (p3, 3), (r, 2), (r, 3)):
                ys = f(h)
            xfree[:] = now()
            return ys

        f_free = [[None], [None]]

        def mlp(i, xt, first, at14=None):
            RT = [TMP[:, 512 * n:512 * n + 512] for n in range(2)]
            fo = {}
            b2i, tb2 = bvec(I["mlp_b2"][i])
            for t in range(2):
                PO.wait(*x_ready[t])
                tx = PO.do(lambda e, t=t: e.tensor_scalar(X[:, t, :], X[:, t, :], ALPHA, None, ALU.mult))
                PO.wait(tx, tb2)
                tx = PO.do(lambda e, t=t: e.tensor_tensor(X[:, t, :], X[:, t, :], BV[b2i][:, :], ALU.add))
                x_ready[t] = [tx]
            bv_free[b2i] = tx
            for j in range(17):
                if j < 16:
                    s = use()
                    bi, W = bank()
                    PE.wait(*xt)
                    for f in range(2):
                        tp = fm_gemm(s, 8, 256, 128 * f, W[:, 256 * f:256 * f + 256])
                    release(s, tp)
                    R = RT[j % 2]
                    AC.wait(tp, *first)
                    AC.wait(*f_free[j % 2])
                    for f in range(2):
                        c = C_B1 + 32 * i + 2 * j + f
                        tr = AC.do(lambda e, f=f, c=c, W=W, R=R: e.activation(
                            R[:, 256 * f:256 * f + 256], W[:, 256 * f:256 * f + 256], ACT.Relu,
                            bias=PC[:, c:c + 1]))
                    bank_free[bi] = tr
                    DVE.wait(tr)
                    tr = DVE.do(lambda e, R=R: e.tensor_tensor(R, R, R, ALU.mult))
                    DVE.wait(*f_free[j % 2])
                    fo[j] = hilo(FH[j % 2][:, :], FL[j % 2][:, :], R, tr)
                if j > 0:
                    n = (j - 1) % 2
                    v = lambda b: b[n][:, :].rearrange("p (f c) -> p f c", f=2)
                    ys = row_chunk(j - 1, 16, v(FH), v(FL), 0, fo[j - 1])
                    f_free[n] = [PE.last(), DVE.last()]
                if j == 14 and at14:
                    at14()
            xfree[:] = now()
            return ys

        cut = now()
        ys = xattn(xt, cut)
        xt = layer_norm(ys, 0, 1)
        cut = now()
        small[("ada", 0)] = small[("ada", 1)] = small[("ada", 2)] = cut
        ys = mlp(0, xt, cut)
        layer_norm(ys, 0, 2, b2=True, turned=False)

        WM = TMP[:, 0:1536]
        PO.wait(*now())
        t_wm = load(PO, "wm", (WM, I["c_win"]))
        sc_i, t_sc = bvec(I["pool_scale"][0])
        s = use()
        po = []
        xfree[:] = now()
        for k in range(8):
            g = k // 2
            if k % 2 == 0:
                i, W = bank()
            PE.wait(t_wm, *x_ready[0], *x_ready[1])
            o = W[:, 256 * (k % 2):256 * (k % 2) + 256]
            wm = WM[:, 384 * g:384 * g + 384]
            fs = slice(128 * k, 128 * k + 128)
            PE.run(mm(o, X[:, 0, fs], wm[:, 0:256], True, False))
            tp = PE.do(mm(o[:, 128:256], X[:, 1, fs], wm[:, 256:384], False, True))
            if k % 2:
                DVE.wait(tp, *xfree)
                AC.wait(*xfree)
                o = S[:, k - 1:k + 1, :]
                bank_free[i] = te = DVE.do(lambda e, o=o, W=W: e.tensor_copy(
                    o, W[:, :].rearrange("p (f c) -> p f c", f=2)))
                po.append(hilo(XH[:, k - 1:k + 1, :], XL[:, k - 1:k + 1, :], o, te))
        ys = []
        PE.wait(*yb_free)
        for t in range(2):
            for g in range(4):
                PE.wait(*po[g])
                tp = tm_gemm(s, 2, 256, 512 * g, 512 * g + 256, YB[2 * t + g // 2][:, 256 * (g % 2):256 * (g % 2) + 256], t,
                             2 * g, True, True)
            ys.append(tp)
        release(s, tp)
        xfree[:] = now()
        xt = layer_norm(ys, 1, 0, yscale=(sc_i, t_sc))
        cut = now()
        ys = xattn(xt, cut)
        xt = layer_norm(ys, 1, 1)
        cut = now()

        MC = cols(48)
        modt = {}

        def modulation():
            i, W = bank()
            PE.wait(small["ada", 0], small["ada", 1], small["ada", 2], ms_one)
            for n in range(48):
                tp = mm(W[:, 2 * n:2 * n + 2], MOD[:, 128 * n:128 * n + 128], ONE[:, 0:2], True, True)
                tp = PE.do(tp) if n == 47 else PE.run(tp)
            DVE.wait(tp)
            t1 = DVE.do(lambda e: e.tensor_tensor(MC, W[:, 0:96].rearrange("p (n a) -> p n a", a=2)[:, :, 0],
                                                  PC[:, C_BA:C_BA + 48], ALU.add))
            bank_free[i] = t1
            DVE.wait(t1)
            for a, g in ((8, C_GM), (32, C_GF)):
                t1 = DVE.do(lambda e, a=a, g=g: e.scalar_tensor_tensor(
                    MC[:, a:a + 8], MC[:, a:a + 8], 1.0, PC[:, g:g + 8], ALU.add, ALU.mult))
            modt["mc"] = t1

        def gate_rows(n, dst, first):
            src = 2048 if n == 0 else 5120
            gi, tg = bvec(I["b_ada_2"][0, src:src + 1024])
            for h in range(2):
                i, W = bank()
                tp = PE.do(mm(W[:, :], ONE[:, :], MOD[:, src + 512 * h:src + 512 * h + 512], True, True))
                DVE.wait(tp, tg, *first)
                bank_free[i] = t = DVE.do(lambda e, h=h, W=W: e.tensor_tensor(
                    dst[:, 512 * h:512 * h + 512], W[:, :], BV[gi][:, 512 * h:512 * h + 512], ALU.add))
            bv_free[gi] = t
            return t

        ys = mlp(1, xt, cut, modulation)
        layer_norm(ys, 1, 2, b2=True, turned=False)
        GB = AR[:, 6144:8192].rearrange("p (n c) -> p n c", n=2)
        cut = now()
        t_gb = [gate_rows(n, GB[:, n, :], cut) for n in range(2)]
        Uf = U[:, :, :].rearrange("p t c -> p (t c)")
        Sf = S[:, :, :].rearrange("p k c -> p (k c)")
        DQ = AR[:, 0:1024].rearrange("p (h c) -> p h c", h=4)
        KD = AR[:, 1024:3072].rearrange("p (h s c) -> p h s c", h=4, s=2)
        DV = AR[:, 3072:4096].rearrange("p (t c) -> p t c", t=2)
        QL = AR[:, 4096:4864].rearrange("p (t c) -> p t c", t=2)
        KL = AR[:, 4864:5504].rearrange("p (t c) -> p t c", t=2)
        PTS = [Uf[:, 1536:1920], AR[:, 5504:5888]]
        OT = AR[:, 5888:6144].rearrange("p (t c) -> p t c", t=2)
        E2 = [[Uf[:, 768 * n + 384 * m:768 * n + 384 * m + 384] for m in range(2)] for n in range(2)]
        CS = AR[:, 8192:8704].rearrange("p (n c) -> p n c", n=2)
        QN = KV[:, 0:1024].rearrange("p (h c) -> p h c", h=4)
        QPE = KV[:, 1024:1536].rearrange("p (j c) -> p j c", j=2)
        KN = KV[:, 1536:2560].rearrange("p (h c) -> p h c", h=4)
        KPE = KV[:, 2560:3072].rearrange("p (s c) -> p s c", s=2)
        V2 = KV[:, 3072:4096].rearrange("p (t c) -> p t c", t=2)
        RT = Sf[:, 0:256].rearrange("p (t c) -> p t c", t=2)
        RA = Sf[:, 256:384].rearrange("p (n t c) -> p n t c", n=2, t=2)
        TB = [BV[0][:, 256 * h:256 * h + 256] for h in range(4)] + [BV[1][:, 0:256]]
        TR = BV[1][:, 256:384].rearrange("p (n t c) -> p n t c", n=2, t=2)

        def rms_turn(a, b, x_toks):
            toks = []
            for t in range(2):
                tr = stats(t, x_toks[t], True, X)
                DVE.wait(tr)
                tz = DVE.do(lambda e, t=t: e.tensor_scalar(U[:, t, :], X[:, t, :], BN[:, t, 14:15], None, ALU.mult))
                toks += turn(t, lambda k, t=t: U[:, t, 128 * k:128 * k + 128], 8, [tz],
                             lambda k: MC[:, a + k:a + k + 1], lambda k: MC[:, b + k:b + k + 1])
            return toks

        xfree[:] = now()
        DVE.wait(modt["mc"])
        AC.wait(modt["mc"])
        xt = rms_turn(8, 0, x_ready)
        cut = now()
        PO.wait(*cut)
        t_tb = load(PO, "tb", (BV[0][:, :], I["c_alibi"]), (BV[1][:, 0:256], I["c_causal"]),
                    (BV[1][:, 256:384], I["c_rope_t"]), (AR[:, 8192:8704], I["c_rope_f"]))
        LB = Uf[:, 0:256].rearrange("p (n c) -> p n c", n=4)
        t_lb = load(PO, "lam", *[(LB[:, n, :], I[f"lambda_{x}_2"][0].partition_broadcast(128))
                                 for n, x in enumerate(("q1", "q2", "k1", "k2"))])
        PO.do(lambda e: e.memset(KD[64:128, :, 0, :], 0.0))
        PO.do(lambda e: e.memset(KD[0:64, :, 1, :], 0.0))
        PO.do(lambda e: e.memset(KPE[64:128, 0, :], 0.0))
        t_zero = PO.do(lambda e: e.memset(KPE[0:64, 1, :], 0.0))
        lam = cols(4)
        DVE.wait(t_lb)
        t1 = DVE.do(lambda e: e.tensor_tensor(LB[:, 0:2, :], LB[:, 0:2, :], LB[:, 2:4, :], ALU.mult))
        DVE.wait(t1)
        t1 = DVE.do(lambda e: e.tensor_reduce(lam[:, 0:2], LB[:, 0:2, :], AX, ALU.add))
        AC.wait(t1)
        t1 = AC.do(lambda e: e.activation(lam[:, 0:2], lam[:, 0:2], ACT.Exp))
        DVE.wait(t1)
        t_lam = DVE.do(lambda e: e.scalar_tensor_tensor(lam[:, 2:3], lam[:, 1:2], LAMBDA_INIT, lam[:, 0:1],
                                                        ALU.subtract, ALU.subtract))
        AC.wait(*cut)
        DVE.wait(*cut)
        dtok = {}

        def dq_chunk(j):
            s = use()
            i, W = bank()
            PE.wait(*xt)
            for f in range(2):
                tp = fm_gemm(s, 8, 256, 128 * f, W[:, 256 * f:256 * f + 256])
            release(s, tp)
            AC.wait(tp)
            W3 = W[:, :].rearrange("p (f c) -> p f c", f=2)
            if j < 2:
                te = AC.do(lambda e: e.copy(DQ[:, 2 * j:2 * j + 2, :], W3))
            else:
                AC.do(lambda e: e.copy(KD[0:64, 2 * j - 4:2 * j - 2, 0, :], W3[0:64]))
                te = AC.do(lambda e: e.copy(KD[64:128, 2 * j - 4:2 * j - 2, 1, :], W3[64:128]))
            bank_free[i] = te
            dtok["k"] = te

        def ev_dv(t, W, tp):
            AC.wait(tp)
            dtok["v"] = AC.do(lambda e: e.copy(DV[:, t, :], W[:, :]))
            return dtok["v"]

        def latent_scale(t, dst, n, W, tp, w):
            AC.wait(tp)
            AC.wait(AC.do(lambda e: e.copy(dst, W[:, 0:dst.shape[1]])))
            te = AC.do(lambda e: e.activation(V2[:, 0, 0:n], W[:, 0:n], ACT.Square, accum_out=w[:, 0:1]))
            PO.wait(te)
            t1 = PO.do(lambda e: e.tensor_scalar(w[:, 0:1], w[:, 0:1], 1 / n, EPS, ALU.mult, ALU.add))
            t1 = rsqrt(w[:, 1:2], w[:, 0:1], t1)
            DVE.wait(te, t1)
            return te, DVE.do(lambda e: e.tensor_scalar(dst[:, 0:n], dst[:, 0:n], w[:, 1:2], None, ALU.mult))

        def ev_ql(t, W, tp):
            te, dtok["ql", t] = latent_scale(t, QL[:, t, :], 384, W, tp, cols(2))
            return te

        def ev_kl(t, W, tp):
            te, dtok["kl", t] = latent_scale(t, KL[:, t, :], 256, W, tp, cols(2))
            return te

        efree, pfree = [None, None], [None, None]

        def softmax_rows(W, E, tb, scale, w, c):
            DVE.do(lambda e: e.scalar_tensor_tensor(E[:, 0:128], W[:, 0:128], scale, tb[:, 128:256],
                                                    ALU.mult, ALU.add))
            t1 = DVE.do(lambda e: e.scalar_tensor_tensor(E[:, 128:384], W[:, 128:384], scale, tb,
                                                         ALU.mult, ALU.add))
            tw = t1
            DVE.wait(t1)
            DVE.do(lambda e: e.tensor_reduce(w[:, c:c + 1], E[:, 0:128], AX, ALU.max, negate=True))
            t1 = DVE.do(lambda e: e.tensor_reduce(w[:, c + 1:c + 2], E[:, 128:384], AX, ALU.max, negate=True))
            AC.wait(t1)
            AC.do(lambda e: e.activation(E[:, 0:128], E[:, 0:128], ACT.Exp, bias=w[:, c:c + 1],
                                         accum_out=w[:, c + 2:c + 3]))
            te = AC.do(lambda e: e.activation(E[:, 128:384], E[:, 128:384], ACT.Exp, bias=w[:, c + 1:c + 2],
                                              accum_out=w[:, c + 3:c + 4]))
            return tw, te

        def d1(h):
            E = E2[h % 2]
            w = cols(12)
            tps, bs = [], []
            for m in range(2):
                i, W = bank()
                bs.append((i, W))
                PE.wait(dtok["k"], t_zero)
                PE.run(mm(W[:, 0:128], DQ[:, h, 0:128], KD[:, h, m, 0:128], True, True))
                tps.append(PE.do(mm(W[:, 128:384], DQ[:, h, 128:256], KD[:, h, m, :], True, True)))
            for m in range(2):
                DVE.wait(tps[m], t_tb, t_lam, efree[h % 2])
                bank_free[bs[m][0]], te = softmax_rows(bs[m][1], E[m], TB[h], 64 ** -0.5, w, 4 * m)
            DVE.wait(te)
            w2 = w[:, 0:8].rearrange("p (m c) -> p m c", m=2)[:, :, 2:4]
            r = w[:, 8:12].rearrange("p (m c) -> p m c", m=2)
            t1 = DVE.do(lambda e: e.reciprocal(r, w2))
            DVE.wait(t1)
            t1 = DVE.do(lambda e: e.tensor_scalar(w[:, 10:12], w[:, 10:12], lam[:, 2:3], None, ALU.mult))
            for c, a in ((0, slice(0, 128)), (1, slice(128, 384))):
                t2 = DVE.do(lambda e, c=c, a=a: e.tensor_scalar(E[0][:, a], E[0][:, a], w[:, 8 + c:9 + c], None,
                                                                ALU.mult))
                DVE.wait(t1, t2)
                t3 = DVE.do(lambda e, c=c, a=a: e.scalar_tensor_tensor(E[0][:, a], E[1][:, a], w[:, 10 + c:11 + c],
                                                                       E[0][:, a], ALU.mult, ALU.add))
            dtok["e", h] = t3
            dtok["dq"] = tps[1]

        def turn_p(h, key, E, n):
            i, W = bank()
            PE.wait(dtok[key, h])
            for b in range(3):
                tp = PE.do(lambda e, b=b: e.transpose(W[:, 128 * b:128 * b + 128], E[:, 128 * b:128 * b + 128],
                                                      IDN[:, :]))
            efree[h % 2] = tp
            AC.wait(tp, pfree[h % 2])
            bank_free[i] = dtok["pt", n] = AC.do(lambda e: e.copy(PTS[h % 2], W[:, 0:384]))

        def d2(h):
            turn_p(h, "e", E2[h % 2][0], h)

        ot_free = [None]

        def d3(h):
            i, W = bank()
            P = PTS[h % 2]
            PE.wait(dtok["pt", h], dtok["v"])
            hs = slice(128 * h, 128 * h + 128)
            PE.run(mm(W[:, 0:128], P[:, 0:128], DV[:, 0, hs], True, True))
            PE.run(mm(W[:, 128:256], P[:, 128:256], DV[:, 0, hs], True, False))
            tp = PE.do(mm(W[:, 128:256], P[:, 256:384], DV[:, 1, hs], False, True))
            pfree[h % 2] = tp
            w = cols(4)
            AC.wait(tp, ot_free[0])
            for t in range(2):
                te = AC.do(lambda e, t=t: e.activation(OT[:, t, :], W[:, 128 * t:128 * t + 128], ACT.Square,
                                                       accum_out=w[:, t:t + 1]))
            PO.wait(te)
            t1 = PO.do(lambda e: e.tensor_scalar(w[:, 0:2], w[:, 0:2], 1 / 128, EPS, ALU.mult, ALU.add))
            t1 = rsqrt(w[:, 2:4], w[:, 0:2], t1)
            DVE.wait(te, t1)
            for t in range(2):
                t2 = DVE.do(lambda e, t=t: e.tensor_scalar(OT[:, t, :], W[:, 128 * t:128 * t + 128],
                                                           w[:, 2 + t:3 + t], 1.0 - LAMBDA_INIT,
                                                           ALU.mult, ALU.mult))
            bank_free[i] = dtok["ot", h] = t2

        def d4(h):
            i, W = bank()
            PE.wait(dtok["ot", h])
            for t in range(2):
                tp = PE.do(lambda e, t=t: e.transpose(W[:, 128 * t:128 * t + 128], OT[:, t, :], IDN[:, :]))
            ot_free[0] = tp
            DVE.wait(tp, dtok["dq"])
            bank_free[i] = dtok["om", h] = DVE.do(lambda e: e.tensor_scalar(
                DQ[:, h, :], W[:, 0:256], PC[:, C_GD:C_GD + 1], None, ALU.mult))

        for j in range(4):
            dq_chunk(j)
        d1(0)
        tm_panel(512, ev_dv)
        d1(1)
        d2(0)
        tm_panel(384, ev_ql)
        d3(0)
        d1(2)
        d2(1)
        tm_panel(320, ev_kl)
        d4(0)
        d3(1)
        d1(3)
        d2(2)
        d4(1)
        cs, sn = TR[:, 0], TR[:, 1]
        kr = KL[:, :, 256:320]
        DVE.wait(dtok["kl", 0], dtok["kl", 1], t_tb, *xt)
        AC.wait(*xt)
        for o, (a, b), op in ((0, (cs, sn), ALU.subtract), (32, (sn, cs), ALU.add)):
            t1 = DVE.do(lambda e, a=a: e.tensor_tensor(RA[:, 0], kr[:, :, 0:32], a, ALU.mult))
            t2 = DVE.do(lambda e, b=b: e.tensor_tensor(RA[:, 1], kr[:, :, 32:64], b, ALU.mult))
            DVE.wait(t1, t2)
            for d in (0, 64):
                t1 = DVE.do(lambda e, o=o, d=d, op=op: e.tensor_tensor(RT[:, :, o + d:o + d + 32], RA[:, 0],
                                                                       RA[:, 1], op))
            DVE.wait(t1)
        i, W = bank()
        PE.wait(t1)
        for t in range(2):
            tp = PE.do(lambda e, t=t, W=W: e.transpose(W[:, 128 * t:128 * t + 128], RT[:, t, :], IDN[:, :]))
        AC.wait(tp, t_zero)
        AC.do(lambda e, W=W: e.copy(KPE[0:64, 0, :], W[0:64, 0:256]))
        bank_free[i] = t_kpe = AC.do(lambda e, W=W: e.copy(KPE[64:128, 1, :], W[64:128, 0:256]))
        xfree[:] = now()
        lt = []
        for t in range(2):
            lt += turn(t, lambda k, t=t: QL[:, t, 128 * k:128 * k + 128], 3, [dtok["ql", t]],
                       lambda k: PC[:, C_GQ + k:C_GQ + k + 1])
            lt += turn(t, lambda k, t=t: KL[:, t, 128 * k:128 * k + 128], 2, [dtok["kl", t]],
                       lambda k: PC[:, C_GK + k:C_GK + k + 1],
                       S_=S[:, 3:5, :], H=XH[:, 3:5, :], L=XL[:, 3:5, :])
        d3(2)
        d2(3)
        QT2 = [Sf[:, 1536:1792], Sf[:, 1792:2048]]
        d4(2)

        def q_up(j):
            s = use()
            PE.wait(*lt)
            for g in range(2):
                i, W = bank()
                for f in range(2):
                    tp = fm_gemm(s, 3, 512, 256 * g + 128 * f, W[:, 256 * f:256 * f + 256])
                if g == 0:
                    AC.wait(tp)
                    te = AC.do(lambda e, W=W: e.copy(QN[:, 2 * j:2 * j + 2, :],
                                                     W[:, :].rearrange("p (f c) -> p f c", f=2)))
                else:
                    DVE.wait(tp, t_tb, dtok.get("qpe"))
                    DVE.do(lambda e, W=W: e.tensor_tensor(QT2[0], W[:, 0:256], CS[:, 0, :], ALU.mult))
                    te = DVE.do(lambda e, W=W: e.tensor_tensor(QT2[1], W[:, 256:512], CS[:, 1, :], ALU.mult))
                    DVE.wait(te)
                    dtok["qpe"] = DVE.do(lambda e: e.tensor_tensor(QPE[:, j, :], QT2[0], QT2[1], ALU.add))
                bank_free[i] = te
            release(s, tp)
            dtok["q", j] = [AC.last(), dtok["qpe"]]

        q_up(0)
        d3(3)
        q_up(1)
        d4(3)
        s = use()
        for g in range(2):
            i, W = bank()
            for f in range(2):
                h = 2 * g + f
                tp = fm_gemm(s, 2, 1024, 256 * h, W[:, 256 * f:256 * f + 256], xh=XH[:, 3:5, :], xl=XL[:, 3:5, :])
            AC.wait(tp)
            bank_free[i] = AC.do(lambda e, g=g, W=W: e.copy(KN[:, 2 * g:2 * g + 2, :],
                                                            W[:, :].rearrange("p (f c) -> p f c", f=2)))
        for t in range(2):
            i, W = bank()
            tk = slice(128 * t, 128 * t + 128)
            wv = [w[s][:, 0:2048].rearrange("p (k h c) -> p k h c", k=2, h=4)[:, :, :, 128:256] for w in (WH, WL)]
            W3 = W[:, :].rearrange("p (h c) -> p h c", h=4)
            for k in range(2):
                tp = three(W3, XH[:, 3 + k, tk], XL[:, 3 + k, tk], wv[0][:, k], wv[1][:, k], k == 0, k == 1, k == 1)
            AC.wait(tp)
            bank_free[i] = AC.do(lambda e, t=t, W=W: e.copy(V2[:, t, :], W[:, :]))
        release(s, tp)
        t_kv2 = AC.last()
        up_done = PE.last()

        def m1(h):
            i, W = bank()
            E = E2[h % 2][0]
            w = cols(6)
            PE.wait(*dtok["q", h // 2], t_kv2, t_kpe)
            for o, tq, n in ((slice(0, 128), slice(0, 128), 128), (slice(128, 384), slice(128, 256), 256)):
                PE.run(mm(W[:, o], QN[:, h, tq], KN[:, h, 0:n], True, False))
                tp = PE.do(mm(W[:, o], QPE[:, h // 2, tq], KPE[:, h % 2, 0:n], False, True))
            DVE.wait(tp, efree[h % 2])
            bank_free[i], te = softmax_rows(W, E, TB[4], 192 ** -0.5, w, 0)
            DVE.wait(te)
            t1 = DVE.do(lambda e: e.reciprocal(w[:, 4:6], w[:, 2:4]))
            DVE.wait(t1)
            DVE.do(lambda e: e.tensor_scalar(E[:, 0:128], E[:, 0:128], w[:, 4:5], None, ALU.mult))
            dtok["m", h] = DVE.do(lambda e: e.tensor_scalar(E[:, 128:384], E[:, 128:384], w[:, 5:6], None, ALU.mult))

        def m2(h):
            turn_p(h, "m", E2[h % 2][0], 4 + h)

        xo = {}

        def m3(h):
            i, W = bank()
            P = PTS[h % 2]
            PE.wait(dtok["pt", 4 + h])
            hs = slice(128 * h, 128 * h + 128)
            PE.run(mm(W[:, 0:128], V2[:, 0, hs], P[:, 0:128], True, True))
            PE.run(mm(W[:, 128:256], V2[:, 0, hs], P[:, 128:256], True, False))
            tp = PE.do(mm(W[:, 128:256], V2[:, 1, hs], P[:, 256:384], False, True))
            pfree[h % 2] = tp
            DVE.wait(tp, up_done)
            bank_free[i] = te = DVE.do(lambda e: e.tensor_copy(S[:, 4 + h, :], W[:, 0:256]))
            AC.wait(up_done)
            xo[2 + h // 2] = xo.get(2 + h // 2, []) + hilo(XH[:, 4 + h, :], XL[:, 4 + h, :], S[:, 4 + h, :], te)

        def r2(j):
            return row_chunk(j, 4, XH, XL, 2 * j, xo[j])

        m1(0)
        AC.wait(up_done)
        DVE.wait(up_done)
        for j in range(2):
            xo[j] = hilo(XH[:, 2 * j:2 * j + 2, :], XL[:, 2 * j:2 * j + 2, :], DQ[:, 2 * j:2 * j + 2, :],
                         dtok["om", 2 * j], dtok["om", 2 * j + 1])
        for f, h in ((m1, 1), (m2, 0), (r2, 0), (m1, 2), (m2, 1), (m3, 0), (r2, 1), (m1, 3), (m2, 2), (m3, 1),
                     (m2, 3), (m3, 2), (m3, 3), (r2, 2), (r2, 3)):
            ys = f(h)

        def gated(ys, n):
            for t in range(2):
                DVE.wait(ys[t], *x_ready[t], *t_gb)
                for h in range(2):
                    cs = slice(512 * h, 512 * h + 512)
                    tu = DVE.do(lambda e, t=t, h=h, cs=cs: e.tensor_tensor(U[:, t, cs], YB[2 * t + h][:, :],
                                                                           GB[:, n, cs], ALU.mult))
                    yb_free[2 * t + h] = tu
                DVE.wait(tu)
                x_ready[t] = [DVE.do(lambda e, t=t: e.tensor_tensor(X[:, t, :], X[:, t, :], U[:, t, :], ALU.add))]

        xfree[:] = now()
        DVE.wait(*xfree)
        gated(ys, 0)
        xt = rms_turn(32, 24, x_ready)
        cut = now()
        AC.wait(*cut)
        DVE.wait(*cut)
        SG = [AR[:, 1024 * n:1024 * n + 512] for n in range(2)]
        SU = [AR[:, 1024 * n + 512:1024 * n + 1024] for n in range(2)]
        fo = {}
        g_i, t_gf = bvec(I["g_final_2"])
        for j in range(12):
            if j < 11:
                n = j % 2
                bs = []
                for m in range(2):
                    s = use()
                    i, W = bank()
                    PE.wait(*xt)
                    for f in range(2):
                        tp = fm_gemm(s, 8, 256, 128 * f, W[:, 256 * f:256 * f + 256])
                    release(s, tp)
                    if m == 0:
                        AC.wait(tp, *f_free[n])
                        bank_free[i] = tg = AC.do(lambda e, W=W, n=n: e.activation(SG[n], W[:, :], ACT.Silu))
                    else:
                        DVE.wait(tp, tg, *f_free[n])
                        bank_free[i] = tu = DVE.do(lambda e, W=W, n=n: e.tensor_tensor(SU[n], W[:, :], SG[n],
                                                                                      ALU.mult))
                fo[j] = hilo(FH[n][:, :], FL[n][:, :], SU[n], tu)
            if j > 0:
                n = (j - 1) % 2
                v = lambda b: b[n][:, :].rearrange("p (f c) -> p f c", f=2)
                ys = row_chunk(j - 1, 11, v(FH), v(FL), 0, fo[j - 1])
                f_free[n] = [PE.last(), DVE.last()]
        DVE.wait(PE.last())
        gated(ys, 1)
        outs = []
        for t in range(2):
            tr = stats(t, x_ready[t], True, X)
            DVE.wait(tr, t_gf)
            tz = DVE.do(lambda e, t=t: e.scalar_tensor_tensor(U[:, t, :], X[:, t, :], BN[:, t, 14:15],
                                                              BV[g_i][:, :], ALU.mult, ALU.mult))
            SP.wait(tz)
            outs.append(load(SP, f"out{t}", (out[0, 128 * t:128 * t + 128, :], U[:, t, :])))
        SP.wait(*outs)
        assert split_n[0] == len(chunks) and issued[0] == len(chunks) and used[0] == mm_n[0]

        block = ctx.enter_context(nc.Block())

        @block.sync
        def _(e):
            SP.emit(e)

        @block.gpsimd
        def _(e):
            PO.emit(e)

        @block.scalar
        def _(e):
            AC.emit(e)

        @block.vector
        def _(e):
            DVE.emit(e)

        @block.tensor
        def _(e):
            PE.emit(e)


def constants():
    f = np.float32
    p = np.arange(128)
    c = {"c_idn": np.eye(128, dtype=f)}
    sel = np.zeros((4, 4, 128), f)
    for h in range(4):
        sel[h, h] = 1.0
    c["c_sel"] = sel.reshape(4, 512)
    c["c_msk"] = np.concatenate([np.where(p[None, :] >= p[:, None], 0.0, NEG), np.zeros((128, 128))], 1).astype(f)
    win = np.zeros((4, 256, 256), f)
    t = np.arange(256)
    for g, w in enumerate((2, 4, 8, 16)):
        inside = (t[None, :] >= t[:, None]) & (t[None, :] - t[:, None] < w)
        win[g] = inside / np.minimum(t + 1, w).astype(f)[None, :]
        win[g] -= np.eye(256, dtype=f)
    c["c_win"] = np.concatenate([np.concatenate([win[g, 0:128, :], win[g, 128:256, 128:256]], 1)
                                 for g in range(4)], 1).astype(f)
    rel = (128 + p[:, None] - t[None, :]).astype(f)
    slopes = 2.0 ** (-8.0 * np.arange(1, 5, dtype=f) / 4)
    c["c_alibi"] = np.concatenate([np.where(rel >= 0, -s * rel, NEG) for s in slopes], 1).astype(f)
    c["c_causal"] = np.where(rel >= 0, 0.0, NEG).astype(f)
    inv = (f(10000.0) ** (-np.arange(0, 64, 2, dtype=f) / f(64))).astype(f)
    ang = (np.arange(256, dtype=f)[:, None] * inv[None, :]).astype(f)
    cos, sin = np.cos(ang).astype(f), np.sin(ang).astype(f)
    c["c_rope_t"] = np.concatenate([x[128 * t:128 * t + 128] for x in (cos, sin) for t in range(2)], 1)
    c["c_rope_f"] = np.concatenate([np.tile(cos.T, (4, 1)), np.tile(np.concatenate([-sin.T, sin.T]), (2, 1))], 1)
    return {k: np.ascontiguousarray(v, dtype=f) for k, v in c.items()}


_INS = ["x", "mem", "mlstm_w_in", "mlstm_gate_b", "mlstm_conv_w", "mlstm_norm_g", "mlstm_w_out", "pool_w",
        "pool_scale", "mem_w_kv", "xattn_wq", "xattn_wo", "mlp_w1", "mlp_b1", "mlp_w2", "mlp_b2", "ln_g", "ln_b",
        "c_2", "w_ada_2", "b_ada_2", "g_mix_2", "w_in_2", "lambda_q1_2", "lambda_k1_2", "lambda_q2_2",
        "lambda_k2_2", "g_diff_out_2", "g_q_lat_2", "w_q_up_2", "g_kv_lat_2", "w_kv_up_2", "w_out_2", "g_ffn_2",
        "w_ffn_gate_2", "w_ffn_up_2", "w_ffn_down_2", "g_final_2"]


def kernel(**inputs):
    import concourse.bacc as bacc
    from concourse.bass_utils import run_bass_kernel_spmd

    nc = bacc.Bacc("TRN2", target_bir_lowering=False, num_devices=1)
    arrays, args = {}, {}
    for name, a in [(n, np.ascontiguousarray(inputs[n])) for n in _INS] + list(constants().items()):
        arrays[f"in_{name}"] = a
        args[name] = nc.dram_tensor(f"in_{name}", a.shape, mybir.dt.from_np(a.dtype), kind="ExternalInput").ap()
    out = nc.dram_tensor("out_0", (1, 256, 1024), F32, kind="ExternalOutput").ap()
    build_program(nc, args, out)
    r = run_bass_kernel_spmd(nc, [arrays], core_ids=[0])
    return r.results[0]["out_0"]
```

```python
import math
from contextlib import ExitStack

import numpy as np

import concourse.bass as bass
from concourse import mybir

F32 = mybir.dt.float32
F32R = mybir.dt.float32r
ACT = mybir.ActivationFunctionType
ALU = mybir.AluOpType
AX = mybir.AxisListType.X

ALPHA = 4 ** 0.25
LN_EPS = 1e-5
EPS = 1e-6
NEG = -1e30
NR = 4
NS = 4
AHEAD = 3
CH = 2048
LAMBDA_INIT = 0.8 - 0.6 * math.exp(0.0)


class Lane:

    def __init__(self, sem):
        self.sem, self.n, self.q, self.seen = sem, 0, [], {}

    def wait(self, *tokens):
        for t in tokens:
            if t is None:
                continue
            if isinstance(t, list):
                self.wait(*t)
                continue
            sem, val = t
            if self.seen.get(id(sem), 0) < val:
                self.seen[id(sem)] = val
                self.q.append(lambda e, s=sem, v=val: e.wait_ge(s, v))

    def run(self, f):
        self.q.append(f)

    def do(self, f):
        self.n += 1
        self.q.append(lambda e, f=f: f(e).then_inc(self.sem, 1))
        return (self.sem, self.n)

    def last(self):
        return (self.sem, self.n)

    def emit(self, e):
        for f in self.q:
            f(e)


def build_program(nc, I, out):
    ctx = ExitStack()
    with ctx:
        def sb(name, shape, dt=F32):
            return ctx.enter_context(nc.sbuf_tensor(name, shape, dt))

        def sem(name):
            return ctx.enter_context(nc.semaphore(name))

        RAW = [sb(f"raw{i}", [128, CH]) for i in range(NR)]
        WH = [sb(f"wh{i}", [128, CH], F32R) for i in range(NS)]
        WL = [sb(f"wl{i}", [128, CH], F32R) for i in range(NS)]
        X = sb("X", [128, 2, 1024])
        U = sb("U", [128, 2, 1024])
        S = sb("S", [128, 8, 256])
        XH = sb("XH", [128, 8, 256], F32R)
        XL = sb("XL", [128, 8, 256], F32R)
        KV = sb("KV", [128, 4096])
        AR = sb("AR", [128, 8800])
        FHT = sb("FHT", [128, 1280], F32R)
        FLT = sb("FLT", [128, 1280], F32R)
        FH = [FHT[:, 512 * i:512 * i + 512] for i in range(2)]
        FL = [FLT[:, 512 * i:512 * i + 512] for i in range(2)]
        BV = [sb(f"bv{i}", [128, 1024]) for i in range(2)]
        IDN = sb("IDN", [128, 128])
        PC = sb("PC", [128, 278])
        SM = sb("SM", [128, 352])
        BN = sb("BN", [128, 2, 16])

        MOD = AR[:, 0:6144]
        sm_at = [0]

        def cols(n):
            sm_at[0] += n
            assert sm_at[0] <= 352
            return SM[:, sm_at[0] - n:sm_at[0]]

        YB = [ctx.enter_context(nc.psum_tensor(f"YB{i}", [128, 512], F32)) for i in range(4)]
        WBt = [ctx.enter_context(nc.psum_tensor(f"WB{i}", [128, 512], F32)) for i in range(4)]

        PE, DVE, AC, PO = (Lane(sem("s_" + n)) for n in ("pe", "dve", "act", "pool"))
        SP = Lane(None)
        s_raw = [sem(f"s_raw{i}") for i in range(NR)]
        s_dma = {}

        def load(lane, name, *pairs):
            if name not in s_dma:
                s_dma[name] = [sem("d_" + name), 0]
            s = s_dma[name]
            for dst, src in pairs:
                s[1] += 16
                lane.run(lambda e, d=dst, r=src, q=s[0]: e.dma_start(d, r).then_inc(q, 16))
            return (s[0], s[1])

        def now():
            return [PE.last(), DVE.last(), AC.last(), PO.last()]

        bank_free = [None] * 4
        bank_at = [0]

        def bank():
            i = bank_at[0] % 4
            bank_at[0] += 1
            PE.wait(bank_free[i])
            return i, WBt[i]

        chunks = []

        def add(src, a, b, kind="mm"):
            chunks.append((src, a, b, kind))

        def rows(w, k0, nk, c0, c1):
            return w[k0 * 128:(k0 + nk) * 128, c0:c1].rearrange("(k p) c -> p k c", p=128)

        w_in, w_kv = I["mlstm_w_in"][0], I["mem_w_kv"]
        for j in range(4):
            add(rows(w_in, 0, 8, 256 * j, 256 * j + 256), 8, 256)
        for j in range(4):
            for kh in range(2):
                add(rows(w_in, 4 * kh, 4, 1024 + 512 * j, 1536 + 512 * j), 4, 512)
        for j in range(4):
            add(rows(w_kv, 0, 8, 256 * j, 256 * j + 256), 8, 256)
        for j in range(2):
            for kh in range(2):
                add(rows(w_kv, 4 * kh, 4, 1024 + 512 * j, 1536 + 512 * j), 4, 512)
        for j in range(4):
            add(rows(I["mlstm_w_out"][0], 2 * j, 2, 0, 1024), 2, 1024)
        ada = [(k, c) for k in range(8) for c in range(3)]
        for i in range(2):
            if i == 1:
                add(I["pool_w"][0].rearrange("g (k p) c -> p (g k) c", p=128), 8, 256)
            for j in range(4):
                add(rows(I["xattn_wq"][i], 0, 8, 256 * j, 256 * j + 256), 8, 256)
            for j in range(4):
                add(rows(I["xattn_wo"][i], 2 * j, 2, 0, 1024), 2, 1024)
            for j in range(17):
                if j < 16:
                    add(rows(I["mlp_w1"][i], 0, 8, 256 * j, 256 * j + 256), 8, 256)
                if j > 0:
                    add(rows(I["mlp_w2"][i], 2 * j - 2, 2, 0, 1024), 2, 1024)
                if 2 <= j < 14:
                    k, c = ada.pop(0)
                    add(I["w_ada_2"][0][k * 128:(k + 1) * 128, 2048 * c:2048 * c + 2048], 1, 2048, ("ada", k, c))
        w2i = I["w_in_2"][0]
        for c0, c1 in ((1920, 2240), (1536, 1920)):
            for kh in range(2):
                add(rows(w2i, 4 * kh, 4, c0, c1), 4, c1 - c0)
        w_dqk = lambda j: add(rows(w2i, 0, 8, 256 * j, 256 * j + 256), 8, 256)
        w_dv = lambda kh: add(rows(w2i, 4 * kh, 4, 1024, 1536), 4, 512)
        w_qup = lambda j: add(rows(I["w_q_up_2"][0], 0, 3, 384 * j, 384 * j + 384), 3, 384, "qup")
        w_dqk(0)
        w_dqk(2)
        w_dqk(1)
        add(rows(I["w_kv_up_2"][0], 0, 2, 0, 1024), 2, 1024)
        w_dv(0)
        w_qup(0)
        w_dv(1)
        w_dqk(3)
        w_qup(1)
        for j in (0, 2, 1, 3):
            add(rows(I["w_out_2"][0], 2 * j, 2, 0, 1024), 2, 1024)
        for j in range(12):
            if j < 11:
                add(rows(I["w_ffn_gate_2"][0], 0, 8, 256 * j, 256 * j + 256), 8, 256)
                add(rows(I["w_ffn_up_2"][0], 0, 8, 256 * j, 256 * j + 256), 8, 256)
            if j > 0:
                add(rows(I["w_ffn_down_2"][0], 2 * j - 2, 2, 0, 1024), 2, 1024)

        issued, split_n, mm_n = [0], [0], [0]
        raw_free = [None] * NR
        slot_done = [None] * NS
        ready = {}
        cact = cols(8)
        small = {}

        def issue():
            n = issued[0]
            if n >= len(chunks):
                return
            issued[0] += 1
            src, a, b, _ = chunks[n]
            SP.wait(raw_free[n % NR])
            dst = RAW[n % NR][:, 0:a * b]
            if len(src.shape) == 3:
                dst = dst.rearrange("p (a b) -> p a b", a=a)
            SP.run(lambda e: e.dma_start(dst, src).then_inc(s_raw[n % NR], 16))

        def split_next():
            n = split_n[0]
            split_n[0] += 1
            src, a, b, kind = chunks[n]
            landed = (s_raw[n % NR], 16 * (n // NR + 1))
            raw = RAW[n % NR]
            if isinstance(kind, tuple):
                _, k, c = kind
                acc = MOD[:, 2048 * c:2048 * c + 2048]
                DVE.wait(landed, small["cact"], small.get(("ada", c)))
                if k == 0:
                    t = DVE.do(lambda e: e.tensor_scalar(acc, raw[:, :], cact[:, 0:1], None, ALU.mult))
                else:
                    t = DVE.do(lambda e: e.scalar_tensor_tensor(acc, raw[:, :], cact[:, k:k + 1], acc,
                                                                ALU.mult, ALU.add))
                small[("ada", c)] = t
                raw_free[n % NR] = [t]
                issue()
                return False
            m = mm_n[0]
            mm_n[0] += 1
            s = m % NS
            AC.wait(landed, slot_done[s])
            DVE.wait(landed, slot_done[s])
            if kind == "qup":
                r = raw[:, 0:1152].rearrange("p (k h c) -> p k h c", k=3, h=2)
                parts = []
                for w in (WH[s], WL[s]):
                    o = w[:, 0:1536].rearrange("p (k c) -> p k c", k=3)
                    parts.append([
                        o[:, :, 0:256].rearrange("p k (h c) -> p k h c", h=2),
                        o[:, :, 256:384].rearrange("p k (h c) -> p k h c", h=2),
                        o[:, :, 384:512].rearrange("p k (h c) -> p k h c", h=2)[:, :, :, 0:32],
                        o[:, :, 384:512].rearrange("p k (h c) -> p k h c", h=2)[:, :, :, 32:64]])
                srcs = [r[:, :, :, 0:128], r[:, :, :, 128:192], r[:, :, :, 160:192], r[:, :, :, 128:160]]
                for hi, lo, x in zip(parts[0], parts[1], srcs):
                    th = AC.do(lambda e, hi=hi, x=x: e.copy(hi, x))
                    DVE.wait(th)
                    tl = DVE.do(lambda e, hi=hi, lo=lo, x=x: e.tensor_tensor(lo, x, hi.bitcast(F32), ALU.subtract))
            else:
                hi, lo, x = WH[s][:, 0:a * b], WL[s][:, 0:a * b], raw[:, 0:a * b]
                th = AC.do(lambda e: e.copy(hi, x))
                DVE.wait(th)
                tl = DVE.do(lambda e: e.tensor_tensor(lo, x, hi.bitcast(F32), ALU.subtract))
            raw_free[n % NR] = [th, tl]
            ready[m] = (s, [th, tl])
            issue()
            return True

        used = [0]

        def use(later=False):
            m = used[0]
            used[0] += 1
            if not later:
                catch_up()
            while not later and mm_n[0] <= m + AHEAD - 1 and split_n[0] < len(chunks):
                if split_next():
                    held[0] = max(held[0] - 1, 0)
            s, (th, tl) = ready.pop(m)
            return s, th, tl

        held = [0]

        def release(s, tok):
            slot_done[s[0]] = tok
            held[0] += 1

        def catch_up():
            while held[0] > 0 and split_n[0] < len(chunks):
                if split_next():
                    held[0] -= 1
            held[0] = 0

        def mm(o, l, r, start, stop):
            return lambda e: e.matmul(o, l, r, start=start, stop=stop)

        class Part:

            def __init__(self, t, k0, k1, hi, lo):
                self.t, self.k0, self.k1, self.hi, self.lo = t, k0, k1, hi, lo

        def wait_part(parts, t, k, lo):
            for p in parts:
                if p.k0 <= k < p.k1 and (t is None or p.t is None or t == p.t):
                    PE.wait(p.lo if lo else p.hi)

        def passes(o, k_n, terms, start, stop):
            for n in range(3):
                for k in range(k_n):
                    wait, l, r = terms(k)[n]
                    wait()
                    f = mm(o, l, r, start and n == 0 and k == 0, stop and n == 2 and k == k_n - 1)
                    tok = PE.do(f) if n == 2 and k == k_n - 1 else PE.run(f)
            return tok

        def fm_gemm(s, a, b, off, o, parts, xh=None, xl=None):
            xh, xl = xh or XH, xl or XL
            _, th, tl = s

            def terms(k):
                l = slice(k * b + off, k * b + off + 128)
                hi, lo = WH[s[0]][:, l], WL[s[0]][:, l]
                return ((lambda: (PE.wait(th), wait_part(parts, None, k, False)), hi, xh[:, k, :]),
                        (lambda: PE.wait(tl), lo, xh[:, k, :]),
                        (lambda: wait_part(parts, None, k, True), hi, xl[:, k, :]))
            return passes(o, a, terms, True, True)

        def tm_gemm(s, a, b, c0, c1, o, t, k0, start, stop, parts, xh=None, xl=None, w=None):
            xh, xl = xh or XH, xl or XL
            tk = slice(128 * t, 128 * t + 128)
            _, th, tl = s

            def terms(k):
                r = slice(k * b + c0, k * b + c1)
                hi, lo = (w(WH[s[0]], k), w(WL[s[0]], k)) if w else (WH[s[0]][:, r], WL[s[0]][:, r])
                x, y = xh[:, k0 + k, tk], xl[:, k0 + k, tk]
                return ((lambda: (PE.wait(th), wait_part(parts, t, k0 + k, False)), x, hi),
                        (lambda: PE.wait(tl), x, lo),
                        (lambda: wait_part(parts, t, k0 + k, True), y, hi))
            return passes(o, a, terms, start, stop)

        yb_free = [None] * 4

        def row_chunks(js, n, xs):
            ss = [use() for _ in js]
            if js[0] == 0:
                PE.wait(*yb_free)
            toks = []
            for t in range(2):
                for nb in range(2):
                    for j, s, (parts, xh, xl, xk) in zip(js, ss, xs):
                        tok = tm_gemm(s, 2, 1024, 512 * nb, 512 * nb + 512, YB[2 * t + nb][:, :], t, xk,
                                      j == 0, j == n - 1, parts, xh, xl)
                    toks.append(tok)
            for s in ss:
                release(s, tok)
            return toks

        def hilo(t, k0, k1, hi, lo, src, *wait, lane=None):
            lane = lane or AC
            lane.wait(*wait)
            DVE.wait(*wait)
            th = lane.do((lambda e: e.copy(hi, src)) if lane is AC else (lambda e: e.tensor_copy(hi, src)))
            DVE.wait(th)
            tl = DVE.do(lambda e: e.tensor_tensor(lo, src, hi.bitcast(F32), ALU.subtract))
            return Part(t, k0, k1, th, tl)

        def hilo_bank(t, k0, k1, hi, lo, i, src, *wait):
            AC.wait(*wait)
            DVE.wait(*wait)
            th = AC.do(lambda e: e.copy(hi, src))
            DVE.wait(th)
            bank_free[i] = tl = DVE.do(lambda e: e.tensor_tensor(lo, src, hi.bitcast(F32), ALU.subtract))
            return Part(t, k0, k1, th, tl)

        xfree = [None]

        def turn_pe(src, ks, wait):
            i, W = bank()
            PE.wait(*wait)
            for n, k in enumerate(ks):
                f = (lambda e, k=k, n=n, W=W: e.transpose(W[:, 128 * n:128 * n + 128], src(k), IDN[:, :]))
                tp = PE.do(f) if k == ks[-1] else PE.run(f)
            return i, W, tp

        def turn(t, src, nk, wait, H=None, L=None, g=None):
            H, L = H if H is not None else XH, L if L is not None else XL
            tk = slice(128 * t, 128 * t + 128)
            parts = []
            for k0 in range(0, nk, 4):
                ks = range(k0, min(nk, k0 + 4))
                i, W, tp = turn_pe(src, ks, wait)
                AC.wait(tp, *xfree)
                DVE.wait(*xfree)
                if g is None:
                    w = W[:, 0:128 * len(ks)].rearrange("p (k c) -> p k c", k=len(ks))
                    parts.append(hilo_bank(t, k0, ks[-1] + 1, H[:, k0:ks[-1] + 1, tk], L[:, k0:ks[-1] + 1, tk],
                                           i, w))
                    continue
                for n, k in enumerate(ks):
                    th = AC.do(lambda e, n=n, k=k, W=W: e.activation(H[:, k, tk], W[:, 128 * n:128 * n + 128],
                                                                     ACT.Identity, scale=g(k)))
                DVE.wait(th)
                for n, k in enumerate(ks):
                    tl = DVE.do(lambda e, n=n, k=k, W=W: e.scalar_tensor_tensor(
                        L[:, k, tk], W[:, 128 * n:128 * n + 128], g(k), H[:, k, tk].bitcast(F32),
                        ALU.mult, ALU.subtract))
                bank_free[i] = tl
                parts.append(Part(t, k0, ks[-1] + 1, th, tl))
            return parts

        def turn_norm(z, stages, g, b):
            parts, lows = [], []

            def evac(t, q, i, W, tp, lane):
                tk = slice(128 * t, 128 * t + 128)
                lane.wait(tp, *xfree)
                for n, k in enumerate((2 * q, 2 * q + 1)):
                    w = W[:, 128 * n:128 * n + 128]
                    if lane is AC:
                        te = AC.do(lambda e, k=k, w=w: e.activation(S[:, k, tk], w, ACT.Identity,
                                                                    bias=b(k), scale=g(k)))
                    else:
                        te = DVE.do(lambda e, k=k, w=w: e.tensor_scalar(S[:, k, tk], w, g(k), b(k),
                                                                        ALU.mult, ALU.add))
                bank_free[i] = te
                lane.wait(te)
                hi, src = XH[:, 2 * q:2 * q + 2, tk], S[:, 2 * q:2 * q + 2, tk]
                th = lane.do((lambda e: e.copy(hi, src)) if lane is AC else (lambda e: e.tensor_copy(hi, src)))
                p = Part(t, 2 * q, 2 * q + 2, th, None)
                parts.append(p)
                lows.append((p, hi, XL[:, 2 * q:2 * q + 2, tk], src))

            tz = [None, None]
            stages[0]()
            tz[0] = z(0)
            stages[1]()
            for q in range(4):
                src = lambda k: U[:, 0, 128 * k:128 * k + 128]
                evac(0, q, *turn_pe(src, (2 * q, 2 * q + 1), [tz[0]]), DVE if q == 1 else AC)
            tz[1] = z(1)
            for q in range(4):
                src = lambda k: U[:, 1, 128 * k:128 * k + 128]
                evac(1, q, *turn_pe(src, (2 * q, 2 * q + 1), [tz[1]]), DVE if q % 2 else AC)
            for p, hi, lo, src in lows:
                DVE.wait(p.hi, *xfree)
                p.lo = DVE.do(lambda e, hi=hi, lo=lo, src=src: e.tensor_tensor(lo, src, hi.bitcast(F32),
                                                                               ALU.subtract))
            catch_up()
            return parts

        MH = cols(2)
        t_mh = PO.do(lambda e: e.memset(MH, -0.5))

        def rsqrt(o, x, *wait):
            PO.wait(*wait, t_mh)
            return PO.do(lambda e: e.tensor_tensor(o, x, MH[:, 0:o.shape[1]], ALU.pow))

        def bn(t, h):
            return DVE.do(lambda e: e.bn_stats(BN[:, t, 6 * h:6 * h + 6], U[:, t, 512 * h:512 * h + 512]))

        def stats(t, tb):
            DVE.wait(tb)
            tb = DVE.do(lambda e: e.bn_aggr(BN[:, t, 12:14], BN[:, t, 0:12]))
            DVE.wait(tb)
            tb = DVE.do(lambda e: e.tensor_scalar(BN[:, t, 13:14], BN[:, t, 13:14], LN_EPS, None, ALU.add))
            return rsqrt(BN[:, t, 14:15], BN[:, t, 13:14], tb)

        bv_n = [0]
        bv_free = [None] * 2

        def bvec(src):
            n = bv_n[0]
            bv_n[0] += 1
            PO.wait(bv_free[n % 2])
            tok = load(PO, f"bv{n % 2}", (BV[n % 2][:, :], src.partition_broadcast(128)))
            return n % 2, tok

        x_ready = [[None], [None]]

        def layer_norm(ytoks, i, j, b2=False, turned=True, yscale=None):
            gb_ = {}

            def vectors():
                if not gb_:
                    gb_["g"] = bvec(I["ln_g"][i, j])
                    gb_["b"] = bvec(I["ln_b"][i, j])

            if yscale is None:
                vectors()
            tr = {}

            def head(t, between=None):
                DVE.wait(*x_ready[t])
                for h in range(2):
                    cs = slice(512 * h, 512 * h + 512)
                    DVE.wait(ytoks[2 * t + h])
                    if yscale is not None:
                        DVE.wait(yscale[1])
                        tu = DVE.do(lambda e, t=t, h=h, cs=cs: e.tensor_tensor(
                            U[:, t, cs], YB[2 * t + h][:, :], BV[yscale[0]][:, cs], ALU.mult))
                        yb_free[2 * t + h] = tu
                        DVE.wait(tu)
                        tu = DVE.do(lambda e, t=t, cs=cs: e.scalar_tensor_tensor(
                            U[:, t, cs], X[:, t, cs], ALPHA, U[:, t, cs], ALU.mult, ALU.add))
                    else:
                        tu = DVE.do(lambda e, t=t, h=h, cs=cs: e.scalar_tensor_tensor(
                            U[:, t, cs], X[:, t, cs], 1.0 if b2 else ALPHA, YB[2 * t + h][:, :],
                            ALU.mult, ALU.add))
                        yb_free[2 * t + h] = tu
                    DVE.wait(tu)
                    tb = bn(t, h)
                    if h == 0 and between:
                        between()
                if yscale is not None and t == 1:
                    bv_free[yscale[0]] = tu
                tr[t] = stats(t, tb)

            def z(t):
                DVE.wait(tr[t])
                tz = DVE.do(lambda e, t=t: e.tensor_scalar(U[:, t, :], U[:, t, :], BN[:, t, 12:13],
                                                           BN[:, t, 14:15], ALU.subtract, ALU.mult))
                x_ready[t] = [tz]
                return tz

            if turned:
                c = 32 + (i * 3 + j) * 8
                parts = turn_norm(z, [lambda: head(0), lambda: head(1)], lambda k: PC[:, c + k:c + k + 1],
                                  lambda k: PC[:, c + 48 + k:c + 49 + k])
                vectors()
                (gi, tg), (bi, tb_) = gb_["g"], gb_["b"]
                for t in range(2):
                    PO.wait(*x_ready[t], tg)
                    tx = PO.do(lambda e, t=t: e.tensor_tensor(X[:, t, :], U[:, t, :], BV[gi][:, :], ALU.mult))
                    PO.wait(tx, tb_)
                    x_ready[t] = [PO.do(lambda e, t=t: e.tensor_tensor(X[:, t, :], X[:, t, :], BV[bi][:, :],
                                                                       ALU.add))]
            else:
                parts = None
                (gi, tg), (bi, tb_) = gb_["g"], gb_["b"]
                tc = {}

                def centre(t):
                    DVE.wait(tr[t], tg)
                    tc[t] = DVE.do(lambda e: e.scalar_tensor_tensor(
                        U[:, t, :], U[:, t, :], BN[:, t, 12:13], BV[gi][:, :], ALU.subtract, ALU.mult))

                def scale(t):
                    DVE.wait(tc[t], tb_)
                    x_ready[t] = [DVE.do(lambda e: e.scalar_tensor_tensor(
                        X[:, t, :], U[:, t, :], BN[:, t, 14:15], BV[bi][:, :], ALU.mult, ALU.add))]

                head(0)
                head(1, lambda: centre(0))
                scale(0)
                centre(1)
                scale(1)
            bv_free[gi] = bv_free[bi] = [x_ready[0][0], x_ready[1][0]]
            return parts

        t_idn = load(SP, "idn", (IDN[:, :], I["c_idn"]))
        t_x = [load(SP, f"x{t}", (X[:, t, :], I["x"][0, 128 * t:128 * t + 128, :])) for t in range(2)]
        for _ in range(2):
            issue()
        GRAW = BV[1][:, 768:832].rearrange("p (k c) -> p k c", k=8)
        gb = cols(2)
        t_g = load(SP, "gates", (GRAW, w_in[:, 3072:3080].rearrange("(k p) c -> p k c", p=128)),
                   (gb[0:4, 0:1], I["mlstm_gate_b"][0, 0:4].rearrange("(p a) -> p a", a=1)),
                   (gb[0:4, 1:2], I["mlstm_gate_b"][0, 4:8].rearrange("(p a) -> p a", a=1)))

        QP = AR[:, 0:8 * 260].rearrange("p (k c) -> p k c", k=8)
        QC = AR[:, 2080:2080 + 2048].rearrange("p (k c) -> p k c", k=8)
        V1 = AR[:, 4128:4128 + 2064].rearrange("p (t h c) -> p t h c", t=2, h=4)
        OG = AR[:, 6192:6192 + 2048].rearrange("p (t c) -> p t c", t=2)
        GT = AR[:, 8240:8240 + 256]
        MSK = AR[:, 8544:8800]
        ROWS = QC.rearrange("p k c -> p (k c)")[:, 0:384].rearrange("p (r c) -> p r c", r=3)
        G = [BV[0][0:4, 256 * n:256 * n + 256] for n in range(4)] + [BV[1][0:4, 0:256]]
        CSEL = BV[1][0:4, 256:768]

        ms_rows = PO.do(lambda e: e.memset(ROWS[:, 2, :], 0.0))
        vec = lambda v: v.rearrange("(k c) -> k c", c=128)
        mat = lambda v: v.rearrange("i (k c) -> (i k) c", c=128)
        lnr = lambda v: v.rearrange("i j (k c) -> (i j k) c", c=128)
        SP.wait(ms_rows)
        t_rows = load(SP, "rows",
                      (ROWS[0:32, 0, :], mat(I["mlstm_conv_w"][0])),
                      (ROWS[32:80, 0, :], lnr(I["ln_g"])),
                      (ROWS[80:128, 0, :], lnr(I["ln_b"])),
                      (ROWS[0:64, 1, :], mat(I["mlp_b1"])),
                      (ROWS[64:72, 1, :], vec(I["mlstm_norm_g"][0])),
                      (ROWS[72:120, 1, :], vec(I["b_ada_2"][0])),
                      (ROWS[120:128, 1, :], vec(I["c_2"][0])),
                      (ROWS[0:8, 2, :], vec(I["g_mix_2"][0])),
                      (ROWS[8:16, 2, :], vec(I["g_ffn_2"][0])),
                      (ROWS[16:19, 2, :], vec(I["g_q_lat_2"][0])),
                      (ROWS[19:21, 2, :], vec(I["g_kv_lat_2"][0])),
                      (ROWS[21:22, 2, :], vec(I["g_diff_out_2"][0])))
        for _ in range(NR - 2):
            issue()
        t_tab = load(PO, "tab", (CSEL, I["c_sel"]), (MSK[:, :], I["c_msk"]))
        t_mem = load(PO, "mem", (U[:, :, :], I["mem"][0].rearrange("(t p) c -> p t c", p=128)))
        GH = FH[0][:, :].rearrange("p (k c) -> p k c", k=8)
        GL = FL[0][:, :].rearrange("p (k c) -> p k c", k=8)
        DVE.do(lambda e: e.memset(GH.bitcast(F32), 0.0))
        z2 = DVE.do(lambda e: e.memset(GL.bitcast(F32), 0.0))
        z3 = DVE.do(lambda e: e.memset(QP[:, :, 0:3], 0.0))
        z4 = DVE.do(lambda e: e.memset(V1[:, :, :, 256:258], 1.0))
        z5 = DVE.do(lambda e: e.memset(GT[0:64, :], 0.0))

        PE.wait(t_idn)
        xt = []
        for t in range(2):
            xt += turn(t, lambda k, t=t: X[:, t, 128 * k:128 * k + 128], 8, [t_x[t]])
        split_next()
        C_LNG, C_LNB, C_B1, C_NG, C_BA, C_C = 32, 80, 128, 192, 200, 248
        C_GM, C_GF, C_GQ, C_GK, C_GD = 256, 264, 272, 275, 277

        def columns():
            ci, CW = bank()
            PE.wait(t_rows)
            for r in range(3):
                tp = PE.do(lambda e, r=r: e.transpose(CW[:, 128 * r:128 * r + 128], ROWS[:, r, :], IDN[:, :]))
            AC.wait(tp)
            small["pc"] = AC.do(lambda e: e.copy(PC[:, :], CW[:, 0:278]))
            bank_free[ci] = small["pc"]

        def gates():
            AC.wait(t_g, z2)
            DVE.wait(t_g)
            for o, c in ((0, 0), (32, 4)):
                th = AC.do(lambda e, o=o, c=c: e.copy(GH[:, :, o:o + 4], GRAW[:, :, c:c + 4]))
                DVE.wait(th)
                tl = DVE.do(lambda e, o=o, c=c: e.tensor_tensor(GL[:, :, o:o + 4], GRAW[:, :, c:c + 4],
                                                                GH[:, :, o:o + 4].bitcast(F32), ALU.subtract))
            gi, GW = bank()
            PE.wait(z2)
            tgm = passes(GW[0:64, 0:256], 8, lambda k: (
                (lambda: (PE.wait(th), wait_part(xt, None, k, False)), GH[:, k, :], XH[:, k, :]),
                (lambda: PE.wait(tl), GL[:, k, :], XH[:, k, :]),
                (lambda: wait_part(xt, None, k, True), GH[:, k, :], XL[:, k, :])), True, True)
            DVE.wait(tgm, t_g)
            DVE.do(lambda e: e.tensor_scalar(G[0], GW[0:4, 0:256], gb[0:4, 0:1], None, ALU.add))
            tb = DVE.do(lambda e: e.tensor_copy(G[1], GW[32:36, 0:256]))
            bank_free[gi] = tb
            DVE.wait(tb)
            tb = DVE.do(lambda e: e.tensor_scalar(G[1], G[1], gb[0:4, 1:2], None, ALU.add))
            DVE.wait(tb)
            tc = DVE.do(lambda e: e.scalar_tensor_tensor(G[2], G[1], -1.0, G[1], ALU.mult, ALU.max))
            yield
            AC.wait(tc)
            td = AC.do(lambda e: e.activation(G[3], G[2], ACT.Exp, scale=-1.0))
            AC.wait(td)
            td = AC.do(lambda e: e.activation(G[4], G[3], ACT.Ln, bias=1.0))

            yield
            DVE.wait(td, z5)
            t1 = DVE.do(lambda e: e.scalar_tensor_tensor(G[2], G[1], 0.0, G[4], ALU.min, ALU.subtract))
            t2 = DVE.do(lambda e: e.memset(G[3], 1.0))
            DVE.wait(t1, t2)
            t1 = DVE.do(lambda e: e.tensor_tensor_scan(G[1], G[3], G[2], 0.0, ALU.mult, ALU.add))
            DVE.wait(t1)
            t1 = DVE.do(lambda e: e.tensor_tensor(GT[0:4, :], G[0], G[1], ALU.subtract))
            DVE.wait(t1)
            tM = DVE.do(lambda e: e.tensor_tensor_scan(G[4], GT[0:4, :], GT[0:4, :], 0.0, ALU.max, ALU.max))
            DVE.wait(tM)
            t3 = DVE.do(lambda e: e.tensor_tensor(G[2], G[1], G[4], ALU.add))
            yield
            AC.wait(t3)
            tem = AC.do(lambda e: e.activation(GT[32:36, :], G[2], ACT.Exp, scale=-1.0))
            small["cact"] = AC.do(lambda e: e.activation(cact, PC[:, C_C:C_C + 8], ACT.Silu))

            small["gates"] = tem, tM
            yield

        qp_tok = {}

        def conv(j):
            DVE.wait(qp_tok[j], small["pc"], z3)
            for f in range(2):
                k = 2 * j + f
                cw = lambda n, k=k: PC[:, 8 * n + k:8 * n + k + 1]
                tv = DVE.do(lambda e, k=k, cw=cw: e.tensor_scalar(QC[:, k, :], QP[:, k, 0:256], cw(0), None,
                                                                  ALU.mult))
                for n in range(1, 4):
                    DVE.wait(tv)
                    tv = DVE.do(lambda e, k=k, n=n, cw=cw: e.scalar_tensor_tensor(
                        QC[:, k, :], QP[:, k, n:n + 256], cw(n), QC[:, k, :], ALU.mult, ALU.add))
            return tv

        for j in range(4):
            s = use()
            i, W = bank()
            for f in range(2):
                tp = fm_gemm(s, 8, 256, 128 * f, W[:, 256 * f:256 * f + 256], xt)
            release(s, tp)
            AC.wait(tp)
            qp_tok[j] = AC.do(lambda e, j=j, W=W: e.copy(QP[:, 2 * j:2 * j + 2, 3:259],
                                                         W[:, :].rearrange("p (f c) -> p f c", f=2)))
            bank_free[i] = qp_tok[j]
            if j == 0:
                columns()
                gate_stages = gates()
            else:
                next(gate_stages)
            if j > 1:
                conv(j - 2)
        next(gate_stages)
        tem, tM = small["gates"]
        def uv_columns():
            ui, UW = bank()
            PE.wait(tem, tM)
            for t in range(2):
                tp = PE.do(lambda e, t=t: e.transpose(UW[:, 64 * t:64 * t + 64], GT[0:64, 128 * t:128 * t + 128],
                                                      IDN[0:64, 0:64]))
            DVE.wait(tp)
            t_uc = DVE.do(lambda e: e.tensor_copy(UC.rearrange("p (t c) -> p t c", t=2),
                                                  UW[:, 0:128].rearrange("p (t c) -> p t c", t=2)[:, :, 0:36]))
            bank_free[ui] = t_uc
            return t_uc

        UC = cols(72)
        def tm_panel(width, evac, parts):
            bs = [bank() for _ in range(2)]
            for kh in range(2):
                s = use()
                for t in range(2):
                    tp = tm_gemm(s, 4, width, 0, width, bs[t][1][:, 0:width], t, 4 * kh, kh == 0, kh == 1,
                                 parts)
                    if kh == 1:
                        bank_free[bs[t][0]] = evac(t, bs[t][1], tp)
                release(s, tp)

        def ev_v(j, dst):
            def f(t, W, tp):
                AC.wait(tp)
                return AC.do(lambda e: e.copy(dst(t), W[:, :].rearrange("p (h c) -> p h c", h=2)))
            return f

        AC.wait(z4)
        for j in range(2):
            tm_panel(512, ev_v(j, lambda t, j=j: V1[:, t, 2 * j:2 * j + 2, 0:256]), xt)
            if j == 0:
                t_uc = uv_columns()
            t_conv = conv(j + 2)
        t_v1 = AC.last()

        def ev_o(j):
            def f(t, W, tp):
                AC.wait(tp)
                return AC.do(lambda e: e.activation(OG[:, t, 512 * j:512 * j + 512], W[:, :], ACT.Sigmoid))
            return f

        def mem_half():
            for t in range(2):
                for k0 in (0, 4):
                    i, W, tp = turn_pe(lambda k, t=t: U[:, t, 128 * k:128 * k + 128], range(k0, k0 + 4), [t_mem])
                    L = (AC, DVE)[k0 // 4]
                    L.wait(tp)
                    o, w = S[:, k0:k0 + 4, 128 * t:128 * t + 128], W[:, :].rearrange("p (k c) -> p k c", k=4)
                    bank_free[i] = L.do((lambda e, o=o, w=w: e.copy(o, w)) if L is AC else
                                        (lambda e, o=o, w=w: e.tensor_copy(o, w)))

        for j in range(2):
            tm_panel(512, ev_o(j), xt)
            AC.wait(t_conv)
            t_qc = AC.do(lambda e, j=j: e.activation(QC[:, 4 * j:4 * j + 4, :], QC[:, 4 * j:4 * j + 4, :], ACT.Silu))
            if j == 0:
                mem_half()
                mem_turned, s_mem = PE.last(), [AC.last(), DVE.last()]
        t_og = AC.last()
        x_gemm = PE.last()

        DT = [AR[:, 384 * n:384 * n + 384] for n in range(2)]
        SC = [AR[:, 768 + 384 * n:1152 + 384 * n] for n in range(2)]
        sc_tok, sc_free, dt_free = {}, [None] * 2, [None] * 2

        def head_a(h):
            bi, MB = bank()
            PE.wait(tM, t_tab)
            tp = PE.do(mm(MB[:, 0:256], CSEL[:, 128 * h:128 * h + 128], G[4], True, True))
            si, SW = bank()
            PE.wait(t_qc)
            PE.run(mm(SW[:, 0:256], QC[:, 4 + h, 0:128], QC[:, h, :], True, True))
            tq = PE.do(mm(SW[:, 256:384], QC[:, 4 + h, 128:256], QC[:, h, 128:256], True, True))
            D, C = DT[h % 2], SC[h % 2]
            DVE.wait(tp, t_tab, dt_free[h % 2], t_conv)
            DVE.do(lambda e: e.scalar_tensor_tensor(D[:, 0:256], MB[:, 0:256], -1.0, MSK[:, :],
                                                    ALU.mult, ALU.add))
            td = DVE.do(lambda e: e.scalar_tensor_tensor(D[:, 256:384], MB[:, 128:256], -1.0, MSK[:, 0:128],
                                                         ALU.mult, ALU.add))
            bank_free[bi] = td
            AC.wait(td, t_uc)
            AC.do(lambda e: e.activation(D[:, 0:256], D[:, 0:256], ACT.Exp, bias=UC[:, h:h + 1]))
            te = AC.do(lambda e: e.activation(D[:, 256:384], D[:, 256:384], ACT.Exp, bias=UC[:, 36 + h:37 + h]))
            DVE.wait(te, tq, sc_free[h % 2])
            sc_tok[h] = DVE.do(lambda e: e.scalar_tensor_tensor(C, SW[:, 0:384], 128 ** -0.5, D,
                                                                ALU.mult, ALU.mult))
            dt_free[h % 2] = bank_free[si] = sc_tok[h]

        y_tok = []

        def head_c(h):
            C = SC[h % 2]
            PE.wait(sc_tok[h], t_v1, z4)
            for t in range(2):
                b = (2 * h + t) % 4
                Y = YB[b]
                PE.wait(yb_free[b])
                if t == 0:
                    tn = PE.do(mm(Y[:, 0:258], C[:, 0:128], V1[:, 0, h, :], True, True))
                else:
                    PE.run(mm(Y[:, 0:258], C[:, 128:256], V1[:, 0, h, :], True, False))
                    tn = PE.do(mm(Y[:, 0:258], C[:, 256:384], V1[:, 1, h, :], False, True))
                    sc_free[h % 2] = tn
                w = cols(4)
                em = UC[:, 36 * t + 32 + h:36 * t + 33 + h]
                DVE.wait(tn)
                t1 = DVE.do(lambda e, w=w, Y=Y, em=em: e.tensor_scalar(w[:, 0:1], Y[:, 256:257], -1.0, em,
                                                                       ALU.mult, ALU.max))
                DVE.wait(t1)
                t1 = DVE.do(lambda e, w=w, Y=Y: e.tensor_scalar(w[:, 0:1], Y[:, 256:257], w[:, 0:1], None,
                                                                ALU.max))
                DVE.wait(t1)
                t1 = DVE.do(lambda e, w=w: e.reciprocal(w[:, 1:2], w[:, 0:1]))
                AC.wait(t1)
                t2 = AC.do(lambda e, w=w, Y=Y, t=t: e.activation(JK, Y[:, 0:256], ACT.Square,
                                                                 scale=w[:, 1:2], accum_out=w[:, 2:3]))
                PO.wait(t2)
                t3 = PO.do(lambda e, w=w: e.tensor_scalar(w[:, 2:3], w[:, 2:3], 1 / 256, LN_EPS,
                                                          ALU.mult, ALU.add))
                t3 = rsqrt(w[:, 3:4], w[:, 2:3], t3)
                PO.wait(t3)
                t3 = PO.do(lambda e, w=w: e.tensor_tensor(w[:, 3:4], w[:, 3:4], w[:, 1:2], ALU.mult))
                DVE.wait(t3, t_og, mem_turned)
                yb_free[b] = t4 = DVE.do(lambda e, w=w, Y=Y, t=t: e.scalar_tensor_tensor(
                    U[:, t, 256 * h:256 * h + 256], Y[:, 0:256], w[:, 3:4],
                    OG[:, t, 256 * h:256 * h + 256], ALU.mult, ALU.mult))
                y_tok.append(t4)

        JK = AR[:, 1536:1792]
        KT = KV[:, 0:2048].rearrange("p (k c) -> p k c", k=8)
        VM = KV[:, 2048:4096].rearrange("p (t c) -> p t c", t=2)

        def k_chunk(j):
            s = use()
            i, W = bank()
            for f in range(2):
                tp = fm_gemm(s, 8, 256, 128 * f, W[:, 256 * f:256 * f + 256], mt)
            release(s, tp)
            AC.wait(tp)
            bank_free[i] = AC.do(lambda e: e.copy(KT[:, 2 * j:2 * j + 2, :],
                                                  W[:, :].rearrange("p (f c) -> p f c", f=2)))

        def ev_m(j):
            def f(t, W, tp):
                AC.wait(tp)
                return AC.do(lambda e: e.copy(VM[:, t, 512 * j:512 * j + 512], W[:, :]))
            return f

        head_a(0)
        mt = [hilo(None, 2 * q, 2 * q + 2, XH[:, 2 * q:2 * q + 2, :], XL[:, 2 * q:2 * q + 2, :],
                   S[:, 2 * q:2 * q + 2, :], x_gemm, s_mem) for q in range(4)]
        head_a(1)
        k_chunk(0)
        head_c(0)
        k_chunk(1)
        head_a(2)
        head_c(1)
        k_chunk(2)
        head_a(3)
        head_c(2)
        k_chunk(3)
        head_c(3)
        for j in range(2):
            tm_panel(512, ev_m(j), mt)
        t_kv = AC.last()
        xfree[:] = now()
        yt = []
        for t in range(2):
            yt += turn(t, lambda k, t=t: U[:, t, 128 * k:128 * k + 128], 8, y_tok[t::2],
                       g=lambda k: PC[:, C_NG + k:C_NG + k + 1])
        for js in ((0,), (1,), (2, 3)):
            ys = row_chunks(js, 4, [(yt, XH, XL, 2 * j) for j in js])
        x_ready = [[t_x[0]], [t_x[1]]]
        xfree[:] = now()
        xt = layer_norm(ys, 0, 0)

        TMP = AR[:, 6144:8800]
        xa_free = {}

        def xattn(xt, first):
            QT = [TMP[:, 512 * n:512 * n + 512] for n in range(2)]
            PB = [TMP[:, 1024 + 512 * n:1536 + 512 * n] for n in range(2)]
            PT = TMP[:, 2048:2560]
            tok = {}
            xo = {}

            def p0(h):
                s = use()
                i, W = bank()
                for f in range(2):
                    tp = fm_gemm(s, 8, 256, 128 * f, W[:, 256 * f:256 * f + 256], xt)
                release(s, tp)
                AC.wait(tp, xa_free.get(("q", h % 2)), *first)
                bank_free[i] = tok["q", h] = AC.do(lambda e: e.copy(QT[h % 2], W[:, :]))
                if h == 3:
                    tok["wq"] = tp

            def p1(h):
                i, W = bank()
                PE.wait(tok["q", h], t_kv)
                Q = QT[h % 2].rearrange("p (f c) -> p f c", f=2)
                for t in range(2):
                    for f in range(2):
                        m = mm(W[:, 256 * t:256 * t + 256], Q[:, f, 128 * t:128 * t + 128],
                               KT[:, 2 * h + f, :], f == 0, f == 1)
                        tp = PE.do(m) if t * f else PE.run(m)
                xa_free["q", h % 2] = tp
                w = cols(6)
                W3 = W[:, :].rearrange("p (t c) -> p t c", t=2)
                P = PB[h % 2].rearrange("p (t c) -> p t c", t=2)
                DVE.wait(tp)
                t1 = DVE.do(lambda e: e.tensor_reduce(w[:, 0:2], W3, AX, ALU.max))
                DVE.wait(t1)
                t1 = DVE.do(lambda e: e.tensor_scalar(w[:, 0:2], w[:, 0:2], -1 / 16, None, ALU.mult))
                AC.wait(t1, xa_free.get(("p", h % 2)), *first)
                for t in range(2):
                    te = AC.do(lambda e, t=t: e.activation(P[:, t, :], W3[:, t, :], ACT.Exp, bias=w[:, t:t + 1],
                                                           scale=1 / 16, accum_out=w[:, 2 + t:3 + t]))
                bank_free[i] = te
                DVE.wait(te)
                t1 = DVE.do(lambda e: e.reciprocal(w[:, 4:6], w[:, 2:4]))
                DVE.wait(t1)
                for t in range(2):
                    t2 = DVE.do(lambda e, t=t: e.tensor_scalar(P[:, t, :], P[:, t, :], w[:, 4 + t:5 + t], None,
                                                               ALU.mult))
                tok["p", h] = t2

            def p2(h):
                i, W = bank()
                P = PB[h % 2].rearrange("p (t c) -> p t c", t=2)
                PE.wait(tok["p", h])
                for m in range(2):
                    for t in range(2):
                        tp = PE.do(lambda e, m=m, t=t: e.transpose(
                            W[:, 256 * m + 128 * t:256 * m + 128 * t + 128], P[:, t, 128 * m:128 * m + 128],
                            IDN[:, :]))
                xa_free["p", h % 2] = tp
                AC.wait(tp, xa_free.get("pt"))
                bank_free[i] = tok["pt", h] = AC.do(lambda e: e.copy(PT, W[:, :]))

            def p3(h):
                i, W = bank()
                PE.wait(tok["pt", h])
                for d in range(2):
                    for m in range(2):
                        f = mm(W[:, 256 * d:256 * d + 256], VM[:, m, 256 * h + 128 * d:256 * h + 128 * d + 128],
                               PT[:, 256 * m:256 * m + 256], m == 0, m == 1)
                        tp = PE.do(f) if d * m else PE.run(f)
                xa_free["pt"] = tp
                xo[h] = hilo_bank(None, 2 * h, 2 * h + 2, XH[:, 2 * h:2 * h + 2, :], XL[:, 2 * h:2 * h + 2, :], i,
                                  W[:, :].rearrange("p (f c) -> p f c", f=2), tp, tok["wq"])

            def r(*hs):
                return row_chunks(hs, 4, [([xo[h]], XH, XL, 2 * h) for h in hs])

            for f, h in ((p0, 0), (p0, 1), (p1, 0), (p0, 2), (p1, 1), (p2, 0), (p0, 3), (p3, 0), (p1, 2), (p2, 1),
                         (p1, 3), (p3, 1), (p2, 2), (r, 0), (p3, 2), (p2, 3), (r, 1), (p3, 3)):
                f(h)
            ys = r(2, 3)
            xfree[:] = now()
            return ys

        f_free = [[None], [None]]

        def mlp(i, xt, first, R0, at14=None):
            RT = [R0[:, 512 * n:512 * n + 512] for n in range(2)]
            RS = R0[:, 1024:1536]
            fo = {}
            b2i, tb2 = bvec(I["mlp_b2"][i])
            for t in range(2):
                PO.wait(*x_ready[t])
                tx = PO.do(lambda e, t=t: e.tensor_scalar(X[:, t, :], X[:, t, :], ALPHA, None, ALU.mult))
                PO.wait(tx, tb2)
                tx = PO.do(lambda e, t=t: e.tensor_tensor(X[:, t, :], X[:, t, :], BV[b2i][:, :], ALU.add))
                x_ready[t] = [tx]
            bv_free[b2i] = tx
            for j in range(17):
                if j < 16:
                    s = use()
                    bi, W = bank()
                    for f in range(2):
                        tp = fm_gemm(s, 8, 256, 128 * f, W[:, 256 * f:256 * f + 256], xt)
                    release(s, tp)
                    R = RT[j % 2]
                    AC.wait(tp, *first)
                    AC.wait(*f_free[j % 2])
                    for f in range(2):
                        c = C_B1 + 32 * i + 2 * j + f
                        tr = AC.do(lambda e, f=f, c=c, W=W, R=R: e.activation(
                            R[:, 256 * f:256 * f + 256], W[:, 256 * f:256 * f + 256], ACT.Relu,
                            bias=PC[:, c:c + 1]))
                    bank_free[bi] = tr
                    AC.wait(tr)
                    H, L = FH[j % 2][:, :], FL[j % 2][:, :]
                    th = AC.do(lambda e, R=R, H=H: e.activation(H, R, ACT.Square))
                    DVE.wait(tr, fo[j - 1].lo if j else None, *f_free[j % 2])
                    tr = DVE.do(lambda e, R=R: e.tensor_tensor(RS, R, R, ALU.mult))
                    DVE.wait(th, tr)
                    tl = DVE.do(lambda e, H=H, L=L: e.tensor_tensor(L, RS, H.bitcast(F32), ALU.subtract))
                    fo[j] = Part(None, 0, 2, th, tl)
                v = lambda b: b.rearrange("p (f c) -> p f c", f=2)
                js = () if j in (0, 15) else (14, 15) if j == 16 else (j - 1,)
                if js:
                    ys = row_chunks(js, 16, [([fo[m]], v(FH[m % 2][:, :]), v(FL[m % 2][:, :]), 0) for m in js])
                    for m in js:
                        f_free[m % 2] = [PE.last(), DVE.last()]
                if j == 14 and at14:
                    at14()
            xfree[:] = now()
            return ys

        cut = now()
        ys = xattn(xt, cut)
        xt = layer_norm(ys, 0, 1)
        cut = now()
        small[("ada", 0)] = small[("ada", 1)] = small[("ada", 2)] = cut
        WM = TMP[:, 1536:2624]
        PO.wait(*cut)
        t_wm = load(PO, "wm", (WM, I["c_win"]))
        ys = mlp(0, xt, cut, TMP)
        layer_norm(ys, 0, 2, b2=True, turned=False)

        sc_i, t_sc = bvec(I["pool_scale"][0])
        po, xfree[:] = [], now()
        wm = lambda g, a, c: WM[:, 272 * g + a:272 * g + c]
        ws = [bank() for _ in range(4)]
        PE.wait(t_wm, *x_ready[0])
        for k in range(8):
            o = ws[k // 2][1][:, 256 * (k % 2):256 * (k % 2) + 256]
            tp = PE.do(mm(o[:, 0:144], X[:, 0, 128 * k:128 * k + 128], wm(k // 2, 0, 144), k % 2 == 0, False))
        PE.wait(*x_ready[1])
        for k in range(8):
            i, W = ws[k // 2]
            o = W[:, 256 * (k % 2):256 * (k % 2) + 256]
            PE.run(mm(o[:, 128:144], X[:, 1, 128 * k:128 * k + 128], wm(k // 2, 144, 160), False, False))
            tp = PE.do(mm(o[:, 144:256], X[:, 1, 128 * k:128 * k + 128], wm(k // 2, 160, 272), False, k % 2 == 1))
            if k % 2:
                po.append(hilo_bank(None, k - 1, k + 1, XH[:, k - 1:k + 1, :], XL[:, k - 1:k + 1, :], i,
                                    W[:, :].rearrange("p (f c) -> p f c", f=2), tp, *xfree))
        s = use(later=True)
        ys = []
        PE.wait(*yb_free)
        for t in range(2):
            for g in range(4):
                tp = tm_gemm(s, 2, 256, 512 * g, 512 * g + 256, YB[2 * t + g // 2][:, 256 * (g % 2):256 * (g % 2) + 256],
                             t, 2 * g, True, True, po)
                if g % 2:
                    ys.append(tp)
        release(s, tp)
        xfree[:] = now()
        xt = layer_norm(ys, 1, 0, yscale=(sc_i, t_sc))
        cut = now()
        ys = xattn(xt, cut)
        xt = layer_norm(ys, 1, 1)
        cut = now()

        MC = cols(48)
        modt = {}

        ONE = TMP[:, 2048:2176]

        def modulation():
            i, W = bank()
            DVE.wait(*cut)
            ms_one = DVE.do(lambda e: e.memset(ONE, 1.0))
            PE.wait(small["ada", 0], small["ada", 1], small["ada", 2], ms_one)
            for n in range(48):
                tp = mm(W[:, 2 * n:2 * n + 2], MOD[:, 128 * n:128 * n + 128], ONE[:, 0:2], True, True)
                tp = PE.do(tp) if n == 47 else PE.run(tp)
            DVE.wait(tp)
            t1 = DVE.do(lambda e: e.tensor_tensor(MC, W[:, 0:96].rearrange("p (n a) -> p n a", a=2)[:, :, 0],
                                                  PC[:, C_BA:C_BA + 48], ALU.add))
            bank_free[i] = t1
            DVE.wait(t1)
            for a, g in ((8, C_GM), (32, C_GF)):
                t1 = DVE.do(lambda e, a=a, g=g: e.scalar_tensor_tensor(
                    MC[:, a:a + 8], MC[:, a:a + 8], 1.0, PC[:, g:g + 8], ALU.add, ALU.mult))
            modt["mc"] = t1

        def gate_rows(n, dst, first):
            src = 2048 if n == 0 else 5120
            gi, tg = bvec(I["b_ada_2"][0, src:src + 1024])
            for h in range(2):
                i, W = bank()
                tp = PE.do(mm(W[:, :], ONE, MOD[:, src + 512 * h:src + 512 * h + 512], True, True))
                DVE.wait(tp, tg, *first)
                bank_free[i] = t = DVE.do(lambda e, h=h, W=W: e.tensor_tensor(
                    dst[:, 512 * h:512 * h + 512], W[:, :], BV[gi][:, 512 * h:512 * h + 512], ALU.add))
            bv_free[gi] = t
            return t

        GB = AR[:, 6144:8192].rearrange("p (n c) -> p n c", n=2)
        t_gb = []

        def late():
            modulation()
            t_gb.extend(gate_rows(n, GB[:, n, :], cut) for n in range(2))

        ys = mlp(1, xt, cut, KV, late)
        layer_norm(ys, 1, 2, b2=True, turned=False)

        Uf = U[:, :, :].rearrange("p t c -> p (t c)")
        Sf = S[:, :, :].rearrange("p k c -> p (k c)")
        DQ = AR[:, 0:1024].rearrange("p (h c) -> p h c", h=4)
        KD = AR[:, 1024:3072].rearrange("p (h s c) -> p h s c", h=4, s=2)
        DV = AR[:, 3072:4096].rearrange("p (t c) -> p t c", t=2)
        QL = AR[:, 4096:4864].rearrange("p (t c) -> p t c", t=2)
        KL = AR[:, 4864:5504].rearrange("p (t c) -> p t c", t=2)
        PTS = [Uf[:, 1536:1920], AR[:, 5504:5888]]
        OTS = [w.rearrange("p (t c) -> p t c", t=2) for w in (AR[:, 5888:6144], BV[1][:, 384:640])]
        E2 = [[Uf[:, 768 * n + 384 * m:768 * n + 384 * m + 384] for m in range(2)] for n in range(2)]
        CS = AR[:, 8192:8704].rearrange("p (n c) -> p n c", n=2)
        QN = KV[:, 0:1024].rearrange("p (h c) -> p h c", h=4)
        QPE = KV[:, 1024:1536].rearrange("p (j c) -> p j c", j=2)
        KN = KV[:, 1536:2560].rearrange("p (h c) -> p h c", h=4)
        KPE = KV[:, 2560:3072].rearrange("p (s c) -> p s c", s=2)
        V2 = Sf[:, 384:1408].rearrange("p (t c) -> p t c", t=2)
        QT2 = [Sf[:, 1536:1792], Sf[:, 1792:2048]]
        LQH, LQL = (w[:, 0:768].rearrange("p (k c) -> p k c", k=3) for w in (FHT, FLT))
        LKH, LKL = (w[:, 768:1280].rearrange("p (k c) -> p k c", k=2) for w in (FHT, FLT))
        RT = Sf[:, 0:256].rearrange("p (t c) -> p t c", t=2)
        RA = Sf[:, 256:384].rearrange("p (n t c) -> p n t c", n=2, t=2)
        TB = [BV[0][:, 256 * h:256 * h + 256] for h in range(4)] + [BV[1][:, 0:256]]
        TR = BV[1][:, 256:384].rearrange("p (n t c) -> p n t c", n=2, t=2)

        JX = [AR[:, 0:1024], AR[:, 1024:2048]]

        def rms_stats(t, ready):
            AC.wait(ready)
            t1 = AC.do(lambda e: e.activation(JX[t], X[:, t, :], ACT.Square, accum_out=BN[:, t, 12:13]))
            PO.wait(t1)
            t1 = PO.do(lambda e: e.tensor_scalar(BN[:, t, 13:14], BN[:, t, 12:13], 1 / 1024, EPS, ALU.mult, ALU.add))
            return rsqrt(BN[:, t, 14:15], BN[:, t, 13:14], t1)

        def rms_turn(a, b, ready):
            tr = {}

            def z(t):
                DVE.wait(tr[t])
                return DVE.do(lambda e: e.tensor_scalar(U[:, t, :], X[:, t, :], BN[:, t, 14:15], None, ALU.mult))

            def stage(t):
                tr[t] = rms_stats(t, ready(t))

            return turn_norm(z, [lambda: stage(0), lambda: stage(1)], lambda k: MC[:, a + k:a + k + 1],
                             lambda k: MC[:, b + k:b + k + 1])

        xfree[:] = now()
        DVE.wait(modt["mc"])
        AC.wait(modt["mc"])
        xt = rms_turn(8, 0, lambda t: x_ready[t])
        xfree[:] = cut = now()
        PO.wait(*cut)
        PO.do(lambda e: e.memset(KD[64:128, :, 0, :], 0.0))
        PO.do(lambda e: e.memset(KD[0:64, :, 1, :], 0.0))
        PO.do(lambda e: e.memset(KPE[64:128, 0, :], 0.0))
        t_zero = PO.do(lambda e: e.memset(KPE[0:64, 1, :], 0.0))
        PO.wait(t_zero)
        SP.wait(*cut)
        t_tb = load(SP, "tb2", (BV[0][:, :], I["c_alibi"]), (BV[1][:, 0:256], I["c_causal"]),
                    (BV[1][:, 256:384], I["c_rope_t"]), (AR[:, 8192:8704], I["c_rope_f"]))
        LB = BV[1][:, 640:896].rearrange("p (n c) -> p n c", n=4)
        t_lb = load(SP, "lam", *[(LB[:, n, :], I[f"lambda_{x}_2"][0].partition_broadcast(128))
                                 for n, x in enumerate(("q1", "q2", "k1", "k2"))])
        AC.wait(*cut)
        DVE.wait(*cut)
        dtok = {}
        lam = cols(4)

        def minus_lambda():
            DVE.wait(t_lb)
            t1 = DVE.do(lambda e: e.tensor_tensor(LB[:, 0:2, :], LB[:, 0:2, :], LB[:, 2:4, :], ALU.mult))
            DVE.wait(t1)
            t1 = DVE.do(lambda e: e.tensor_reduce(lam[:, 0:2], LB[:, 0:2, :], AX, ALU.add))
            AC.wait(t1)
            t1 = AC.do(lambda e: e.activation(lam[:, 0:2], lam[:, 0:2], ACT.Exp))
            DVE.wait(t1)
            dtok["lam"] = DVE.do(lambda e: e.scalar_tensor_tensor(lam[:, 2:3], lam[:, 1:2], LAMBDA_INIT, lam[:, 0:1],
                                                            ALU.subtract, ALU.subtract))


        def dq_chunk(j):
            s = use()
            i, W = bank()
            for f in range(2):
                tp = fm_gemm(s, 8, 256, 128 * f, W[:, 256 * f:256 * f + 256], xt)
            release(s, tp)
            dtok["x"] = tp
            AC.wait(tp)
            W3 = W[:, :].rearrange("p (f c) -> p f c", f=2)
            if j < 2:
                te = AC.do(lambda e: e.copy(DQ[:, 2 * j:2 * j + 2, :], W3))
            else:
                AC.do(lambda e: e.copy(KD[0:64, 2 * j - 4:2 * j - 2, 0, :], W3[0:64]))
                te = AC.do(lambda e: e.copy(KD[64:128, 2 * j - 4:2 * j - 2, 1, :], W3[64:128]))
            bank_free[i] = te
            dtok["k", j // 2, j % 2] = te

        def ev_dv(t, W, tp):
            AC.wait(tp)
            dtok["v"] = AC.do(lambda e: e.copy(DV[:, t, :], W[:, :]))
            return dtok["v"]

        def latent_scale(t, dst, n, W, tp, w):
            AC.wait(tp)
            AC.wait(AC.do(lambda e: e.copy(dst, W[:, 0:dst.shape[1]])))
            te = AC.do(lambda e: e.activation(V2[:, t, 0:n], W[:, 0:n], ACT.Square, accum_out=w[:, 0:1]))
            PO.wait(te)
            t1 = PO.do(lambda e: e.tensor_scalar(w[:, 0:1], w[:, 0:1], 1 / n, EPS, ALU.mult, ALU.add))
            t1 = rsqrt(w[:, 1:2], w[:, 0:1], t1)
            DVE.wait(te, t1)
            return te, DVE.do(lambda e: e.tensor_scalar(dst[:, 0:n], dst[:, 0:n], w[:, 1:2], None, ALU.mult))

        def ev_ql(t, W, tp):
            te, dtok["ql", t] = latent_scale(t, QL[:, t, :], 384, W, tp, cols(2))
            return te

        def ev_kl(t, W, tp):
            te, dtok["kl", t] = latent_scale(t, KL[:, t, :], 256, W, tp, cols(2))
            return te

        efree, pfree = [None, None], [None, None]

        def softmax_rows(W, E, tb, scale, w, c):
            DVE.do(lambda e: e.scalar_tensor_tensor(E[:, 0:128], W[:, 0:128], scale, tb[:, 128:256],
                                                    ALU.mult, ALU.add))
            t1 = DVE.do(lambda e: e.scalar_tensor_tensor(E[:, 128:384], W[:, 128:384], scale, tb,
                                                         ALU.mult, ALU.add))
            tw = t1
            DVE.wait(t1)
            DVE.do(lambda e: e.tensor_reduce(w[:, c:c + 1], E[:, 0:128], AX, ALU.max, negate=True))
            t1 = DVE.do(lambda e: e.tensor_reduce(w[:, c + 1:c + 2], E[:, 128:384], AX, ALU.max, negate=True))
            AC.wait(t1)
            AC.do(lambda e: e.activation(E[:, 0:128], E[:, 0:128], ACT.Exp, bias=w[:, c:c + 1],
                                         accum_out=w[:, c + 2:c + 3]))
            te = AC.do(lambda e: e.activation(E[:, 128:384], E[:, 128:384], ACT.Exp, bias=w[:, c + 1:c + 2],
                                              accum_out=w[:, c + 3:c + 4]))
            return tw, te

        def d1(h):
            E = E2[h % 2]
            w = cols(12)
            tps, bs = [], []
            for m in range(2):
                i, W = bank()
                bs.append((i, W))
                PE.wait(dtok["k", 0, h // 2], dtok["k", 1, h // 2], t_zero)
                PE.run(mm(W[:, 0:128], DQ[:, h, 0:128], KD[:, h, m, 0:128], True, True))
                tps.append(PE.do(mm(W[:, 128:384], DQ[:, h, 128:256], KD[:, h, m, :], True, True)))
            for m in range(2):
                DVE.wait(tps[m], t_tb, dtok["lam"], efree[h % 2])
                bank_free[bs[m][0]], te = softmax_rows(bs[m][1], E[m], TB[h], 64 ** -0.5, w, 4 * m)
            DVE.wait(te)
            w2 = w[:, 0:8].rearrange("p (m c) -> p m c", m=2)[:, :, 2:4]
            r = w[:, 8:12].rearrange("p (m c) -> p m c", m=2)
            t1 = DVE.do(lambda e: e.reciprocal(r, w2))
            DVE.wait(t1)
            t1 = DVE.do(lambda e: e.tensor_scalar(w[:, 10:12], w[:, 10:12], lam[:, 2:3], None, ALU.mult))
            for c, a in ((0, slice(0, 128)), (1, slice(128, 384))):
                t2 = DVE.do(lambda e, c=c, a=a: e.tensor_scalar(E[0][:, a], E[0][:, a], w[:, 8 + c:9 + c], None,
                                                                ALU.mult))
                DVE.wait(t1, t2)
                t3 = DVE.do(lambda e, c=c, a=a: e.scalar_tensor_tensor(E[0][:, a], E[1][:, a], w[:, 10 + c:11 + c],
                                                                       E[0][:, a], ALU.mult, ALU.add))
            dtok["e", h] = t3
            dtok["dq"] = tps[1]

        def turn_p(h, key, E, n):
            i, W = bank()
            PE.wait(dtok[key, h])
            for b in range(3):
                tp = PE.do(lambda e, b=b: e.transpose(W[:, 128 * b:128 * b + 128], E[:, 128 * b:128 * b + 128],
                                                      IDN[:, :]))
            efree[h % 2] = tp
            AC.wait(tp, pfree[h % 2])
            bank_free[i] = dtok["pt", n] = AC.do(lambda e: e.copy(PTS[h % 2], W[:, 0:384]))

        def d2(h):
            turn_p(h, "e", E2[h % 2][0], h)

        ot_free = [None, None]

        def d3(h):
            i, W = bank()
            P = PTS[h % 2]
            PE.wait(dtok["pt", h], dtok["v"])
            hs = slice(128 * h, 128 * h + 128)
            PE.run(mm(W[:, 0:128], P[:, 0:128], DV[:, 0, hs], True, True))
            PE.run(mm(W[:, 128:256], P[:, 128:256], DV[:, 0, hs], True, False))
            tp = PE.do(mm(W[:, 128:256], P[:, 256:384], DV[:, 1, hs], False, True))
            pfree[h % 2] = tp
            w, OT = cols(4), OTS[h % 2]
            AC.wait(tp, ot_free[h % 2], t_tb)
            for t in range(2):
                te = AC.do(lambda e, t=t: e.activation(OT[:, t, :], W[:, 128 * t:128 * t + 128], ACT.Square,
                                                       accum_out=w[:, t:t + 1]))
            PO.wait(te)
            t1 = PO.do(lambda e: e.tensor_scalar(w[:, 0:2], w[:, 0:2], 1 / 128, EPS, ALU.mult, ALU.add))
            t1 = rsqrt(w[:, 2:4], w[:, 0:2], t1)
            DVE.wait(te, t1)
            for t in range(2):
                t2 = DVE.do(lambda e, t=t: e.tensor_scalar(OT[:, t, :], W[:, 128 * t:128 * t + 128],
                                                           w[:, 2 + t:3 + t], 1.0 - LAMBDA_INIT,
                                                           ALU.mult, ALU.mult))
            bank_free[i] = dtok["ot", h] = t2

        def d4(h):
            i, W = bank()
            OT = OTS[h % 2]
            PE.wait(dtok["ot", h])
            for t in range(2):
                tp = PE.do(lambda e, t=t: e.transpose(W[:, 128 * t:128 * t + 128], OT[:, t, :], IDN[:, :]))
            ot_free[h % 2] = tp
            DVE.wait(tp, dtok["dq"])
            bank_free[i] = dtok["om", h] = DVE.do(lambda e: e.tensor_scalar(
                DQ[:, h, :], W[:, 0:256], PC[:, C_GD:C_GD + 1], None, ALU.mult))

        def panel(width, evac, ys):
            def half(kh):
                s = use()
                for t in range(2):
                    Y = YB[ys[t]]
                    if kh == 0:
                        PE.wait(yb_free[ys[t]])
                    tp = tm_gemm(s, 4, width, 0, width, Y[:, 0:width], t, 4 * kh, kh == 0, kh == 1, xt)
                    if kh == 1:
                        yb_free[ys[t]] = evac(t, Y, tp)
                release(s, tp)
                dtok["x"] = tp
            return half

        lq, lk = [], []

        def latents(_):
            for t in range(2):
                lk.extend(turn(t, lambda k, t=t: KL[:, t, 128 * k:128 * k + 128], 2, [dtok["kl", t]],
                               LKH, LKL, lambda k: PC[:, C_GK + k:C_GK + k + 1]))
            for t in range(2):
                lq.extend(turn(t, lambda k, t=t: QL[:, t, 128 * k:128 * k + 128], 3, [dtok["ql", t]],
                               LQH, LQL, lambda k: PC[:, C_GQ + k:C_GQ + k + 1]))

        def rotary_keys(_):
            cs, sn = TR[:, 0], TR[:, 1]
            kr = KL[:, :, 256:320]
            DVE.wait(dtok["kl", 0], dtok["kl", 1], t_tb, *[[p.hi, p.lo] for p in xt])
            for o, (a, b), op in ((0, (cs, sn), ALU.subtract), (32, (sn, cs), ALU.add)):
                t1 = DVE.do(lambda e, a=a: e.tensor_tensor(RA[:, 0], kr[:, :, 0:32], a, ALU.mult))
                t2 = DVE.do(lambda e, b=b: e.tensor_tensor(RA[:, 1], kr[:, :, 32:64], b, ALU.mult))
                DVE.wait(t1, t2)
                for d in (0, 64):
                    t1 = DVE.do(lambda e, o=o, d=d, op=op: e.tensor_tensor(RT[:, :, o + d:o + d + 32], RA[:, 0],
                                                                           RA[:, 1], op))
                DVE.wait(t1)
            i, W = bank()
            PE.wait(t1)
            for t in range(2):
                tp = PE.do(lambda e, t=t, W=W: e.transpose(W[:, 128 * t:128 * t + 128], RT[:, t, :], IDN[:, :]))
            AC.wait(tp, t_zero)
            AC.do(lambda e, W=W: e.copy(KPE[0:64, 0, :], W[0:64, 0:256]))
            bank_free[i] = dtok["kpe"] = AC.do(lambda e, W=W: e.copy(KPE[64:128, 1, :], W[64:128, 0:256]))

        def q_up(j):
            s = use()
            for g in range(2):
                i, W = bank()
                for f in range(2):
                    tp = fm_gemm(s, 3, 512, 256 * g + 128 * f, W[:, 256 * f:256 * f + 256], lq, LQH, LQL)
                if g == 0:
                    AC.wait(tp)
                    te = AC.do(lambda e, W=W: e.copy(QN[:, 2 * j:2 * j + 2, :],
                                                     W[:, :].rearrange("p (f c) -> p f c", f=2)))
                else:
                    DVE.wait(tp, t_tb, dtok.get("qpe"))
                    DVE.do(lambda e, W=W: e.tensor_tensor(QT2[0], W[:, 0:256], CS[:, 0, :], ALU.mult))
                    te = DVE.do(lambda e, W=W: e.tensor_tensor(QT2[1], W[:, 256:512], CS[:, 1, :], ALU.mult))
                    DVE.wait(te)
                    dtok["qpe"] = DVE.do(lambda e: e.tensor_tensor(QPE[:, j, :], QT2[0], QT2[1], ALU.add))
                bank_free[i] = te
            release(s, tp)
            dtok["q", j] = [AC.last(), dtok["qpe"]]

        def kv_up(_):
            s = use()
            for g in range(2):
                i, W = bank()
                for f in range(2):
                    tp = fm_gemm(s, 2, 1024, 256 * (2 * g + f), W[:, 256 * f:256 * f + 256], lk, LKH, LKL)
                AC.wait(tp)
                bank_free[i] = AC.do(lambda e, g=g, W=W: e.copy(KN[:, 2 * g:2 * g + 2, :],
                                                                W[:, :].rearrange("p (f c) -> p f c", f=2)))
            for t in range(2):
                i, W = bank()
                tp = tm_gemm(s, 2, 1024, 0, 0, W[:, :].rearrange("p (h c) -> p h c", h=4), t, 0, True, True, lk,
                             LKH, LKL, lambda w, k: w[:, 0:2048].rearrange(
                                 "p (k h c) -> p k h c", k=2, h=4)[:, k, :, 128:256])
                AC.wait(tp, dtok["ql", t])
                bank_free[i] = AC.do(lambda e, t=t, W=W: e.copy(V2[:, t, :], W[:, :]))
            release(s, tp)
            dtok["kv"] = AC.last()

        def m1(h):
            i, W = bank()
            E = E2[h % 2][0]
            w = cols(6)
            PE.wait(*dtok["q", h // 2], dtok["kv"], dtok["kpe"])
            for o, tq, n in ((slice(0, 128), slice(0, 128), 128), (slice(128, 384), slice(128, 256), 256)):
                PE.run(mm(W[:, o], QN[:, h, tq], KN[:, h, 0:n], True, False))
                tp = PE.do(mm(W[:, o], QPE[:, h // 2, tq], KPE[:, h % 2, 0:n], False, True))
            DVE.wait(tp, efree[h % 2])
            bank_free[i], te = softmax_rows(W, E, TB[4], 192 ** -0.5, w, 0)
            DVE.wait(te)
            t1 = DVE.do(lambda e: e.reciprocal(w[:, 4:6], w[:, 2:4]))
            DVE.wait(t1)
            DVE.do(lambda e: e.tensor_scalar(E[:, 0:128], E[:, 0:128], w[:, 4:5], None, ALU.mult))
            dtok["m", h] = DVE.do(lambda e: e.tensor_scalar(E[:, 128:384], E[:, 128:384], w[:, 5:6], None, ALU.mult))

        def m2(h):
            turn_p(h, "m", E2[h % 2][0], 4 + h)

        xo = {}

        def m3(h):
            i, W = bank()
            P = PTS[h % 2]
            PE.wait(dtok["pt", 4 + h])
            hs = slice(128 * h, 128 * h + 128)
            PE.run(mm(W[:, 0:128], V2[:, 0, hs], P[:, 0:128], True, True))
            PE.run(mm(W[:, 128:256], V2[:, 0, hs], P[:, 128:256], True, False))
            tp = PE.do(mm(W[:, 128:256], V2[:, 1, hs], P[:, 256:384], False, True))
            pfree[h % 2] = tp
            xo[2 + h // 2] = xo.get(2 + h // 2, []) + [hilo_bank(None, 4 + h, 5 + h, XH[:, 4 + h, :], XL[:, 4 + h, :],
                                                                 i, W[:, 0:256], tp, dtok["x"])]

        def xo_diff(j):
            xo[j] = [hilo(None, 2 * j, 2 * j + 2, XH[:, 2 * j:2 * j + 2, :], XL[:, 2 * j:2 * j + 2, :],
                          DQ[:, 2 * j:2 * j + 2, :], dtok["x"], dtok["om", 2 * j], dtok["om", 2 * j + 1])]

        def r2(*js):
            return row_chunks(js, 4, [(xo[b], XH, XL, 2 * b) for b in ((0, 2, 1, 3)[j] for j in js)])

        dv = panel(512, ev_dv, (0, 1))
        for width, ev, ys in ((320, ev_kl, (0, 1)), (384, ev_ql, (2, 3))):
            p = panel(width, ev, ys)
            p(0)
            p(1)
        dq_chunk(0)
        minus_lambda()
        for f, h in ((dq_chunk, 2), (latents, 0), (d1, 0), (dq_chunk, 1), (rotary_keys, 0), (d1, 1), (d2, 0), (kv_up, 0), (dv, 0), (d2, 1), (q_up, 0),
                     (dv, 1), (d3, 0), (m1, 0), (d3, 1), (d4, 0), (dq_chunk, 3), (m1, 1), (m2, 0), (d4, 1),
                     (xo_diff, 0), (q_up, 1), (d1, 2), (m2, 1), (m3, 0), (r2, 0), (d1, 3), (m3, 1), (d2, 2), (r2, 1),
                     (m1, 2), (d2, 3), (d3, 2), (m1, 3), (m2, 2), (d4, 2), (d3, 3), (m2, 3), (m3, 2), (d4, 3),
                     (m3, 3), (xo_diff, 1)):
            f(h)
        ys = r2(2, 3)

        def gated(ys, n, t):
            DVE.wait(*x_ready[t], *t_gb)
            for h in range(2):
                cs = slice(512 * h, 512 * h + 512)
                DVE.wait(ys[2 * t + h])
                yb_free[2 * t + h] = tu = DVE.do(lambda e, h=h, cs=cs: e.tensor_tensor(
                    U[:, t, cs], YB[2 * t + h][:, :], GB[:, n, cs], ALU.mult))
                DVE.wait(tu)
                tu = DVE.do(lambda e, cs=cs: e.tensor_tensor(X[:, t, cs], X[:, t, cs], U[:, t, cs], ALU.add))
            x_ready[t] = [tu]
            return tu

        xfree[:] = now()
        DVE.wait(dtok["x"])
        xt = rms_turn(32, 24, lambda t: gated(ys, 0, t))
        cut = now()
        SG = [AR[:, 1024 * n:1024 * n + 512] for n in range(2)]
        SU = [AR[:, 1024 * n + 512:1024 * n + 1024] for n in range(2)]
        fo = {}
        bv_free[:] = [cut, cut]
        g_i, t_gf = bvec(I["g_final_2"])
        for j in range(12):
            if j < 11:
                n = j % 2
                for m in range(2):
                    s = use()
                    i, W = bank()
                    for f in range(2):
                        tp = fm_gemm(s, 8, 256, 128 * f, W[:, 256 * f:256 * f + 256], xt)
                    release(s, tp)
                    if m == 0:
                        AC.wait(tp, *cut, *f_free[n])
                        bank_free[i] = tg = AC.do(lambda e, W=W, n=n: e.activation(SG[n], W[:, :], ACT.Silu))
                    else:
                        DVE.wait(tp, tg, *f_free[n])
                        bank_free[i] = tu = DVE.do(lambda e, W=W, n=n: e.tensor_tensor(SU[n], W[:, :], SG[n],
                                                                                      ALU.mult))
                fo[j] = hilo(None, 0, 2, FH[n][:, :], FL[n][:, :], SU[n], tu)
            v = lambda b: b.rearrange("p (f c) -> p f c", f=2)
            js = () if j in (0, 10) else (9, 10) if j == 11 else (j - 1,)
            if js:
                ys = row_chunks(js, 11, [([fo[m]], v(FH[m % 2][:, :]), v(FL[m % 2][:, :]), 0) for m in js])
                for m in js:
                    f_free[m % 2] = [PE.last(), DVE.last()]
        outs = []
        for t in range(2):
            tr = rms_stats(t, gated(ys, 1, t))
            DVE.wait(tr, t_gf)
            tz = DVE.do(lambda e, t=t: e.scalar_tensor_tensor(U[:, t, :], X[:, t, :], BN[:, t, 14:15],
                                                              BV[g_i][:, :], ALU.mult, ALU.mult))
            SP.wait(tz)
            outs.append(load(SP, f"out{t}", (out[0, 128 * t:128 * t + 128, :], U[:, t, :])))
        SP.wait(*outs)
        assert split_n[0] == len(chunks) and issued[0] == len(chunks) and used[0] == mm_n[0]

        block = ctx.enter_context(nc.Block())

        @block.sync
        def _(e):
            SP.emit(e)

        @block.gpsimd
        def _(e):
            PO.emit(e)

        @block.scalar
        def _(e):
            AC.emit(e)

        @block.vector
        def _(e):
            DVE.emit(e)

        @block.tensor
        def _(e):
            PE.emit(e)


def constants():
    f = np.float32
    p = np.arange(128)
    c = {"c_idn": np.eye(128, dtype=f)}
    sel = np.zeros((4, 4, 128), f)
    for h in range(4):
        sel[h, h] = 1.0
    c["c_sel"] = sel.reshape(4, 512)
    c["c_msk"] = np.concatenate([np.where(p[None, :] >= p[:, None], 0.0, NEG), np.zeros((128, 128))], 1).astype(f)
    win = np.zeros((4, 256, 256), f)
    t = np.arange(256)
    for g, w in enumerate((2, 4, 8, 16)):
        inside = (t[None, :] >= t[:, None]) & (t[None, :] - t[:, None] < w)
        win[g] = inside / np.minimum(t + 1, w).astype(f)[None, :]
        win[g] -= np.eye(256, dtype=f)
    c["c_win"] = np.concatenate([np.concatenate([win[g, 0:128, 0:144], win[g, 128:256, 128:256]], 1)
                                 for g in range(4)], 1).astype(f)
    rel = (128 + p[:, None] - t[None, :]).astype(f)
    slopes = 2.0 ** (-8.0 * np.arange(1, 5, dtype=f) / 4)
    c["c_alibi"] = np.concatenate([np.where(rel >= 0, -s * rel, NEG) for s in slopes], 1).astype(f)
    c["c_causal"] = np.where(rel >= 0, 0.0, NEG).astype(f)
    inv = (f(10000.0) ** (-np.arange(0, 64, 2, dtype=f) / f(64))).astype(f)
    ang = (np.arange(256, dtype=f)[:, None] * inv[None, :]).astype(f)
    cos, sin = np.cos(ang).astype(f), np.sin(ang).astype(f)
    c["c_rope_t"] = np.concatenate([x[128 * t:128 * t + 128] for x in (cos, sin) for t in range(2)], 1)
    c["c_rope_f"] = np.concatenate([np.tile(cos.T, (4, 1)), np.tile(np.concatenate([-sin.T, sin.T]), (2, 1))], 1)
    return {k: np.ascontiguousarray(v, dtype=f) for k, v in c.items()}


_INS = ["x", "mem", "mlstm_w_in", "mlstm_gate_b", "mlstm_conv_w", "mlstm_norm_g", "mlstm_w_out", "pool_w",
        "pool_scale", "mem_w_kv", "xattn_wq", "xattn_wo", "mlp_w1", "mlp_b1", "mlp_w2", "mlp_b2", "ln_g", "ln_b",
        "c_2", "w_ada_2", "b_ada_2", "g_mix_2", "w_in_2", "lambda_q1_2", "lambda_k1_2", "lambda_q2_2",
        "lambda_k2_2", "g_diff_out_2", "g_q_lat_2", "w_q_up_2", "g_kv_lat_2", "w_kv_up_2", "w_out_2", "g_ffn_2",
        "w_ffn_gate_2", "w_ffn_up_2", "w_ffn_down_2", "g_final_2"]


def kernel(**inputs):
    import concourse.bacc as bacc
    from concourse.bass_utils import run_bass_kernel_spmd

    nc = bacc.Bacc("TRN2", target_bir_lowering=False, num_devices=1)
    arrays, args = {}, {}
    for name, a in [(n, np.ascontiguousarray(inputs[n])) for n in _INS] + list(constants().items()):
        arrays[f"in_{name}"] = a
        args[name] = nc.dram_tensor(f"in_{name}", a.shape, mybir.dt.from_np(a.dtype), kind="ExternalInput").ap()
    out = nc.dram_tensor("out_0", (1, 256, 1024), F32, kind="ExternalOutput").ap()
    build_program(nc, args, out)
    r = run_bass_kernel_spmd(nc, [arrays], core_ids=[0])
    return r.results[0]["out_0"]
```

```python
import math
from contextlib import ExitStack

import numpy as np

import concourse.bass as bass
from concourse import mybir

F32 = mybir.dt.float32
F32R = mybir.dt.float32r
ACT = mybir.ActivationFunctionType
ALU = mybir.AluOpType
AX = mybir.AxisListType.X

ALPHA = 4 ** 0.25
LN_EPS = 1e-5
EPS = 1e-6
NEG = -1e30
NR = 4
NS = 4
AHEAD = 4
CH = 2048
LAMBDA_INIT = 0.8 - 0.6 * math.exp(0.0)

MLSTM = "k0 a0 a1 k1 c0 k2 a2 c1 k3 a3 c2 v0 c3 v1".split()
XATTN = "q0 q1 s0 q2 s1 t0 q3 v0 t1 s2 s3 v1 t2 r0 v2 t3 r1 v3".split()
MIXER = ("k0 k2 y0 l0 v0 n0 a0 k1 z0 a1 b0 v1 q0 u0 c0 b1 e0 e1 c1 d0 k3 f0 d1 a2 g0 x0 q1 f1 r0 a3 b2 e2 "
         "c2 g1 b3 e3 f2 d2 c3 r1 f3 d3 g2 x1 g3").split()


class Lane:

    def __init__(self, sem):
        self.sem, self.n, self.q, self.seen = sem, 0, [], {}

    def wait(self, *tokens):
        for t in tokens:
            if t is None:
                continue
            if isinstance(t, list):
                self.wait(*t)
                continue
            sem, val = t
            if self.seen.get(id(sem), 0) < val:
                self.seen[id(sem)] = val
                self.q.append(lambda e, s=sem, v=val: e.wait_ge(s, v))

    def run(self, f):
        self.q.append(f)

    def do(self, f):
        self.n += 1
        self.q.append(lambda e, f=f: f(e).then_inc(self.sem, 1))
        return (self.sem, self.n)

    def last(self):
        return (self.sem, self.n)

    def emit(self, e):
        for f in self.q:
            f(e)


def build_program(nc, I, out):
    ctx = ExitStack()
    with ctx:
        def sb(name, shape, dt=F32):
            return ctx.enter_context(nc.sbuf_tensor(name, shape, dt))

        def sem(name):
            return ctx.enter_context(nc.semaphore(name))

        RAW = [sb(f"raw{i}", [128, CH]) for i in range(NR)]
        WH = [sb(f"wh{i}", [128, CH], F32R) for i in range(NS)]
        WL = [sb(f"wl{i}", [128, CH], F32R) for i in range(NS)]
        X = sb("X", [128, 2, 1024])
        U = sb("U", [128, 2, 1024])
        S = sb("S", [128, 8, 256])
        XH = sb("XH", [128, 8, 256], F32R)
        XL = sb("XL", [128, 8, 256], F32R)
        KV = sb("KV", [128, 4096])
        AR = sb("AR", [128, 8800])
        FHT = sb("FHT", [128, 1280], F32R)
        FLT = sb("FLT", [128, 1280], F32R)
        FH = [FHT[:, 512 * i:512 * i + 512] for i in range(2)]
        FL = [FLT[:, 512 * i:512 * i + 512] for i in range(2)]
        BV = [sb(f"bv{i}", [128, 1024]) for i in range(2)]
        IDN = sb("IDN", [128, 128])
        PC = sb("PC", [128, 278])
        SM = sb("SM", [128, 352])
        BN = sb("BN", [128, 2, 16])

        MOD = AR[:, 0:6144]
        sm_at = [0]

        def cols(n):
            sm_at[0] += n
            assert sm_at[0] <= 352
            return SM[:, sm_at[0] - n:sm_at[0]]

        YB = [ctx.enter_context(nc.psum_tensor(f"YB{i}", [128, 512], F32)) for i in range(4)]
        WBt = [ctx.enter_context(nc.psum_tensor(f"WB{i}", [128, 512], F32)) for i in range(4)]

        PE, DVE, AC, PO = (Lane(sem("s_" + n)) for n in ("pe", "dve", "act", "pool"))
        SP = Lane(None)
        s_raw = [sem(f"s_raw{i}") for i in range(NR)]
        s_dma = {}

        def load(lane, name, *pairs):
            if name not in s_dma:
                s_dma[name] = [sem("d_" + name), 0]
            s = s_dma[name]
            for dst, src in pairs:
                s[1] += 16
                lane.run(lambda e, d=dst, r=src, q=s[0]: e.dma_start(d, r).then_inc(q, 16))
            return (s[0], s[1])

        def now():
            return [PE.last(), DVE.last(), AC.last(), PO.last()]

        bank_free = [None] * 4
        bank_at = [0]

        def bank():
            i = bank_at[0] % 4
            bank_at[0] += 1
            PE.wait(bank_free[i])
            return i, WBt[i]

        chunks = []

        def add(src, a, b, kind="mm"):
            chunks.append((src, a, b, kind))

        def rows(w, k0, nk, c0, c1):
            return w[k0 * 128:(k0 + nk) * 128, c0:c1].rearrange("(k p) c -> p k c", p=128)

        w_in, w_kv = I["mlstm_w_in"][0], I["mem_w_kv"]
        for j in range(4):
            add(rows(w_in, 0, 8, 256 * j, 256 * j + 256), 8, 256)
        for j in range(4):
            for kh in range(2):
                add(rows(w_in, 4 * kh, 4, 1024 + 512 * j, 1536 + 512 * j), 4, 512)
        for j in range(4):
            add(rows(w_kv, 0, 8, 256 * j, 256 * j + 256), 8, 256)
        for j in range(2):
            for kh in range(2):
                add(rows(w_kv, 4 * kh, 4, 1024 + 512 * j, 1536 + 512 * j), 4, 512)
        for j in range(4):
            add(rows(I["mlstm_w_out"][0], 2 * j, 2, 0, 1024), 2, 1024)
        ada = [(k, c) for k in range(8) for c in range(3)]
        for i in range(2):
            if i == 1:
                add(I["pool_w"][0].rearrange("g (k p) c -> p (g k) c", p=128), 8, 256, "pool")
            for j in range(4):
                add(rows(I["xattn_wq"][i], 0, 8, 256 * j, 256 * j + 256), 8, 256)
            for j in range(4):
                add(rows(I["xattn_wo"][i], 2 * j, 2, 0, 1024), 2, 1024)
            for j in range(17):
                if j < 16:
                    add(rows(I["mlp_w1"][i], 0, 8, 256 * j, 256 * j + 256), 8, 256)
                if j > 0:
                    add(rows(I["mlp_w2"][i], 2 * j - 2, 2, 0, 1024), 2, 1024)
                if 2 <= j < 14:
                    k, c = ada.pop(0)
                    add(I["w_ada_2"][0][k * 128:(k + 1) * 128, 2048 * c:2048 * c + 2048], 1, 2048, ("ada", k, c))
        w2i = I["w_in_2"][0]
        for c0, c1 in ((1920, 2240), (1536, 1920)):
            for kh in range(2):
                add(rows(w2i, 4 * kh, 4, c0, c1), 4, c1 - c0)
        w_dqk = lambda j: add(rows(w2i, 0, 8, 256 * j, 256 * j + 256), 8, 256)
        w_dv = lambda kh: add(rows(w2i, 4 * kh, 4, 1024, 1536), 4, 512)
        w_qup = lambda j: add(rows(I["w_q_up_2"][0], 0, 3, 384 * j, 384 * j + 384), 3, 384, "qup")
        w_up = lambda _: add(rows(I["w_kv_up_2"][0], 0, 2, 0, 1024), 2, 1024)
        for f, n in MIXER:
            if f in "kvuq":
                {"k": w_dqk, "v": w_dv, "u": w_up, "q": w_qup}[f](int(n))
        for j in (0, 2, 1, 3):
            add(rows(I["w_out_2"][0], 2 * j, 2, 0, 1024), 2, 1024)
        for j in range(12):
            if j < 11:
                add(rows(I["w_ffn_gate_2"][0], 0, 8, 256 * j, 256 * j + 256), 8, 256)
                add(rows(I["w_ffn_up_2"][0], 0, 8, 256 * j, 256 * j + 256), 8, 256)
            if j > 0:
                add(rows(I["w_ffn_down_2"][0], 2 * j - 2, 2, 0, 1024), 2, 1024)

        issued, split_n, mm_n = [0], [0], [0]
        raw_free = [None] * NR
        slot_done = [None] * NS
        ready = {}
        cact = cols(8)
        small = {}

        def issue():
            n = issued[0]
            if n >= len(chunks):
                return
            issued[0] += 1
            src, a, b, kind = chunks[n]
            SP.wait(raw_free[n % NR])
            dst = RAW[n % NR][:, 0:a * b]
            if len(src.shape) == 3:
                dst = dst.rearrange("p (a b) -> p a b", a=a)
            SP.run(lambda e: e.dma_start(dst, src).then_inc(s_raw[n % NR], 16))
            if kind == "pool":
                v, tv = small["scale"]
                r4 = RAW[n % NR][:, :].rearrange("p (g k c) -> p g k c", g=4, k=2)
                PO.wait(tv, (s_raw[n % NR], 16 * (n // NR + 1)))
                for k in range(2):
                    small["scaled"] = bv_free[v] = PO.do(lambda e, k=k: e.tensor_tensor(
                        r4[:, :, k], r4[:, :, k], BV[v][:, :].rearrange("p (g c) -> p g c", g=4), ALU.mult))

        def split_next():
            n = split_n[0]
            split_n[0] += 1
            src, a, b, kind = chunks[n]
            landed = (s_raw[n % NR], 16 * (n // NR + 1))
            raw = RAW[n % NR]
            if isinstance(kind, tuple):
                _, k, c = kind
                acc = MOD[:, 2048 * c:2048 * c + 2048]
                DVE.wait(landed, small["cact"], small.get(("ada", c)))
                t = DVE.do(lambda e: e.scalar_tensor_tensor(acc, raw[:, :], cact[:, k:k + 1], acc,
                                                            ALU.mult, ALU.add))
                small[("ada", c)] = t
                raw_free[n % NR] = [t]
                issue()
                return False
            m = mm_n[0]
            mm_n[0] += 1
            s = m % NS
            AC.wait(landed, slot_done[s])
            DVE.wait(landed, slot_done[s])
            if kind == "pool":
                AC.wait(small["scaled"])
                DVE.wait(small["scaled"])
            if kind == "qup":
                r = raw[:, 0:1152].rearrange("p (k h c) -> p k h c", k=3, h=2)
                parts = []
                for w in (WH[s], WL[s]):
                    o = w[:, 0:1536].rearrange("p (k c) -> p k c", k=3)
                    parts.append([
                        o[:, :, 0:256].rearrange("p k (h c) -> p k h c", h=2),
                        o[:, :, 256:384].rearrange("p k (h c) -> p k h c", h=2),
                        o[:, :, 384:512].rearrange("p k (h c) -> p k h c", h=2)[:, :, :, 0:32],
                        o[:, :, 384:512].rearrange("p k (h c) -> p k h c", h=2)[:, :, :, 32:64]])
                srcs = [r[:, :, :, 0:128], r[:, :, :, 128:192], r[:, :, :, 160:192], r[:, :, :, 128:160]]
                for hi, lo, x in zip(parts[0], parts[1], srcs):
                    th = AC.do(lambda e, hi=hi, x=x: e.copy(hi, x))
                    DVE.wait(th)
                    tl = DVE.do(lambda e, hi=hi, lo=lo, x=x: e.tensor_tensor(lo, x, hi.bitcast(F32), ALU.subtract))
            else:
                hi, lo, x = WH[s][:, 0:a * b], WL[s][:, 0:a * b], raw[:, 0:a * b]
                th = AC.do(lambda e: e.copy(hi, x))
                DVE.wait(th)
                tl = DVE.do(lambda e: e.tensor_tensor(lo, x, hi.bitcast(F32), ALU.subtract))
            raw_free[n % NR] = [th, tl]
            ready[m] = (s, [th, tl])
            issue()
            return True

        used = [0]

        def use(later=False):
            m = used[0]
            used[0] += 1
            if not later:
                catch_up()
            while not later and mm_n[0] <= m + AHEAD - 1 and split_n[0] < len(chunks):
                if split_next():
                    held[0] = max(held[0] - 1, 0)
            s, (th, tl) = ready.pop(m)
            return s, th, tl

        held = [0]

        def release(s, tok):
            slot_done[s[0]] = tok
            held[0] += 1

        def catch_up(most=9):
            while held[0] > 0 and most > 0 and split_n[0] < len(chunks):
                if split_next():
                    held[0] -= 1
                    most -= 1

        def mm(o, l, r, start, stop):
            return lambda e: e.matmul(o, l, r, start=start, stop=stop)

        class Part:

            def __init__(self, t, k0, k1, hi, lo):
                self.t, self.k0, self.k1, self.hi, self.lo = t, k0, k1, hi, lo

        def wait_part(parts, t, k, lo):
            for p in parts:
                if p.k0 <= k < p.k1 and (t is None or p.t is None or t == p.t):
                    PE.wait(p.lo if lo else p.hi)

        def passes(o, k_n, terms, start, stop):
            for n in range(3):
                for k in range(k_n):
                    wait, l, r = terms(k)[n]
                    wait()
                    f = mm(o, l, r, start and n == 0 and k == 0, stop and n == 2 and k == k_n - 1)
                    tok = PE.do(f) if n == 2 and k == k_n - 1 else PE.run(f)
            return tok

        def fm_gemm(s, a, b, off, o, parts, xh=None, xl=None):
            xh, xl = xh or XH, xl or XL
            _, th, tl = s

            def terms(k):
                l = slice(k * b + off, k * b + off + 128)
                hi, lo = WH[s[0]][:, l], WL[s[0]][:, l]
                return ((lambda: (PE.wait(th), wait_part(parts, None, k, False)), hi, xh[:, k, :]),
                        (lambda: PE.wait(tl), lo, xh[:, k, :]),
                        (lambda: wait_part(parts, None, k, True), hi, xl[:, k, :]))
            return passes(o, a, terms, True, True)

        def tm_gemm(s, a, b, c0, c1, o, t, k0, start, stop, parts, xh=None, xl=None, w=None):
            xh, xl = xh or XH, xl or XL
            tk = slice(128 * t, 128 * t + 128)
            _, th, tl = s

            def terms(k):
                r = slice(k * b + c0, k * b + c1)
                hi, lo = (w(WH[s[0]], k), w(WL[s[0]], k)) if w else (WH[s[0]][:, r], WL[s[0]][:, r])
                x, y = xh[:, k0 + k, tk], xl[:, k0 + k, tk]
                return ((lambda: (PE.wait(th), wait_part(parts, t, k0 + k, False)), x, hi),
                        (lambda: PE.wait(tl), x, lo),
                        (lambda: wait_part(parts, t, k0 + k, True), y, hi))
            return passes(o, a, terms, start, stop)

        yb_free = [None] * 4

        def row_chunks(js, n, xs):
            ss = [use(later=js[-1] == n - 1) for _ in js]
            if js[0] == 0:
                PE.wait(*yb_free)
            toks = []
            for t in range(2):
                for nb in range(2):
                    for j, s, (parts, xh, xl, xk) in zip(js, ss, xs):
                        tok = tm_gemm(s, 2, 1024, 512 * nb, 512 * nb + 512, YB[2 * t + nb][:, :], t, xk,
                                      j == 0, j == n - 1, parts, xh, xl)
                    toks.append(tok)
            for s in ss:
                release(s, tok)
            return toks

        def hilo(t, k0, k1, hi, lo, src, *wait, lane=None):
            lane = lane or AC
            lane.wait(*wait)
            DVE.wait(*wait)
            th = lane.do((lambda e: e.copy(hi, src)) if lane is AC else (lambda e: e.tensor_copy(hi, src)))
            DVE.wait(th)
            tl = DVE.do(lambda e: e.tensor_tensor(lo, src, hi.bitcast(F32), ALU.subtract))
            return Part(t, k0, k1, th, tl)

        def hilo_bank(t, k0, k1, hi, lo, i, src, *wait):
            AC.wait(*wait)
            DVE.wait(*wait)
            th = AC.do(lambda e: e.copy(hi, src))
            DVE.wait(th)
            bank_free[i] = tl = DVE.do(lambda e: e.tensor_tensor(lo, src, hi.bitcast(F32), ALU.subtract))
            return Part(t, k0, k1, th, tl)

        xfree = [None]

        def turn_pe(src, ks, wait):
            i, W = bank()
            PE.wait(*wait)
            for n, k in enumerate(ks):
                f = (lambda e, k=k, n=n, W=W: e.transpose(W[:, 128 * n:128 * n + 128], src(k), IDN[:, :]))
                tp = PE.do(f) if k == ks[-1] else PE.run(f)
            return i, W, tp

        def turn(t, src, nk, wait, H=None, L=None, g=None):
            H, L = H if H is not None else XH, L if L is not None else XL
            tk = slice(128 * t, 128 * t + 128)
            parts = []
            for k0 in range(0, nk, 4):
                ks = range(k0, min(nk, k0 + 4))
                i, W, tp = turn_pe(src, ks, wait)
                AC.wait(tp, *xfree)
                DVE.wait(*xfree)
                if g is None:
                    w = W[:, 0:128 * len(ks)].rearrange("p (k c) -> p k c", k=len(ks))
                    parts.append(hilo_bank(t, k0, ks[-1] + 1, H[:, k0:ks[-1] + 1, tk], L[:, k0:ks[-1] + 1, tk],
                                           i, w))
                    continue
                for n, k in enumerate(ks):
                    th = AC.do(lambda e, n=n, k=k, W=W: e.activation(H[:, k, tk], W[:, 128 * n:128 * n + 128],
                                                                     ACT.Identity, scale=g(k)))
                DVE.wait(th)
                for n, k in enumerate(ks):
                    tl = DVE.do(lambda e, n=n, k=k, W=W: e.scalar_tensor_tensor(
                        L[:, k, tk], W[:, 128 * n:128 * n + 128], g(k), H[:, k, tk].bitcast(F32),
                        ALU.mult, ALU.subtract))
                bank_free[i] = tl
                parts.append(Part(t, k0, ks[-1] + 1, th, tl))
            return parts

        def turn_norm(z, stage, g, b):
            parts, lows = [], []

            def evac(t, q, i, W, tp, lane):
                tk = slice(128 * t, 128 * t + 128)
                lane.wait(tp, *xfree)
                for n, k in enumerate((2 * q, 2 * q + 1)):
                    w = W[:, 128 * n:128 * n + 128]
                    if lane is AC:
                        te = AC.do(lambda e, k=k, w=w: e.activation(S[:, k, tk], w, ACT.Identity,
                                                                    bias=b(k), scale=g(k)))
                    else:
                        te = DVE.do(lambda e, k=k, w=w: e.tensor_scalar(S[:, k, tk], w, g(k), b(k),
                                                                        ALU.mult, ALU.add))
                bank_free[i] = te
                lane.wait(te)
                hi, src = XH[:, 2 * q:2 * q + 2, tk], S[:, 2 * q:2 * q + 2, tk]
                th = lane.do((lambda e: e.copy(hi, src)) if lane is AC else (lambda e: e.tensor_copy(hi, src)))
                p = Part(t, 2 * q, 2 * q + 2, th, None)
                parts.append(p)
                lows.append((p, hi, XL[:, 2 * q:2 * q + 2, tk], src))

            stage(0, 0)
            stage(0, 1)
            stage(1, 0)
            tz = [z(0, h) for h in range(2)]
            stage(1, 1)
            for q in range(4):
                src = lambda k: U[:, 0, 128 * k:128 * k + 128]
                evac(0, q, *turn_pe(src, (2 * q, 2 * q + 1), [tz[q // 2]]), DVE if q == 1 else AC)
            tz = [z(1, h) for h in range(2)]
            for q in range(4):
                src = lambda k: U[:, 1, 128 * k:128 * k + 128]
                evac(1, q, *turn_pe(src, (2 * q, 2 * q + 1), [tz[q // 2]]), DVE if q % 2 else AC)
            for p, hi, lo, src in lows:
                DVE.wait(p.hi, *xfree)
                p.lo = DVE.do(lambda e, hi=hi, lo=lo, src=src: e.tensor_tensor(lo, src, hi.bitcast(F32),
                                                                               ALU.subtract))
            catch_up()
            return parts

        MH = cols(2)
        t_mh = PO.do(lambda e: e.memset(MH, -0.5))

        def rsqrt(o, x, *wait):
            PO.wait(*wait, t_mh)
            return PO.do(lambda e: e.tensor_tensor(o, x, MH[:, 0:o.shape[1]], ALU.pow))

        def bn(t, h):
            return DVE.do(lambda e: e.bn_stats(BN[:, t, 6 * h:6 * h + 6], U[:, t, 512 * h:512 * h + 512]))

        def stats(t, tb):
            DVE.wait(tb)
            tb = DVE.do(lambda e: e.bn_aggr(BN[:, t, 12:14], BN[:, t, 0:12]))
            DVE.wait(tb)
            tb = DVE.do(lambda e: e.tensor_scalar(BN[:, t, 13:14], BN[:, t, 13:14], LN_EPS, None, ALU.add))
            return rsqrt(BN[:, t, 14:15], BN[:, t, 13:14], tb)

        bv_n = [0]
        bv_free = [None] * 2

        def bvec(src):
            n = bv_n[0]
            bv_n[0] += 1
            PO.wait(bv_free[n % 2])
            tok = load(PO, f"bv{n % 2}", (BV[n % 2][:, :], src.partition_broadcast(128)))
            return n % 2, tok

        x_ready = [[None], [None]]

        def layer_norm(ytoks, i, j, b2=False, turned=True):
            (gi, tg), (bi, tb_) = bvec(I["ln_g"][i, j]), bvec(I["ln_b"][i, j])
            tr = {}

            def head(t, h):
                cs = slice(512 * h, 512 * h + 512)
                DVE.wait(*x_ready[t])
                DVE.wait(ytoks[2 * t + h])
                yb_free[2 * t + h] = tu = DVE.do(lambda e: e.scalar_tensor_tensor(
                    U[:, t, cs], X[:, t, cs], 1.0 if b2 else ALPHA, YB[2 * t + h][:, :], ALU.mult, ALU.add))
                DVE.wait(tu)
                tb = bn(t, h)
                if h == 1:
                    tr[t] = stats(t, tb)

            def z(t, h):
                DVE.wait(tr[t])
                cs = slice(512 * h, 512 * h + 512)
                tz = DVE.do(lambda e: e.tensor_scalar(U[:, t, cs], U[:, t, cs], BN[:, t, 12:13],
                                                      BN[:, t, 14:15], ALU.subtract, ALU.mult))
                x_ready[t] = [tz]
                return tz

            if turned:
                c = 32 + (i * 3 + j) * 8
                parts = turn_norm(z, head, lambda k: PC[:, c + k:c + k + 1],
                                  lambda k: PC[:, c + 48 + k:c + 49 + k])
                for t in range(2):
                    PO.wait(*x_ready[t], tg)
                    tx = PO.do(lambda e, t=t: e.tensor_tensor(X[:, t, :], U[:, t, :], BV[gi][:, :], ALU.mult))
                    PO.wait(tx, tb_)
                    x_ready[t] = [PO.do(lambda e, t=t: e.tensor_tensor(X[:, t, :], X[:, t, :], BV[bi][:, :],
                                                                       ALU.add))]
            else:
                parts = None
                tc = {}

                def centre(t):
                    DVE.wait(tr[t], tg)
                    tc[t] = DVE.do(lambda e: e.scalar_tensor_tensor(
                        U[:, t, :], U[:, t, :], BN[:, t, 12:13], BV[gi][:, :], ALU.subtract, ALU.mult))

                def scale(t):
                    DVE.wait(tc[t], tb_)
                    x_ready[t] = [DVE.do(lambda e, cs=slice(512 * h, 512 * h + 512): e.scalar_tensor_tensor(
                        X[:, t, cs], U[:, t, cs], BN[:, t, 14:15], BV[bi][:, cs], ALU.mult, ALU.add))
                        for h in range(2)]

                head(0, 0)
                head(0, 1)
                head(1, 0)
                centre(0)
                head(1, 1)
                scale(0)
                centre(1)
                scale(1)
            bv_free[gi] = bv_free[bi] = [*x_ready[0], *x_ready[1]]
            return parts

        t_idn = load(SP, "idn", (IDN[:, :], I["c_idn"]))
        t_x = []
        for t in range(2):
            t_x.append(load(SP, f"x{t}", (X[:, t, :], I["x"][0, 128 * t:128 * t + 128, :])))
            issue()
        GRAW = BV[1][:, 768:832].rearrange("p (k c) -> p k c", k=8)
        gb = cols(2)
        t_g = load(SP, "gates", (GRAW, w_in[:, 3072:3080].rearrange("(k p) c -> p k c", p=128)),
                   (gb[0:4, 0:1], I["mlstm_gate_b"][0, 0:4].rearrange("(p a) -> p a", a=1)),
                   (gb[0:4, 1:2], I["mlstm_gate_b"][0, 4:8].rearrange("(p a) -> p a", a=1)))

        QP = AR[:, 0:8 * 260].rearrange("p (k c) -> p k c", k=8)
        QC = AR[:, 2080:2080 + 2048].rearrange("p (k c) -> p k c", k=8)
        V1 = AR[:, 4128:4128 + 2064].rearrange("p (t h c) -> p t h c", t=2, h=4)
        OG = AR[:, 6192:6192 + 2048].rearrange("p (t c) -> p t c", t=2)
        GT = AR[:, 8240:8240 + 256]
        MSK = AR[:, 8544:8800]
        ROWS = QC.rearrange("p k c -> p (k c)")[:, 0:384].rearrange("p (r c) -> p r c", r=3)
        G = [BV[0][0:4, 256 * n:256 * n + 256] for n in range(4)] + [BV[1][0:4, 0:256]]
        CSEL = BV[1][0:4, 256:768]

        ms_rows = PO.do(lambda e: e.memset(ROWS[:, 1:3, :], 0.0))
        vec = lambda v: v.rearrange("(k c) -> k c", c=128)
        mat = lambda v: v.rearrange("i (k c) -> (i k) c", c=128)
        lnr = lambda v: v.rearrange("i j (k c) -> (i j k) c", c=128)
        SP.wait(ms_rows)
        t_rows = load(SP, "rows",
                      (ROWS[0:32, 0, :], mat(I["mlstm_conv_w"][0])),
                      (ROWS[32:80, 0, :], lnr(I["ln_g"])),
                      (ROWS[80:128, 0, :], lnr(I["ln_b"])),
                      (ROWS[0:64, 1, :], mat(I["mlp_b1"])),
                      (ROWS[64:72, 1, :], vec(I["mlstm_norm_g"][0])),
                      (ROWS[72:80, 1, :], vec(I["c_2"][0])),
                      (ROWS[0:8, 2, :], vec(I["g_mix_2"][0])),
                      (ROWS[8:16, 2, :], vec(I["g_ffn_2"][0])),
                      (ROWS[16:19, 2, :], vec(I["g_q_lat_2"][0])),
                      (ROWS[19:21, 2, :], vec(I["g_kv_lat_2"][0])),
                      (ROWS[21:22, 2, :], vec(I["g_diff_out_2"][0])))
        for _ in range(NR - 2):
            issue()
        t_tab = load(PO, "tab", (CSEL, I["c_sel"]), (MSK[:, :], I["c_msk"]))
        GH = FH[0][:, :].rearrange("p (k c) -> p k c", k=8)
        GL = FL[0][:, :].rearrange("p (k c) -> p k c", k=8)
        DVE.do(lambda e: e.memset(GH.bitcast(F32), 0.0))
        z2 = DVE.do(lambda e: e.memset(GL.bitcast(F32), 0.0))
        z3 = DVE.do(lambda e: e.memset(QP[:, :, 0:3], 0.0))
        z4 = DVE.do(lambda e: e.memset(V1[:, :, :, 256:258], 1.0))
        z5 = DVE.do(lambda e: e.memset(GT[0:64, :], 0.0))

        PE.wait(t_idn)
        xt = []
        for t in range(2):
            xt += turn(t, lambda k, t=t: X[:, t, 128 * k:128 * k + 128], 8, [t_x[t]])
            if t == 0:
                split_next()
        C_LNG, C_LNB, C_B1, C_NG, C_C = 32, 80, 128, 192, 200
        C_GM, C_GF, C_GQ, C_GK, C_GD = 256, 264, 272, 275, 277

        def columns():
            ci, CW = bank()
            PE.wait(t_rows)
            for r in range(3):
                tp = PE.do(lambda e, r=r: e.transpose(CW[:, 128 * r:128 * r + 128], ROWS[:, r, :], IDN[:, :]))
            AC.wait(tp)
            small["pc"] = AC.do(lambda e: e.copy(PC[:, :], CW[:, 0:278]))
            bank_free[ci] = small["pc"]

        def gates():
            AC.wait(t_g, z2)
            DVE.wait(t_g)
            for o, c in ((0, 0), (32, 4)):
                th = AC.do(lambda e, o=o, c=c: e.copy(GH[:, :, o:o + 4], GRAW[:, :, c:c + 4]))
                DVE.wait(th)
                tl = DVE.do(lambda e, o=o, c=c: e.tensor_tensor(GL[:, :, o:o + 4], GRAW[:, :, c:c + 4],
                                                                GH[:, :, o:o + 4].bitcast(F32), ALU.subtract))
            yield
            gi, GW = bank()
            PE.wait(z2)
            tgm = passes(GW[0:64, 0:256], 8, lambda k: (
                (lambda: (PE.wait(th), wait_part(xt, None, k, False)), GH[:, k, :], XH[:, k, :]),
                (lambda: PE.wait(tl), GL[:, k, :], XH[:, k, :]),
                (lambda: wait_part(xt, None, k, True), GH[:, k, :], XL[:, k, :])), True, True)
            DVE.wait(tgm, t_g)
            DVE.do(lambda e: e.tensor_scalar(G[0], GW[0:4, 0:256], gb[0:4, 0:1], None, ALU.add))
            tb = DVE.do(lambda e: e.tensor_copy(G[1], GW[32:36, 0:256]))
            bank_free[gi] = tb
            DVE.wait(tb)
            tb = DVE.do(lambda e: e.tensor_scalar(G[1], G[1], gb[0:4, 1:2], None, ALU.add))
            DVE.wait(tb)
            tc = DVE.do(lambda e: e.scalar_tensor_tensor(G[2], G[1], -1.0, G[1], ALU.mult, ALU.max))
            yield
            AC.wait(tc)
            td = AC.do(lambda e: e.activation(G[3], G[2], ACT.Exp, scale=-1.0))
            AC.wait(td)
            td = AC.do(lambda e: e.activation(G[4], G[3], ACT.Ln, bias=1.0))

            yield
            DVE.wait(td, z5)
            t1 = DVE.do(lambda e: e.scalar_tensor_tensor(G[2], G[1], 0.0, G[4], ALU.min, ALU.subtract))
            t2 = DVE.do(lambda e: e.memset(G[3], 1.0))
            DVE.wait(t1, t2)
            t1 = DVE.do(lambda e: e.tensor_tensor_scan(G[1], G[3], G[2], 0.0, ALU.mult, ALU.add))
            DVE.wait(t1)
            t1 = DVE.do(lambda e: e.tensor_tensor(GT[0:4, :], G[0], G[1], ALU.subtract))
            DVE.wait(t1)
            tM = DVE.do(lambda e: e.tensor_tensor_scan(G[4], GT[0:4, :], GT[0:4, :], 0.0, ALU.max, ALU.max))
            DVE.wait(tM)
            t3 = DVE.do(lambda e: e.tensor_tensor(G[2], G[1], G[4], ALU.add))
            yield
            AC.wait(t3)
            tem = AC.do(lambda e: e.activation(GT[32:36, :], G[2], ACT.Exp, scale=-1.0))
            small["cact"] = AC.do(lambda e: e.activation(cact, PC[:, C_C:C_C + 8], ACT.Silu))

            small["gates"] = tem, tM
            yield

        qp_tok, t_conv = {}, []

        def conv(j):
            DVE.wait(qp_tok[j], small["pc"], z3)
            for f in range(2):
                k = 2 * j + f
                cw = lambda n, k=k: PC[:, 8 * n + k:8 * n + k + 1]
                tv = DVE.do(lambda e, k=k, cw=cw: e.tensor_scalar(QC[:, k, :], QP[:, k, 0:256], cw(0), None,
                                                                  ALU.mult))
                for n in range(1, 4):
                    DVE.wait(tv)
                    tv = DVE.do(lambda e, k=k, n=n, cw=cw: e.scalar_tensor_tensor(
                        QC[:, k, :], QP[:, k, n:n + 256], cw(n), QC[:, k, :], ALU.mult, ALU.add))
            return tv

        for j in range(4):
            s = use()
            i, W = bank()
            for f in range(2):
                tp = fm_gemm(s, 8, 256, 128 * f, W[:, 256 * f:256 * f + 256], xt)
            release(s, tp)
            AC.wait(tp)
            qp_tok[j] = AC.do(lambda e, j=j, W=W: e.copy(QP[:, 2 * j:2 * j + 2, 3:259],
                                                         W[:, :].rearrange("p (f c) -> p f c", f=2)))
            bank_free[i] = qp_tok[j]
            if j == 0:
                PO.wait(tp)
                t_mem = load(PO, "mem", (U[:, :, :], I["mem"][0].rearrange("(t p) c -> p t c", p=128)))
                columns()
                gate_stages = gates()
                next(gate_stages)
            else:
                next(gate_stages)
            if j > 1:
                t_conv[:] = [conv(j - 2)]
        next(gate_stages)
        tem, tM = small["gates"]
        def uv_columns():
            ui, UW = bank()
            PE.wait(tem, tM)
            for t in range(2):
                tp = PE.do(lambda e, t=t: e.transpose(UW[:, 64 * t:64 * t + 64], GT[0:64, 128 * t:128 * t + 128],
                                                      IDN[0:64, 0:64]))
            DVE.wait(tp)
            t_uc = DVE.do(lambda e: e.tensor_copy(UC.rearrange("p (t c) -> p t c", t=2),
                                                  UW[:, 0:128].rearrange("p (t c) -> p t c", t=2)[:, :, 0:36]))
            bank_free[ui] = t_uc
            return t_uc

        UC = cols(72)
        def tm_panel(width, evac, parts):
            bs = [bank() for _ in range(2)]
            for kh in range(2):
                s = use()
                for t in range(2):
                    tp = tm_gemm(s, 4, width, 0, width, bs[t][1][:, 0:width], t, 4 * kh, kh == 0, kh == 1,
                                 parts)
                    if kh == 1:
                        bank_free[bs[t][0]] = evac(t, bs[t][1], tp)
                release(s, tp)

        def ev_v(j, dst):
            def f(t, W, tp):
                AC.wait(tp)
                return AC.do(lambda e: e.copy(dst(t), W[:, :].rearrange("p (h c) -> p h c", h=2)))
            return f

        AC.wait(z4)
        for j in range(2):
            tm_panel(512, ev_v(j, lambda t, j=j: V1[:, t, 2 * j:2 * j + 2, 0:256]), xt)
            if j == 0:
                t_uc = uv_columns()
                AC.wait(t_conv[0])
                AC.do(lambda e: e.activation(QC[:, 0:4, :], QC[:, 0:4, :], ACT.Silu))
            t_conv.append(conv(j + 2))
        t_v1 = AC.last()

        def ev_o(j):
            def f(t, W, tp):
                AC.wait(tp)
                return AC.do(lambda e: e.activation(OG[:, t, 512 * j:512 * j + 512], W[:, :], ACT.Sigmoid))
            return f

        def mem_half():
            for t in range(2):
                for k0 in (0, 4):
                    i, W, tp = turn_pe(lambda k, t=t: U[:, t, 128 * k:128 * k + 128], range(k0, k0 + 4), [t_mem])
                    L = (AC, DVE)[k0 // 4]
                    L.wait(tp)
                    o, w = S[:, k0:k0 + 4, 128 * t:128 * t + 128], W[:, :].rearrange("p (k c) -> p k c", k=4)
                    bank_free[i] = L.do((lambda e, o=o, w=w: e.copy(o, w)) if L is AC else
                                        (lambda e, o=o, w=w: e.tensor_copy(o, w)))

        for j in range(2):
            tm_panel(512, ev_o(j), xt)
            if j == 0:
                AC.wait(t_conv[-1])
                t_qc = AC.do(lambda e: e.activation(QC[:, 4:8, :], QC[:, 4:8, :], ACT.Silu))
                mem_half()
                mem_turned, s_mem = PE.last(), [AC.last(), DVE.last()]
        t_og = AC.last()
        x_gemm = PE.last()

        DT = [AR[:, 384 * n:384 * n + 384] for n in range(2)]
        SC = [AR[:, 768 + 384 * n:1152 + 384 * n] for n in range(2)]
        sc_tok, sc_free, dt_free = {}, [None] * 2, [None] * 2

        def head_a(h):
            bi, MB = bank()
            PE.wait(tM, t_tab)
            tp = PE.do(mm(MB[:, 0:256], CSEL[:, 128 * h:128 * h + 128], G[4], True, True))
            si, SW = bank()
            PE.wait(t_qc)
            PE.run(mm(SW[:, 0:256], QC[:, 4 + h, 0:128], QC[:, h, :], True, True))
            tq = PE.do(mm(SW[:, 256:384], QC[:, 4 + h, 128:256], QC[:, h, 128:256], True, True))
            D, C = DT[h % 2], SC[h % 2]
            DVE.wait(tp, t_tab, dt_free[h % 2], *t_conv)
            DVE.do(lambda e: e.scalar_tensor_tensor(D[:, 0:256], MB[:, 0:256], -1.0, MSK[:, :],
                                                    ALU.mult, ALU.add))
            td = DVE.do(lambda e: e.scalar_tensor_tensor(D[:, 256:384], MB[:, 128:256], -1.0, MSK[:, 0:128],
                                                         ALU.mult, ALU.add))
            bank_free[bi] = td
            AC.wait(td, t_uc)
            AC.do(lambda e: e.activation(D[:, 0:256], D[:, 0:256], ACT.Exp, bias=UC[:, h:h + 1]))
            te = AC.do(lambda e: e.activation(D[:, 256:384], D[:, 256:384], ACT.Exp, bias=UC[:, 36 + h:37 + h]))
            DVE.wait(te, tq, sc_free[h % 2])
            sc_tok[h] = DVE.do(lambda e: e.scalar_tensor_tensor(C, SW[:, 0:384], 128 ** -0.5, D,
                                                                ALU.mult, ALU.mult))
            dt_free[h % 2] = bank_free[si] = sc_tok[h]

        y_tok = []

        def head_c(h):
            C = SC[h % 2]
            PE.wait(sc_tok[h], t_v1, z4)
            for t in range(2):
                b = (2 * h + t) % 4
                Y = YB[b]
                PE.wait(yb_free[b])
                if t == 0:
                    tn = PE.do(mm(Y[:, 0:258], C[:, 0:128], V1[:, 0, h, :], True, True))
                else:
                    PE.run(mm(Y[:, 0:258], C[:, 128:256], V1[:, 0, h, :], True, False))
                    tn = PE.do(mm(Y[:, 0:258], C[:, 256:384], V1[:, 1, h, :], False, True))
                    sc_free[h % 2] = tn
                w = cols(4)
                em = UC[:, 36 * t + 32 + h:36 * t + 33 + h]
                DVE.wait(tn)
                t1 = DVE.do(lambda e, w=w, Y=Y, em=em: e.tensor_scalar(w[:, 0:1], Y[:, 256:257], -1.0, em,
                                                                       ALU.mult, ALU.max))
                DVE.wait(t1)
                t1 = DVE.do(lambda e, w=w, Y=Y: e.tensor_scalar(w[:, 0:1], Y[:, 256:257], w[:, 0:1], None,
                                                                ALU.max))
                DVE.wait(t1)
                t1 = DVE.do(lambda e, w=w: e.reciprocal(w[:, 1:2], w[:, 0:1]))
                AC.wait(t1)
                t2 = AC.do(lambda e, w=w, Y=Y, t=t: e.activation(JK, Y[:, 0:256], ACT.Square,
                                                                 scale=w[:, 1:2], accum_out=w[:, 2:3]))
                PO.wait(t2)
                t3 = PO.do(lambda e, w=w: e.tensor_scalar(w[:, 2:3], w[:, 2:3], 1 / 256, LN_EPS,
                                                          ALU.mult, ALU.add))
                t3 = rsqrt(w[:, 3:4], w[:, 2:3], t3)
                PO.wait(t3)
                t3 = PO.do(lambda e, w=w: e.tensor_tensor(w[:, 3:4], w[:, 3:4], w[:, 1:2], ALU.mult))
                DVE.wait(t3, t_og, mem_turned)
                yb_free[b] = t4 = DVE.do(lambda e, w=w, Y=Y, t=t: e.scalar_tensor_tensor(
                    U[:, t, 256 * h:256 * h + 256], Y[:, 0:256], w[:, 3:4],
                    OG[:, t, 256 * h:256 * h + 256], ALU.mult, ALU.mult))
                y_tok.append(t4)

        JK = AR[:, 1536:1792]
        KT = KV[:, 0:2048].rearrange("p (k c) -> p k c", k=8)
        VM = KV[:, 2048:4096].rearrange("p (t c) -> p t c", t=2)

        def k_chunk(j):
            s = use()
            i, W = bank()
            for f in range(2):
                tp = fm_gemm(s, 8, 256, 128 * f, W[:, 256 * f:256 * f + 256], mt)
            release(s, tp)
            AC.wait(tp)
            bank_free[i] = AC.do(lambda e: e.copy(KT[:, 2 * j:2 * j + 2, :],
                                                  W[:, :].rearrange("p (f c) -> p f c", f=2)))

        def ev_m(j):
            def f(t, W, tp):
                AC.wait(tp)
                return AC.do(lambda e: e.copy(VM[:, t, 512 * j:512 * j + 512], W[:, :]))
            return f

        mt = [hilo(None, 2 * q, 2 * q + 2, XH[:, 2 * q:2 * q + 2, :], XL[:, 2 * q:2 * q + 2, :],
                   S[:, 2 * q:2 * q + 2, :], x_gemm, s_mem) for q in range(4)]
        steps = {"k": k_chunk, "a": head_a, "c": head_c, "v": lambda j: tm_panel(512, ev_m(j), mt)}
        for f, n in MLSTM:
            steps[f](int(n))
        t_kv = AC.last()
        xfree[:] = now()
        yt = []
        for t in range(2):
            yt += turn(t, lambda k, t=t: U[:, t, 128 * k:128 * k + 128], 8, y_tok[t::2],
                       g=lambda k: PC[:, C_NG + k:C_NG + k + 1])
        for js in ((0,), (1,), (2, 3)):
            ys = row_chunks(js, 4, [(yt, XH, XL, 2 * j) for j in js])
        x_ready = [[t_x[0]], [t_x[1]]]
        xfree[:] = now()
        xt = layer_norm(ys, 0, 0)

        TMP = AR[:, 6144:8800]
        xa_free = {}

        def xattn(xt, first):
            QT = [TMP[:, 512 * n:512 * n + 512] for n in range(2)]
            PB = [TMP[:, 1024 + 512 * n:1536 + 512 * n] for n in range(2)]
            PT = TMP[:, 2048:2560]
            tok = {}
            xo = {}

            def p0(h):
                s = use()
                i, W = bank()
                for f in range(2):
                    tp = fm_gemm(s, 8, 256, 128 * f, W[:, 256 * f:256 * f + 256], xt)
                release(s, tp)
                AC.wait(tp, xa_free.get(("q", h % 2)), *first)
                bank_free[i] = tok["q", h] = AC.do(lambda e: e.copy(QT[h % 2], W[:, :]))
                if h == 3:
                    tok["wq"] = tp

            def p1(h):
                i, W = bank()
                PE.wait(tok["q", h], t_kv)
                Q = QT[h % 2].rearrange("p (f c) -> p f c", f=2)
                for t in range(2):
                    for f in range(2):
                        m = mm(W[:, 256 * t:256 * t + 256], Q[:, f, 128 * t:128 * t + 128],
                               KT[:, 2 * h + f, :], f == 0, f == 1)
                        tp = PE.do(m) if t * f else PE.run(m)
                xa_free["q", h % 2] = tp
                w = cols(6)
                W3 = W[:, :].rearrange("p (t c) -> p t c", t=2)
                P = PB[h % 2].rearrange("p (t c) -> p t c", t=2)
                DVE.wait(tp)
                t1 = DVE.do(lambda e: e.tensor_reduce(w[:, 0:2], W3, AX, ALU.max))
                DVE.wait(t1)
                t1 = DVE.do(lambda e: e.tensor_scalar(w[:, 0:2], w[:, 0:2], -1 / 16, None, ALU.mult))
                AC.wait(t1, xa_free.get(("p", h % 2)), *first)
                for t in range(2):
                    te = AC.do(lambda e, t=t: e.activation(P[:, t, :], W3[:, t, :], ACT.Exp, bias=w[:, t:t + 1],
                                                           scale=1 / 16, accum_out=w[:, 2 + t:3 + t]))
                bank_free[i] = te
                DVE.wait(te)
                t1 = DVE.do(lambda e: e.reciprocal(w[:, 4:6], w[:, 2:4]))
                DVE.wait(t1)
                for t in range(2):
                    t2 = DVE.do(lambda e, t=t: e.tensor_scalar(P[:, t, :], P[:, t, :], w[:, 4 + t:5 + t], None,
                                                               ALU.mult))
                tok["p", h] = t2

            def p2(h):
                i, W = bank()
                P = PB[h % 2].rearrange("p (t c) -> p t c", t=2)
                PE.wait(tok["p", h])
                for m in range(2):
                    for t in range(2):
                        tp = PE.do(lambda e, m=m, t=t: e.transpose(
                            W[:, 256 * m + 128 * t:256 * m + 128 * t + 128], P[:, t, 128 * m:128 * m + 128],
                            IDN[:, :]))
                xa_free["p", h % 2] = tp
                AC.wait(tp, xa_free.get("pt"))
                bank_free[i] = tok["pt", h] = AC.do(lambda e: e.copy(PT, W[:, :]))

            def p3(h):
                i, W = bank()
                PE.wait(tok["pt", h])
                for d in range(2):
                    for m in range(2):
                        f = mm(W[:, 256 * d:256 * d + 256], VM[:, m, 256 * h + 128 * d:256 * h + 128 * d + 128],
                               PT[:, 256 * m:256 * m + 256], m == 0, m == 1)
                        tp = PE.do(f) if d * m else PE.run(f)
                xa_free["pt"] = tp
                xo[h] = hilo_bank(None, 2 * h, 2 * h + 2, XH[:, 2 * h:2 * h + 2, :], XL[:, 2 * h:2 * h + 2, :], i,
                                  W[:, :].rearrange("p (f c) -> p f c", f=2), tp, tok["wq"])

            def r(*hs):
                return row_chunks(hs, 4, [([xo[h]], XH, XL, 2 * h) for h in hs])

            steps = {"q": p0, "s": p1, "t": p2, "v": p3, "r": r}
            for f, h in XATTN:
                steps[f](int(h))
            ys = r(2, 3)
            xfree[:] = now()
            return ys

        f_free = [[None], [None]]

        def mlp(i, xt, first, R0, at14=None):
            RT = [R0[:, 512 * n:512 * n + 512] for n in range(2)]
            RS = R0[:, 1024:1536]
            fo = {}
            b2i, tb2 = bvec(I["mlp_b2"][i])
            for t in range(2):
                PO.wait(*x_ready[t])
                tx = PO.do(lambda e, t=t: e.tensor_scalar(X[:, t, :], X[:, t, :], ALPHA, None, ALU.mult))
                PO.wait(tx, tb2)
                tx = PO.do(lambda e, t=t: e.tensor_tensor(X[:, t, :], X[:, t, :], BV[b2i][:, :], ALU.add))
                x_ready[t] = [tx]
            bv_free[b2i] = tx
            if i == 0:
                small["scale"] = bvec(I["pool_scale"][0])
            for j in range(17):
                if j < 16:
                    s = use()
                    bi, W = bank()
                    for f in range(2):
                        tp = fm_gemm(s, 8, 256, 128 * f, W[:, 256 * f:256 * f + 256], xt)
                    release(s, tp)
                    R = RT[j % 2]
                    AC.wait(tp, *first)
                    AC.wait(*f_free[j % 2])
                    for f in range(2):
                        c = C_B1 + 32 * i + 2 * j + f
                        tr = AC.do(lambda e, f=f, c=c, W=W, R=R: e.activation(
                            R[:, 256 * f:256 * f + 256], W[:, 256 * f:256 * f + 256], ACT.Relu,
                            bias=PC[:, c:c + 1]))
                    bank_free[bi] = tr
                    AC.wait(tr)
                    H, L = FH[j % 2][:, :], FL[j % 2][:, :]
                    th = AC.do(lambda e, R=R, H=H: e.activation(H, R, ACT.Square))
                    DVE.wait(tr, fo[j - 1].lo if j else None, *f_free[j % 2])
                    tr = DVE.do(lambda e, R=R: e.tensor_tensor(RS, R, R, ALU.mult))
                    DVE.wait(th, tr)
                    tl = DVE.do(lambda e, H=H, L=L: e.tensor_tensor(L, RS, H.bitcast(F32), ALU.subtract))
                    fo[j] = Part(None, 0, 2, th, tl)
                v = lambda b: b.rearrange("p (f c) -> p f c", f=2)
                js = () if j in (0, 15) else (14, 15) if j == 16 else (j - 1,)
                if js:
                    ys = row_chunks(js, 16, [([fo[m]], v(FH[m % 2][:, :]), v(FL[m % 2][:, :]), 0) for m in js])
                    for m in js:
                        f_free[m % 2] = [PE.last(), DVE.last()]
                if j == 14 and at14:
                    at14()
            xfree[:] = now()
            return ys

        cut = now()
        ys = xattn(xt, cut)
        xt = layer_norm(ys, 0, 1)
        cut = now()
        WM = TMP[:, 1536:2624]
        PO.wait(*cut)
        PO.wait(PO.do(lambda e: e.memset(MOD, 0.0)))
        small[("ada", 0)] = small[("ada", 1)] = small[("ada", 2)] = load(
            PO, "mod", (MOD[0:1, :], I["b_ada_2"][0].rearrange("(a c) -> a c", a=1)))
        t_wm = load(PO, "wm", (WM, I["c_win"]))
        ys = mlp(0, xt, cut, TMP)
        layer_norm(ys, 0, 2, b2=True, turned=False)

        catch_up(1)
        po, xfree[:] = [], now()
        wm = lambda g, a, c: WM[:, 272 * g + a:272 * g + c]
        ws = [bank() for _ in range(4)]
        PE.wait(t_wm, *x_ready[0])
        for k in range(8):
            o = ws[k // 2][1][:, 256 * (k % 2):256 * (k % 2) + 256]
            tp = PE.do(mm(o[:, 0:144], X[:, 0, 128 * k:128 * k + 128], wm(k // 2, 0, 144), k % 2 == 0, False))
        PE.wait(*x_ready[1])
        for k in range(8):
            i, W = ws[k // 2]
            o = W[:, 256 * (k % 2):256 * (k % 2) + 256]
            PE.run(mm(o[:, 128:144], X[:, 1, 128 * k:128 * k + 128], wm(k // 2, 144, 160), False, False))
            tp = PE.do(mm(o[:, 144:256], X[:, 1, 128 * k:128 * k + 128], wm(k // 2, 160, 272), False, k % 2 == 1))
            if k % 2:
                po.append(hilo_bank(None, k - 1, k + 1, XH[:, k - 1:k + 1, :], XL[:, k - 1:k + 1, :], i,
                                    W[:, :].rearrange("p (f c) -> p f c", f=2), tp, *xfree))
        s = use(later=True)
        ys = []
        PE.wait(*yb_free)
        for t in range(2):
            for g in range(4):
                tp = tm_gemm(s, 2, 256, 512 * g, 512 * g + 256, YB[2 * t + g // 2][:, 256 * (g % 2):256 * (g % 2) + 256],
                             t, 2 * g, True, True, po)
                if g % 2:
                    ys.append(tp)
        release(s, tp)
        xfree[:] = now()
        xt = layer_norm(ys, 1, 0)
        cut = now()
        ys = xattn(xt, cut)
        xt = layer_norm(ys, 1, 1)
        cut = now()

        MC = cols(32)
        modt = {}

        ONE = TMP[:, 2048:2176]
        DVE.wait(*cut)
        ms_one = DVE.do(lambda e: e.memset(ONE, 1.0))

        def modulation(n, o):
            for k in range(16):
                m = 24 * n + k
                tp = mm(o[:, 2 * k:2 * k + 2], MOD[:, 128 * m:128 * m + 128], ONE[:, 0:2], True, True)
                tp = PE.do(tp) if k == 15 else PE.run(tp)
            return tp

        def modulation_out(n, o, tp):
            a, g = 16 * n, (C_GM, C_GF)[n]
            DVE.wait(tp)
            te = DVE.do(lambda e: e.tensor_copy(MC[:, a:a + 16], o[:, 0:32].rearrange("p (n a) -> p n a", a=2)[:, :, 0]))
            DVE.wait(te)
            modt[n] = DVE.do(lambda e: e.scalar_tensor_tensor(
                MC[:, a + 8:a + 16], MC[:, a + 8:a + 16], 1.0, PC[:, g:g + 8], ALU.add, ALU.mult))
            return te

        GB = AR[:, 6144:8192].rearrange("p (n c) -> p n c", n=2)

        def late():
            PE.wait(small["ada", 0], small["ada", 1], small["ada", 2], ms_one)
            i, W = bank()
            bank_free[i] = modulation_out(0, W, modulation(0, W))

        ys = mlp(1, xt, cut, KV, late)
        layer_norm(ys, 1, 2, b2=True, turned=False)
        for n in range(2):
            for h in range(2):
                Y, src = YB[2 * n + h], (2048, 5120)[n] + 512 * h
                PE.wait(yb_free[2 * n + h])
                tp = PE.do(mm(Y[:, :], ONE, MOD[:, src:src + 512], True, True))
                AC.wait(tp)
                yb_free[2 * n + h] = AC.do(lambda e, n=n, h=h, Y=Y: e.copy(GB[:, n, 512 * h:512 * h + 512], Y[:, :]))
        t_gb = [AC.last()]
        PE.wait(yb_free[0])
        t_mf = modulation(1, YB[0])

        Uf = U[:, :, :].rearrange("p t c -> p (t c)")
        Sf = S[:, :, :].rearrange("p k c -> p (k c)")
        DQ = AR[:, 0:1024].rearrange("p (h c) -> p h c", h=4)
        KD = AR[:, 1024:3072].rearrange("p (h s c) -> p h s c", h=4, s=2)
        DV = AR[:, 3072:4096].rearrange("p (t c) -> p t c", t=2)
        QL = AR[:, 4096:4864].rearrange("p (t c) -> p t c", t=2)
        KL = AR[:, 4864:5504].rearrange("p (t c) -> p t c", t=2)
        PTS = [Uf[:, 1536:1920], AR[:, 5504:5888]]
        OTS = [w.rearrange("p (t c) -> p t c", t=2) for w in (AR[:, 5888:6144], BV[1][:, 384:640])]
        E2 = [[Uf[:, 768 * n + 384 * m:768 * n + 384 * m + 384] for m in range(2)] for n in range(2)]
        CS = AR[:, 8192:8704].rearrange("p (n c) -> p n c", n=2)
        QN = KV[:, 0:1024].rearrange("p (h c) -> p h c", h=4)
        QPE = KV[:, 1024:1536].rearrange("p (j c) -> p j c", j=2)
        KN = KV[:, 1536:2560].rearrange("p (h c) -> p h c", h=4)
        KPE = KV[:, 2560:3072].rearrange("p (s c) -> p s c", s=2)
        V2 = Sf[:, 384:1408].rearrange("p (t c) -> p t c", t=2)
        QT2 = [Sf[:, 1536:1792], Sf[:, 1792:2048]]
        LQH, LQL = (w[:, 0:768].rearrange("p (k c) -> p k c", k=3) for w in (FHT, FLT))
        LKH, LKL = (w[:, 768:1280].rearrange("p (k c) -> p k c", k=2) for w in (FHT, FLT))
        RT = Sf[:, 0:256].rearrange("p (t c) -> p t c", t=2)
        RA = Sf[:, 256:384].rearrange("p (n t c) -> p n t c", n=2, t=2)
        TB = [BV[0][:, 256 * h:256 * h + 256] for h in range(4)] + [BV[1][:, 0:256]]
        TR = BV[1][:, 256:384].rearrange("p (n t c) -> p n t c", n=2, t=2)

        JX = [AR[:, 0:1024], AR[:, 1024:2048]]

        def rms_half(t, h, ready):
            cs = slice(512 * h, 512 * h + 512)
            AC.wait(ready)
            return AC.do(lambda e: e.activation(JX[t][:, cs], X[:, t, cs], ACT.Square, scale=1 / 32,
                                                accum_out=BN[:, t, 12 + h:13 + h]))

        def rms_stats(t, halves):
            PO.wait(halves)
            t1 = PO.do(lambda e: e.tensor_scalar(BN[:, t, 13:14], BN[:, t, 13:14], BN[:, t, 12:13], EPS,
                                                 ALU.add, ALU.add))
            return rsqrt(BN[:, t, 14:15], BN[:, t, 13:14], t1)

        def rms_turn(a, b, step):
            tr = {}

            def z(t, h):
                DVE.wait(tr[t])
                cs = slice(512 * h, 512 * h + 512)
                return DVE.do(lambda e: e.tensor_scalar(U[:, t, cs], X[:, t, cs], BN[:, t, 14:15], None, ALU.mult))

            def stage(t, h):
                done = rms_half(t, h, step(t, h))
                if h == 1:
                    tr[t] = rms_stats(t, done)

            return turn_norm(z, stage, lambda k: MC[:, a + k:a + k + 1],
                             lambda k: MC[:, b + k:b + k + 1])

        xfree[:] = now()
        DVE.wait(modt[0])
        AC.wait(modt[0])
        xt = rms_turn(8, 0, lambda t, h: x_ready[t][h])
        yb_free[0] = modulation_out(1, YB[0], t_mf)
        xfree[:] = cut = now()
        PO.wait(*cut)
        PO.do(lambda e: e.memset(KD[64:128, :, 0, :], 0.0))
        PO.do(lambda e: e.memset(KD[0:64, :, 1, :], 0.0))
        PO.do(lambda e: e.memset(KPE[64:128, 0, :], 0.0))
        t_zero = PO.do(lambda e: e.memset(KPE[0:64, 1, :], 0.0))
        PO.wait(t_zero)
        SP.wait(*cut)
        t_tb = load(SP, "tb2", (BV[0][:, :], I["c_alibi"]), (BV[1][:, 0:256], I["c_causal"]),
                    (BV[1][:, 256:384], I["c_rope_t"]), (AR[:, 8192:8704], I["c_rope_f"]))
        LB = BV[1][:, 640:896].rearrange("p (n c) -> p n c", n=4)
        t_lb = load(SP, "lam", *[(LB[:, n, :], I[f"lambda_{x}_2"][0].partition_broadcast(128))
                                 for n, x in enumerate(("q1", "q2", "k1", "k2"))])
        AC.wait(*cut)
        DVE.wait(*cut)
        dtok = {}
        lam = cols(4)

        def minus_lambda(_):
            DVE.wait(t_lb)
            t1 = DVE.do(lambda e: e.tensor_tensor(LB[:, 0:2, :], LB[:, 0:2, :], LB[:, 2:4, :], ALU.mult))
            DVE.wait(t1)
            t1 = DVE.do(lambda e: e.tensor_reduce(lam[:, 0:2], LB[:, 0:2, :], AX, ALU.add))
            AC.wait(t1)
            t1 = AC.do(lambda e: e.activation(lam[:, 0:2], lam[:, 0:2], ACT.Exp))
            DVE.wait(t1)
            dtok["lam"] = DVE.do(lambda e: e.scalar_tensor_tensor(lam[:, 2:3], lam[:, 1:2], LAMBDA_INIT, lam[:, 0:1],
                                                            ALU.subtract, ALU.subtract))


        def dq_chunk(j):
            s = use()
            i, W = bank()
            for f in range(2):
                tp = fm_gemm(s, 8, 256, 128 * f, W[:, 256 * f:256 * f + 256], xt)
            release(s, tp)
            dtok["x"] = tp
            AC.wait(tp)
            W3 = W[:, :].rearrange("p (f c) -> p f c", f=2)
            if j < 2:
                te = AC.do(lambda e: e.copy(DQ[:, 2 * j:2 * j + 2, :], W3))
            else:
                AC.do(lambda e: e.copy(KD[0:64, 2 * j - 4:2 * j - 2, 0, :], W3[0:64]))
                te = AC.do(lambda e: e.copy(KD[64:128, 2 * j - 4:2 * j - 2, 1, :], W3[64:128]))
            bank_free[i] = te
            dtok["k", j // 2, j % 2] = te

        def ev_dv(t, W, tp):
            AC.wait(tp)
            dtok["v"] = AC.do(lambda e: e.copy(DV[:, t, :], W[:, :]))
            return dtok["v"]

        def latent_scale(t, dst, n, W, tp, w):
            AC.wait(tp)
            AC.wait(AC.do(lambda e: e.copy(dst, W[:, 0:dst.shape[1]])))
            te = AC.do(lambda e: e.activation(V2[:, t, 0:n], W[:, 0:n], ACT.Square, accum_out=w[:, 0:1]))
            PO.wait(te)
            t1 = PO.do(lambda e: e.tensor_scalar(w[:, 0:1], w[:, 0:1], 1 / n, EPS, ALU.mult, ALU.add))
            t1 = rsqrt(w[:, 1:2], w[:, 0:1], t1)
            DVE.wait(te, t1)
            return te, DVE.do(lambda e: e.tensor_scalar(dst[:, 0:n], dst[:, 0:n], w[:, 1:2], None, ALU.mult))

        def ev_ql(t, W, tp):
            te, dtok["ql", t] = latent_scale(t, QL[:, t, :], 384, W, tp, cols(2))
            return te

        def ev_kl(t, W, tp):
            te, dtok["kl", t] = latent_scale(t, KL[:, t, :], 256, W, tp, cols(2))
            return te

        efree, pfree = [None, None], [None, None]

        def softmax_rows(W, E, tb, scale, w, c):
            DVE.do(lambda e: e.scalar_tensor_tensor(E[:, 0:128], W[:, 0:128], scale, tb[:, 128:256],
                                                    ALU.mult, ALU.add))
            t1 = DVE.do(lambda e: e.scalar_tensor_tensor(E[:, 128:384], W[:, 128:384], scale, tb,
                                                         ALU.mult, ALU.add))
            tw = t1
            DVE.wait(t1)
            DVE.do(lambda e: e.tensor_reduce(w[:, c:c + 1], E[:, 0:128], AX, ALU.max, negate=True))
            t1 = DVE.do(lambda e: e.tensor_reduce(w[:, c + 1:c + 2], E[:, 128:384], AX, ALU.max, negate=True))
            AC.wait(t1)
            AC.do(lambda e: e.activation(E[:, 0:128], E[:, 0:128], ACT.Exp, bias=w[:, c:c + 1],
                                         accum_out=w[:, c + 2:c + 3]))
            te = AC.do(lambda e: e.activation(E[:, 128:384], E[:, 128:384], ACT.Exp, bias=w[:, c + 1:c + 2],
                                              accum_out=w[:, c + 3:c + 4]))
            return tw, te

        def d1(h):
            E = E2[h % 2]
            w = cols(12)
            tps, bs = [], []
            for m in range(2):
                i, W = bank()
                bs.append((i, W))
                PE.wait(dtok["k", 0, h // 2], dtok["k", 1, h // 2], t_zero)
                PE.run(mm(W[:, 0:128], DQ[:, h, 0:128], KD[:, h, m, 0:128], True, True))
                tps.append(PE.do(mm(W[:, 128:384], DQ[:, h, 128:256], KD[:, h, m, :], True, True)))
            for m in range(2):
                DVE.wait(tps[m], t_tb, dtok["lam"], efree[h % 2])
                bank_free[bs[m][0]], te = softmax_rows(bs[m][1], E[m], TB[h], 64 ** -0.5, w, 4 * m)
            DVE.wait(te)
            w2 = w[:, 0:8].rearrange("p (m c) -> p m c", m=2)[:, :, 2:4]
            r = w[:, 8:12].rearrange("p (m c) -> p m c", m=2)
            t1 = DVE.do(lambda e: e.reciprocal(r, w2))
            DVE.wait(t1)
            t1 = DVE.do(lambda e: e.tensor_scalar(w[:, 10:12], w[:, 10:12], lam[:, 2:3], None, ALU.mult))
            for c, a in ((0, slice(0, 128)), (1, slice(128, 384))):
                t2 = DVE.do(lambda e, c=c, a=a: e.tensor_scalar(E[0][:, a], E[0][:, a], w[:, 8 + c:9 + c], None,
                                                                ALU.mult))
                DVE.wait(t1, t2)
                t3 = DVE.do(lambda e, c=c, a=a: e.scalar_tensor_tensor(E[0][:, a], E[1][:, a], w[:, 10 + c:11 + c],
                                                                       E[0][:, a], ALU.mult, ALU.add))
            dtok["e", h] = t3
            dtok["dq"] = tps[1]

        def turn_p(h, key, E, n):
            i, W = bank()
            PE.wait(dtok[key, h])
            for b in range(3):
                tp = PE.do(lambda e, b=b: e.transpose(W[:, 128 * b:128 * b + 128], E[:, 128 * b:128 * b + 128],
                                                      IDN[:, :]))
            efree[h % 2] = tp
            AC.wait(tp, pfree[h % 2])
            bank_free[i] = dtok["pt", n] = AC.do(lambda e: e.copy(PTS[h % 2], W[:, 0:384]))

        def d2(h):
            turn_p(h, "e", E2[h % 2][0], h)

        ot_free = [None, None]

        def d3(h):
            i, W = bank()
            P = PTS[h % 2]
            PE.wait(dtok["pt", h], dtok["v"])
            hs = slice(128 * h, 128 * h + 128)
            PE.run(mm(W[:, 0:128], P[:, 0:128], DV[:, 0, hs], True, True))
            PE.run(mm(W[:, 128:256], P[:, 128:256], DV[:, 0, hs], True, False))
            tp = PE.do(mm(W[:, 128:256], P[:, 256:384], DV[:, 1, hs], False, True))
            pfree[h % 2] = tp
            w, OT = cols(4), OTS[h % 2]
            AC.wait(tp, ot_free[h % 2], t_tb)
            for t in range(2):
                te = AC.do(lambda e, t=t: e.activation(OT[:, t, :], W[:, 128 * t:128 * t + 128], ACT.Square,
                                                       accum_out=w[:, t:t + 1]))
            PO.wait(te)
            t1 = PO.do(lambda e: e.tensor_scalar(w[:, 0:2], w[:, 0:2], 1 / 128, EPS, ALU.mult, ALU.add))
            t1 = rsqrt(w[:, 2:4], w[:, 0:2], t1)
            DVE.wait(te, t1)
            for t in range(2):
                t2 = DVE.do(lambda e, t=t: e.tensor_scalar(OT[:, t, :], W[:, 128 * t:128 * t + 128],
                                                           w[:, 2 + t:3 + t], 1.0 - LAMBDA_INIT,
                                                           ALU.mult, ALU.mult))
            bank_free[i] = dtok["ot", h] = t2

        def d4(h):
            i, W = bank()
            OT = OTS[h % 2]
            PE.wait(dtok["ot", h])
            for t in range(2):
                tp = PE.do(lambda e, t=t: e.transpose(W[:, 128 * t:128 * t + 128], OT[:, t, :], IDN[:, :]))
            ot_free[h % 2] = tp
            DVE.wait(tp, dtok["dq"])
            bank_free[i] = dtok["om", h] = DVE.do(lambda e: e.tensor_scalar(
                DQ[:, h, :], W[:, 0:256], PC[:, C_GD:C_GD + 1], None, ALU.mult))

        def panel(width, evac, ys):
            def half(kh):
                s = use()
                for t in range(2):
                    Y = YB[ys[t]]
                    if kh == 0:
                        PE.wait(yb_free[ys[t]])
                    tp = tm_gemm(s, 4, width, 0, width, Y[:, 0:width], t, 4 * kh, kh == 0, kh == 1, xt)
                    if kh == 1:
                        yb_free[ys[t]] = evac(t, Y, tp)
                release(s, tp)
                dtok["x"] = tp
            return half

        lq, lk = [], []

        def latents(_):
            for t in range(2):
                lk.extend(turn(t, lambda k, t=t: KL[:, t, 128 * k:128 * k + 128], 2, [dtok["kl", t]],
                               LKH, LKL, lambda k: PC[:, C_GK + k:C_GK + k + 1]))
            for t in range(2):
                lq.extend(turn(t, lambda k, t=t: QL[:, t, 128 * k:128 * k + 128], 3, [dtok["ql", t]],
                               LQH, LQL, lambda k: PC[:, C_GQ + k:C_GQ + k + 1]))

        def rotary_a(_):
            cs, sn = TR[:, 0], TR[:, 1]
            kr = KL[:, :, 256:320]
            DVE.wait(dtok["kl", 0], dtok["kl", 1], t_tb, *[[p.hi, p.lo] for p in xt])
            for o, (a, b), op in ((0, (cs, sn), ALU.subtract), (32, (sn, cs), ALU.add)):
                t1 = DVE.do(lambda e, a=a: e.tensor_tensor(RA[:, 0], kr[:, :, 0:32], a, ALU.mult))
                t2 = DVE.do(lambda e, b=b: e.tensor_tensor(RA[:, 1], kr[:, :, 32:64], b, ALU.mult))
                DVE.wait(t1, t2)
                for d in (0, 64):
                    t1 = DVE.do(lambda e, o=o, d=d, op=op: e.tensor_tensor(RT[:, :, o + d:o + d + 32], RA[:, 0],
                                                                           RA[:, 1], op))
                DVE.wait(t1)
            dtok["rt"] = t1

        def rotary_b(_):
            i, W = bank()
            PE.wait(dtok["rt"])
            for t in range(2):
                tp = PE.do(lambda e, t=t, W=W: e.transpose(W[:, 128 * t:128 * t + 128], RT[:, t, :], IDN[:, :]))
            AC.wait(tp, t_zero)
            AC.do(lambda e, W=W: e.copy(KPE[0:64, 0, :], W[0:64, 0:256]))
            bank_free[i] = dtok["kpe"] = AC.do(lambda e, W=W: e.copy(KPE[64:128, 1, :], W[64:128, 0:256]))

        def q_up(j):
            s = use()
            for g in range(2):
                i, W = bank()
                for f in range(2):
                    tp = fm_gemm(s, 3, 512, 256 * g + 128 * f, W[:, 256 * f:256 * f + 256], lq, LQH, LQL)
                if g == 0:
                    AC.wait(tp)
                    te = AC.do(lambda e, W=W: e.copy(QN[:, 2 * j:2 * j + 2, :],
                                                     W[:, :].rearrange("p (f c) -> p f c", f=2)))
                else:
                    DVE.wait(tp, t_tb, dtok.get("qpe"))
                    DVE.do(lambda e, W=W: e.tensor_tensor(QT2[0], W[:, 0:256], CS[:, 0, :], ALU.mult))
                    te = DVE.do(lambda e, W=W: e.tensor_tensor(QT2[1], W[:, 256:512], CS[:, 1, :], ALU.mult))
                    DVE.wait(te)
                    dtok["qpe"] = DVE.do(lambda e: e.tensor_tensor(QPE[:, j, :], QT2[0], QT2[1], ALU.add))
                bank_free[i] = te
            release(s, tp)
            dtok["q", j] = [AC.last(), dtok["qpe"]]

        def kv_up(_):
            s = use()
            for g in range(2):
                i, W = bank()
                for f in range(2):
                    tp = fm_gemm(s, 2, 1024, 256 * (2 * g + f), W[:, 256 * f:256 * f + 256], lk, LKH, LKL)
                AC.wait(tp)
                bank_free[i] = AC.do(lambda e, g=g, W=W: e.copy(KN[:, 2 * g:2 * g + 2, :],
                                                                W[:, :].rearrange("p (f c) -> p f c", f=2)))
            for t in range(2):
                i, W = bank()
                tp = tm_gemm(s, 2, 1024, 0, 0, W[:, :].rearrange("p (h c) -> p h c", h=4), t, 0, True, True, lk,
                             LKH, LKL, lambda w, k: w[:, 0:2048].rearrange(
                                 "p (k h c) -> p k h c", k=2, h=4)[:, k, :, 128:256])
                AC.wait(tp, dtok["ql", t])
                bank_free[i] = AC.do(lambda e, t=t, W=W: e.copy(V2[:, t, :], W[:, :]))
            release(s, tp)
            dtok["kv"] = AC.last()

        def m1(h):
            i, W = bank()
            E = E2[h % 2][0]
            w = cols(6)
            PE.wait(*dtok["q", h // 2], dtok["kv"], dtok["kpe"])
            for o, tq, n in ((slice(0, 128), slice(0, 128), 128), (slice(128, 384), slice(128, 256), 256)):
                PE.run(mm(W[:, o], QN[:, h, tq], KN[:, h, 0:n], True, False))
                tp = PE.do(mm(W[:, o], QPE[:, h // 2, tq], KPE[:, h % 2, 0:n], False, True))
            DVE.wait(tp, efree[h % 2])
            bank_free[i], te = softmax_rows(W, E, TB[4], 192 ** -0.5, w, 0)
            DVE.wait(te)
            t1 = DVE.do(lambda e: e.reciprocal(w[:, 4:6], w[:, 2:4]))
            DVE.wait(t1)
            DVE.do(lambda e: e.tensor_scalar(E[:, 0:128], E[:, 0:128], w[:, 4:5], None, ALU.mult))
            dtok["m", h] = DVE.do(lambda e: e.tensor_scalar(E[:, 128:384], E[:, 128:384], w[:, 5:6], None, ALU.mult))

        def m2(h):
            turn_p(h, "m", E2[h % 2][0], 4 + h)

        xo = {}

        def m3(h):
            i, W = bank()
            P = PTS[h % 2]
            PE.wait(dtok["pt", 4 + h])
            hs = slice(128 * h, 128 * h + 128)
            PE.run(mm(W[:, 0:128], V2[:, 0, hs], P[:, 0:128], True, True))
            PE.run(mm(W[:, 128:256], V2[:, 0, hs], P[:, 128:256], True, False))
            tp = PE.do(mm(W[:, 128:256], V2[:, 1, hs], P[:, 256:384], False, True))
            pfree[h % 2] = tp
            xo[2 + h // 2] = xo.get(2 + h // 2, []) + [hilo_bank(None, 4 + h, 5 + h, XH[:, 4 + h, :], XL[:, 4 + h, :],
                                                                 i, W[:, 0:256], tp, dtok["x"])]

        def xo_diff(j):
            xo[j] = [hilo(None, 2 * j, 2 * j + 2, XH[:, 2 * j:2 * j + 2, :], XL[:, 2 * j:2 * j + 2, :],
                          DQ[:, 2 * j:2 * j + 2, :], dtok["x"], dtok["om", 2 * j], dtok["om", 2 * j + 1])]

        def r2(*js):
            return row_chunks(js, 4, [(xo[b], XH, XL, 2 * b) for b in ((0, 2, 1, 3)[j] for j in js)])

        dv = panel(512, ev_dv, (0, 1))
        for width, ev, ys in ((320, ev_kl, (2, 3)), (384, ev_ql, (0, 1))):
            p = panel(width, ev, ys)
            p(0)
            p(1)
        steps = {"k": dq_chunk, "n": minus_lambda, "l": latents, "y": rotary_a, "z": rotary_b, "v": dv, "u": kv_up,
                 "q": q_up, "a": d1, "b": d2, "c": d3, "d": d4, "e": m1, "f": m2, "g": m3, "x": xo_diff, "r": r2}
        for f, n in MIXER:
            steps[f](int(n))
        ys = r2(2, 3)

        def gated(ys, n, t, h):
            cs = slice(512 * h, 512 * h + 512)
            DVE.wait(*x_ready[t], *t_gb)
            DVE.wait(ys[2 * t + h])
            yb_free[2 * t + h] = tu = DVE.do(lambda e: e.tensor_tensor(U[:, t, cs], YB[2 * t + h][:, :],
                                                                       GB[:, n, cs], ALU.mult))
            DVE.wait(tu)
            tu = DVE.do(lambda e: e.tensor_tensor(X[:, t, cs], X[:, t, cs], U[:, t, cs], ALU.add))
            x_ready[t] = [tu]
            return tu

        xfree[:] = now()
        DVE.wait(dtok["x"])
        AC.wait(modt[1])
        xt = rms_turn(24, 16, lambda t, h: gated(ys, 0, t, h))
        cut = now()
        SG = [AR[:, 1024 * n:1024 * n + 512] for n in range(2)]
        SU = [AR[:, 1024 * n + 512:1024 * n + 1024] for n in range(2)]
        fo = {}
        bv_free[:] = [cut, cut]
        g_i, t_gf = bvec(I["g_final_2"])
        for j in range(12):
            if j < 11:
                n = j % 2
                for m in range(2):
                    s = use()
                    i, W = bank()
                    for f in range(2):
                        tp = fm_gemm(s, 8, 256, 128 * f, W[:, 256 * f:256 * f + 256], xt)
                    release(s, tp)
                    if m == 0:
                        AC.wait(tp, *cut, *f_free[n])
                        bank_free[i] = tg = AC.do(lambda e, W=W, n=n: e.activation(SG[n], W[:, :], ACT.Silu))
                    else:
                        DVE.wait(tp, tg, *f_free[n])
                        bank_free[i] = tu = DVE.do(lambda e, W=W, n=n: e.tensor_tensor(SU[n], W[:, :], SG[n],
                                                                                      ALU.mult))
                fo[j] = hilo(None, 0, 2, FH[n][:, :], FL[n][:, :], SU[n], tu)
            v = lambda b: b.rearrange("p (f c) -> p f c", f=2)
            js = () if j in (0, 10) else (9, 10) if j == 11 else (j - 1,)
            if js:
                ys = row_chunks(js, 11, [([fo[m]], v(FH[m % 2][:, :]), v(FL[m % 2][:, :]), 0) for m in js])
                for m in js:
                    f_free[m % 2] = [PE.last(), DVE.last()]
        outs = []
        for t in range(2):
            for h in range(2):
                done = rms_half(t, h, gated(ys, 1, t, h))
            DVE.wait(rms_stats(t, done), t_gf)
            for h in range(2):
                cs = slice(512 * h, 512 * h + 512)
                tz = DVE.do(lambda e, t=t, cs=cs: e.scalar_tensor_tensor(
                    U[:, t, cs], X[:, t, cs], BN[:, t, 14:15], BV[g_i][:, cs], ALU.mult, ALU.mult))
                lane = (SP, AC)[h]
                lane.wait(tz)
                outs.append(load(lane, f"out{t}{h}", (out[0, 128 * t:128 * t + 128, cs], U[:, t, cs])))
        SP.wait(*outs)
        assert split_n[0] == len(chunks) and issued[0] == len(chunks) and used[0] == mm_n[0]

        block = ctx.enter_context(nc.Block())

        @block.sync
        def _(e):
            SP.emit(e)

        @block.gpsimd
        def _(e):
            PO.emit(e)

        @block.scalar
        def _(e):
            AC.emit(e)

        @block.vector
        def _(e):
            DVE.emit(e)

        @block.tensor
        def _(e):
            PE.emit(e)


def constants():
    f = np.float32
    p = np.arange(128)
    c = {"c_idn": np.eye(128, dtype=f)}
    sel = np.zeros((4, 4, 128), f)
    for h in range(4):
        sel[h, h] = 1.0
    c["c_sel"] = sel.reshape(4, 512)
    c["c_msk"] = np.concatenate([np.where(p[None, :] >= p[:, None], 0.0, NEG), np.zeros((128, 128))], 1).astype(f)
    win = np.zeros((4, 256, 256), f)
    t = np.arange(256)
    for g, w in enumerate((2, 4, 8, 16)):
        inside = (t[None, :] >= t[:, None]) & (t[None, :] - t[:, None] < w)
        win[g] = inside / np.minimum(t + 1, w).astype(f)[None, :]
        win[g] -= np.eye(256, dtype=f)
    c["c_win"] = np.concatenate([np.concatenate([win[g, 0:128, 0:144], win[g, 128:256, 128:256]], 1)
                                 for g in range(4)], 1).astype(f)
    rel = (128 + p[:, None] - t[None, :]).astype(f)
    slopes = 2.0 ** (-8.0 * np.arange(1, 5, dtype=f) / 4)
    c["c_alibi"] = np.concatenate([np.where(rel >= 0, -s * rel, NEG) for s in slopes], 1).astype(f)
    c["c_causal"] = np.where(rel >= 0, 0.0, NEG).astype(f)
    inv = (f(10000.0) ** (-np.arange(0, 64, 2, dtype=f) / f(64))).astype(f)
    ang = (np.arange(256, dtype=f)[:, None] * inv[None, :]).astype(f)
    cos, sin = np.cos(ang).astype(f), np.sin(ang).astype(f)
    c["c_rope_t"] = np.concatenate([x[128 * t:128 * t + 128] for x in (cos, sin) for t in range(2)], 1)
    c["c_rope_f"] = np.concatenate([np.tile(cos.T, (4, 1)), np.tile(np.concatenate([-sin.T, sin.T]), (2, 1))], 1)
    return {k: np.ascontiguousarray(v, dtype=f) for k, v in c.items()}


_INS = ["x", "mem", "mlstm_w_in", "mlstm_gate_b", "mlstm_conv_w", "mlstm_norm_g", "mlstm_w_out", "pool_w",
        "pool_scale", "mem_w_kv", "xattn_wq", "xattn_wo", "mlp_w1", "mlp_b1", "mlp_w2", "mlp_b2", "ln_g", "ln_b",
        "c_2", "w_ada_2", "b_ada_2", "g_mix_2", "w_in_2", "lambda_q1_2", "lambda_k1_2", "lambda_q2_2",
        "lambda_k2_2", "g_diff_out_2", "g_q_lat_2", "w_q_up_2", "g_kv_lat_2", "w_kv_up_2", "w_out_2", "g_ffn_2",
        "w_ffn_gate_2", "w_ffn_up_2", "w_ffn_down_2", "g_final_2"]


def kernel(**inputs):
    import concourse.bacc as bacc
    from concourse.bass_utils import run_bass_kernel_spmd

    nc = bacc.Bacc("TRN2", target_bir_lowering=False, num_devices=1)
    arrays, args = {}, {}
    for name, a in [(n, np.ascontiguousarray(inputs[n])) for n in _INS] + list(constants().items()):
        arrays[f"in_{name}"] = a
        args[name] = nc.dram_tensor(f"in_{name}", a.shape, mybir.dt.from_np(a.dtype), kind="ExternalInput").ap()
    out = nc.dram_tensor("out_0", (1, 256, 1024), F32, kind="ExternalOutput").ap()
    build_program(nc, args, out)
    r = run_bass_kernel_spmd(nc, [arrays], core_ids=[0])
    return r.results[0]["out_0"]
```
